# Optimizing a Trainium2 kernel written in Bass

```python
import math
import jax
import jax.numpy as jnp
from jax import lax
import numpy as np

D_MODEL = 1024
BATCH = 1
SEQ = 128
DEPTH = 2
DEC_BATCH = 1
DEC_SEQ = 512
PAST_LEN = 128

GRID_W = 64
ROPE_BASE = 10000.0
NORM_EPS = 1e-6
Q_BLOCK = 128
F_GROUPS = 4
F_CH = 64
D_FOURIER = F_GROUPS * F_CH
DIFF_HEADS = 4
DIFF_DH = 64
D_DIFF = DIFF_HEADS * 2 * DIFF_DH
MLA_HEADS = 4
MLA_Q_RANK = 256
MLA_KV_RANK = 128
MLA_NOPE = 64
MLA_ROPE = 32
MLA_V = 64
D_MLA = MLA_HEADS * MLA_V
D_MIX = D_FOURIER + D_DIFF + D_MLA
IN_SPLITS = (D_FOURIER, D_DIFF, D_DIFF, D_DIFF, MLA_Q_RANK, MLA_KV_RANK, MLA_ROPE)
IN_COLS = sum(IN_SPLITS)
IN_OFFSETS = tuple(int(o) for o in np.cumsum(IN_SPLITS)[:-1])
N_EXPERTS = 16
EC_CAPACITY_FACTOR = 2
EXPERT_FF = 1024
N_MOD = 6

kernel_name = 'hybrid_fourier_diffattn_mla_ec_dit_step'

def rms_norm(x, g):
    xf = x.astype(jnp.float32)
    y = xf * lax.rsqrt(jnp.mean(xf * xf, axis=-1, keepdims=True) + NORM_EPS)
    return (y * g.astype(jnp.float32)).astype(x.dtype)

def axial_rope(n_tok, dim):
    rows = n_tok // GRID_W
    row = jnp.repeat(jnp.arange(rows, dtype=jnp.float32), GRID_W)
    col = jnp.tile(jnp.arange(GRID_W, dtype=jnp.float32), rows)
    nf = dim // 4
    inv = ROPE_BASE ** (-jnp.arange(nf, dtype=jnp.float32) / nf)
    ang = jnp.concatenate([row[:, None] * inv, col[:, None] * inv], axis=-1)
    return jnp.cos(ang), jnp.sin(ang)

def apply_rope(x, cos, sin):
    half = x.shape[-1] // 2
    shape = (x.shape[1],) + (1,) * (x.ndim - 3) + (half,)
    c = cos.reshape(shape).astype(x.dtype)
    s = sin.reshape(shape).astype(x.dtype)
    x1, x2 = x[..., :half], x[..., half:]
    return jnp.concatenate([x1 * c - x2 * s, x2 * c + x1 * s], axis=-1)

def blocked_over_queries(fn, q):
    B, sq = q.shape[:2]
    nb = sq // Q_BLOCK
    qb = jnp.moveaxis(q.reshape((B, nb, Q_BLOCK) + q.shape[2:]), 1, 0)
    out = lax.map(fn, qb)
    out = jnp.moveaxis(out, 0, 1)
    return out.reshape((B, sq) + out.shape[3:])

def diff_attention_block(qb, k, v, lam):
    s = jnp.einsum('bqhcd,bkhcd->bhcqk', qb, k).astype(jnp.float32) * (DIFF_DH ** -0.5)
    p = jax.nn.softmax(s, axis=-1).astype(v.dtype)
    o = jnp.einsum('bhcqk,bkhe->bqhce', p, v)
    return o[..., 0, :] - lam.astype(v.dtype) * o[..., 1, :]

def softmax_attention_block(qb, k, v, scale):
    s = jnp.einsum('bqhd,bkhd->bhqk', qb, k).astype(jnp.float32) * scale
    p = jax.nn.softmax(s, axis=-1).astype(v.dtype)
    return jnp.einsum('bhqk,bkhe->bqhe', p, v)

def token_mixers(h, layer_idx, ctx, rope_diff, rope_mla, w_in, w_four, diff_lambda, g_subln,
                 g_mla_q, w_mla_uq, g_mla_kv, w_mla_ukv, w_out):
    latent = ctx is not None
    B, n, _ = h.shape
    zf, zq, zk, zv, zcq, zckv, zkpe = jnp.split(h @ w_in, IN_OFFSETS, axis=-1)

    f = zf.reshape(B, n, F_GROUPS, F_CH).astype(jnp.float32)
    f = jnp.fft.fft2(f, axes=(1, 3), norm='ortho').real.astype(h.dtype)
    y_four = jnp.einsum('bngc,gce->bnge', f, w_four).reshape(B, n, D_FOURIER)

    q = zq.reshape(B, n, DIFF_HEADS, 2, DIFF_DH)
    k = zk.reshape(B, n, DIFF_HEADS, 2, DIFF_DH)
    v = zv.reshape(B, n, DIFF_HEADS, 2 * DIFF_DH)
    lam_init = 0.8 - 0.6 * math.exp(-0.3 * layer_idx)
    lf = diff_lambda.astype(jnp.float32)
    lam = jnp.exp(jnp.sum(lf[0] * lf[1])) - jnp.exp(jnp.sum(lf[2] * lf[3])) + lam_init
    if latent:
        q_r = apply_rope(q, *rope_diff)
        k_r = apply_rope(k, *rope_diff)
        k_all = jnp.concatenate([k_r, ctx[0].reshape(B, -1, DIFF_HEADS, 2, DIFF_DH)], axis=1)
        v_all = jnp.concatenate([v, ctx[1]], axis=1)
    else:
        q_r, k_all, v_all = q, k, v
    o = blocked_over_queries(lambda qb: diff_attention_block(qb, k_all, v_all, lam), q_r)
    y_diff = (rms_norm(o, g_subln) * (1.0 - lam_init)).reshape(B, n, D_DIFF)

    cq = rms_norm(zcq, g_mla_q)
    qm = (cq @ w_mla_uq).reshape(B, n, MLA_HEADS, MLA_NOPE + MLA_ROPE)
    q_nope, q_pe = qm[..., :MLA_NOPE], qm[..., MLA_NOPE:]
    ckv = rms_norm(zckv, g_mla_kv)
    kpe = zkpe
    if latent:
        q_pe = apply_rope(q_pe, *rope_mla)
        kpe_lat = apply_rope(kpe, *rope_mla)
        ckv_all = jnp.concatenate([ckv, ctx[2]], axis=1)
        kpe_all = jnp.concatenate([kpe_lat, ctx[3]], axis=1)
    else:
        ckv_all, kpe_all = ckv, kpe
    kv = (ckv_all @ w_mla_ukv).reshape(B, -1, MLA_HEADS, MLA_NOPE + MLA_V)
    k_nope, v_m = kv[..., :MLA_NOPE], kv[..., MLA_NOPE:]
    k_m = jnp.concatenate([k_nope, jnp.broadcast_to(kpe_all[:, :, None, :], k_nope.shape[:-1] + (MLA_ROPE,))], axis=-1)
    q_m = jnp.concatenate([q_nope, q_pe], axis=-1)
    mla_scale = (MLA_NOPE + MLA_ROPE) ** -0.5
    o_m = blocked_over_queries(lambda qb: softmax_attention_block(qb, k_m, v_m, mla_scale), q_m)
    y_mla = o_m.reshape(B, n, D_MLA)

    y = jnp.concatenate([y_four, y_diff, y_mla], axis=-1) @ w_out
    new_ctx = None if latent else (k.reshape(B, n, DIFF_HEADS, 2 * DIFF_DH), v, ckv, kpe)
    return y, new_ctx

def expert_choice_ffn(h, w_router, w_e_gate, w_e_up, w_e_down):
    B, n, D = h.shape
    cap = max(1, EC_CAPACITY_FACTOR * n // N_EXPERTS)
    aff = jax.nn.softmax(jnp.einsum('bnd,de->bne', h, w_router).astype(jnp.float32), axis=-1)
    gate, idx = lax.top_k(jnp.swapaxes(aff, 1, 2), cap)
    xs = jax.vmap(lambda hb, ib: hb[ib])(h, idx)
    a = jnp.einsum('becd,edf->becf', xs, w_e_gate)
    u = jnp.einsum('becd,edf->becf', xs, w_e_up)
    ye = jnp.einsum('becf,efd->becd', jax.nn.silu(a) * u, w_e_down) * gate[..., None].astype(h.dtype)
    return jax.vmap(lambda ib, yb: jnp.zeros((n, D), yb.dtype).at[ib.reshape(-1)].add(yb.reshape(-1, D)))(idx, ye)

def setup_inputs(seed: int = 0) -> dict:
    key = jax.random.key(seed)
    ks = jax.random.split(key, 26)
    f32 = jnp.float32
    nrm = lambda k, shape, s=1.0: (jax.random.normal(k, shape, f32) * s)
    return {
        'x_prompt': nrm(ks[0], (BATCH, SEQ, D_MODEL)),
        'x_sample': nrm(ks[1], (DEC_BATCH, DEC_SEQ, D_MODEL)),
        'cache_diff_k': nrm(ks[2], (DEC_BATCH, DEPTH, PAST_LEN, DIFF_HEADS, 2 * DIFF_DH)),
        'cache_diff_v': nrm(ks[3], (DEC_BATCH, DEPTH, PAST_LEN, DIFF_HEADS, 2 * DIFF_DH)),
        'cache_mla_ckv': nrm(ks[4], (DEC_BATCH, DEPTH, PAST_LEN, MLA_KV_RANK)),
        'cache_mla_kpe': nrm(ks[5], (DEC_BATCH, DEPTH, PAST_LEN, MLA_ROPE)),
        'c': nrm(ks[6], (DEC_BATCH, D_MODEL)),
        'c_ctx': nrm(ks[7], (D_MODEL,)),
        'w_ada': nrm(ks[8], (DEPTH, D_MODEL, N_MOD * D_MODEL), 0.5 * D_MODEL ** -0.5),
        'b_ada': nrm(ks[9], (DEPTH, N_MOD * D_MODEL), 0.02),
        'g_attn': 1.0 + nrm(ks[10], (DEPTH, D_MODEL), 0.1),
        'g_ffn': 1.0 + nrm(ks[11], (DEPTH, D_MODEL), 0.1),
        'w_in': nrm(ks[12], (DEPTH, D_MODEL, IN_COLS), D_MODEL ** -0.5),
        'w_four': nrm(ks[13], (DEPTH, F_GROUPS, F_CH, F_CH), F_CH ** -0.5),
        'diff_lambda': nrm(ks[14], (DEPTH, 4, DIFF_DH), 0.1),
        'g_subln': 1.0 + nrm(ks[15], (DEPTH, 2 * DIFF_DH), 0.1),
        'g_mla_q': 1.0 + nrm(ks[16], (DEPTH, MLA_Q_RANK), 0.1),
        'w_mla_uq': nrm(ks[17], (DEPTH, MLA_Q_RANK, MLA_HEADS * (MLA_NOPE + MLA_ROPE)), MLA_Q_RANK ** -0.5),
        'g_mla_kv': 1.0 + nrm(ks[18], (DEPTH, MLA_KV_RANK), 0.1),
        'w_mla_ukv': nrm(ks[19], (DEPTH, MLA_KV_RANK, MLA_HEADS * (MLA_NOPE + MLA_V)), MLA_KV_RANK ** -0.5),
        'w_out': nrm(ks[20], (DEPTH, D_MIX, D_MODEL), D_MIX ** -0.5),
        'w_router': nrm(ks[21], (DEPTH, D_MODEL, N_EXPERTS), D_MODEL ** -0.5),
        'w_e_gate': nrm(ks[22], (DEPTH, N_EXPERTS, D_MODEL, EXPERT_FF), D_MODEL ** -0.5),
        'w_e_up': nrm(ks[23], (DEPTH, N_EXPERTS, D_MODEL, EXPERT_FF), D_MODEL ** -0.5),
        'w_e_down': nrm(ks[24], (DEPTH, N_EXPERTS, EXPERT_FF, D_MODEL), EXPERT_FF ** -0.5),
        'g_final': 1.0 + nrm(ks[25], (D_MODEL,), 0.1),
    }

def reference(x_prompt, x_sample, cache_diff_k, cache_diff_v, cache_mla_ckv, cache_mla_kpe, c, c_ctx,
              w_ada, b_ada, g_attn, g_ffn, w_in, w_four, diff_lambda, g_subln, g_mla_q, w_mla_uq,
              g_mla_kv, w_mla_ukv, w_out, w_router, w_e_gate, w_e_up, w_e_down, g_final):

    def layer(x, cond, l, ctx, rope_diff, rope_mla):
        mod = (jax.nn.silu(cond) @ w_ada[l] + b_ada[l])[:, None, :]
        sh_a, sc_a, gt_a, sh_f, sc_f, gt_f = jnp.split(mod, N_MOD, axis=-1)
        h = rms_norm(x, g_attn[l]) * (1.0 + sc_a) + sh_a
        mix, new_ctx = token_mixers(h, l, ctx, rope_diff, rope_mla, w_in[l], w_four[l], diff_lambda[l],
                                    g_subln[l], g_mla_q[l], w_mla_uq[l], g_mla_kv[l], w_mla_ukv[l], w_out[l])
        x = x + gt_a * mix
        h = rms_norm(x, g_ffn[l]) * (1.0 + sc_f) + sh_f
        x = x + gt_f * expert_choice_ffn(h, w_router[l], w_e_gate[l], w_e_up[l], w_e_down[l])
        return x, new_ctx

    x = x_prompt
    cond_ctx = c_ctx[None, :]
    dk, dv, dckv, dkpe = [], [], [], []
    for l in range(DEPTH):
        x, (k_l, v_l, ckv_l, kpe_l) = layer(x, cond_ctx, l, None, None, None)
        dk.append(k_l)
        dv.append(v_l)
        dckv.append(ckv_l)
        dkpe.append(kpe_l)
    y_prompt = rms_norm(x, g_final)
    new_diff_k = jnp.stack(dk, axis=1)
    new_diff_v = jnp.stack(dv, axis=1)
    new_mla_ckv = jnp.stack(dckv, axis=1)
    new_mla_kpe = jnp.stack(dkpe, axis=1)

    n_lat = x_sample.shape[1]
    rope_diff = axial_rope(n_lat, DIFF_DH)
    rope_mla = axial_rope(n_lat, MLA_ROPE)
    x = x_sample
    for l in range(DEPTH):
        ctx = (cache_diff_k[:, l], cache_diff_v[:, l], cache_mla_ckv[:, l], cache_mla_kpe[:, l])
        x, _ = layer(x, c, l, ctx, rope_diff, rope_mla)
    y_sample = rms_norm(x, g_final)

    return (y_prompt, y_sample, new_diff_k, new_diff_v, new_mla_ckv, new_mla_kpe)


_drawn_inputs = setup_inputs


def setup_inputs(seed=0):
    import zlib

    import numpy as np

    out = dict(_drawn_inputs(seed))
    spreads = {}
    factors = {'cache_mla_ckv': 7.161, 'cache_mla_kpe': 8.0, 'g_subln': 2.681, 'g_mla_q': 8.0}
    for name, (base, spread) in spreads.items():
        noise = np.random.default_rng([zlib.crc32(name.encode()), seed]).standard_normal(out[name].shape)
        drawn = base * np.exp(spread * noise) if base else spread * noise
        out[name] = jnp.asarray(drawn.astype(out[name].dtype))
    for name, factor in factors.items():
        out[name] = (out[name] * factor).astype(out[name].dtype)
    return out
```

```python
from contextlib import ExitStack

import numpy as np

import concourse.bass as bass
from concourse import mybir

F32 = mybir.dt.float32
ALU = mybir.AluOpType
ACT = mybir.ActivationFunctionType
AX = mybir.AxisListType

P = 128
D = 1024
KD = D // P
DEPTH = 2
CTX, LAT, PAST = 128, 512, 128
TOK = CTX + LAT
NB = TOK // P
KEYS = LAT + PAST
GRID_W = 64
ROPE_BASE = 10000.0
EPS = 1e-6
HEADS = 4
DH = 64
NOPE, ROPE, VDIM = 64, 32, 64
QM = NOPE + ROPE
F_CH = 64
E_N = 16
PAIRS = E_N // 2
CAP = 2 * LAT // E_N
CAPX = 2 * CTX // E_N
SLOT_TOK = CAP + CAPX
N_MOD = 6
N_VEC = N_MOD * KD + 2 * KD + 2 + 1 + 1
DIFF_SCALE = float(DH) ** -0.5
MLA_SCALE = float(QM) ** -0.5

C_F, C_Q, C_K, C_V, C_CQ, C_CKV, C_KPE, C_END = 0, 256, 768, 1280, 1792, 2048, 2176, 2208

RING = 4
ADA_CHUNKS = 12
CH_MLA, CH_Q, CH_K, CH_V, CH_F, CH_DFT, CH_OUT = 12, 13, 14, 15, 16, 17, 18
DENSE_CHUNKS = 20
PAIR_CHUNKS = 12
LAYER_CHUNKS = DENSE_CHUNKS + PAIRS * PAIR_CHUNKS
assert LAYER_CHUNKS % RING == 0 and DENSE_CHUNKS % RING == 0 and PAIR_CHUNKS % RING == 0

K_ID, K_ROTD, K_ROTM = 0, 128, 256
K_ROPED = K_ROTM + QM
K_ROPEM = K_ROPED + 2 * LAT
K_CHAN = K_ROPEM + 2 * LAT
K_SEQX = K_CHAN + 2 * P
K_IOTA = K_SEQX + 2 * CTX
K_SLOT = K_IOTA + CAP
K_SLOTX = K_SLOT + 1
K_EPS = K_SLOTX + 1
K_W = K_EPS + 1

UNITS = 22
ROPES = 13
ATT_IT = HEADS * NB
GROUPS = 3 * ATT_IT
SMALL = 19
OUTS = 4


class Signal:

    def __init__(self, sem, per, setup=0, step=1):
        self.sem, self.per, self.setup, self.step = sem, per, setup, step

    def at(self, turn, k):
        return turn * (self.per * self.step) + (self.setup + k) * self.step


def build(nc, a):
    ctx = ExitStack()
    with ctx:
        def sb(name, shape):
            return ctx.enter_context(nc.sbuf_tensor(name, shape, F32))

        def signal(name, per, setup=0, step=1):
            return Signal(ctx.enter_context(nc.semaphore(name)), per, setup, step)

        ring = sb("ring", [P, RING, KD, 512])
        xT = sb("xT", [P, KD, TOK])
        hT = sb("hT", [P, KD, TOK])
        arena = sb("arena", [P, 14848])
        consts = sb("consts", [P, K_W])
        ones = sb("ones", [P, P])
        scr = sb("scr", [P, 2, TOK])
        rstd = sb("rstd", [P, TOK])
        rope_a = sb("rope_a", [P, 2, LAT])
        vec_rows = sb("vec_rows", [N_VEC, P])
        vecT = sb("vecT", [P, N_VEC])
        mod = sb("mod", [P, N_MOD * KD, 2])
        gain = sb("gain", [P, 2, KD, 2])
        cond_rows = sb("cond_rows", [3 * KD, P])
        cond_e = sb("cond_e", [2 * KD, P])
        condT = sb("condT", [P, 3 * KD])
        wuq = sb("wuq", [P, 2, HEADS * QM])
        wukv = sb("wukv", [P, HEADS * (NOPE + VDIM)])
        wfour = sb("wfour", [P, 2, P])
        wrt = sb("wrt", [P, KD, E_N])
        dlam = sb("dlam", [P, 4, DH])
        dprod = sb("dprod", [P, 2, DH])
        lamt = sb("lamt", [P, 2])
        lamw = sb("lamw", [P, 4])
        gsub = sb("gsub", [P, 1])
        cache_k = sb("cache_k", [P, HEADS * P])
        cache_v = sb("cache_v", [P, HEADS * P])
        cache_ckv = sb("cache_ckv", [P, P])
        cache_kpe = sb("cache_kpe", [P, QM])
        chanw = sb("chanw", [P, 2, 2, P])
        k_rows = sb("k_rows", [P, HEADS * P])
        ckv_rows = sb("ckv_rows", [P, P])
        kpe_rows = sb("kpe_rows", [P, ROPE])
        smax = sb("smax", [P, 2])
        negm = sb("negm", [P, 2])
        ssum = sb("ssum", [P, 2, 2])
        srec = sb("srec", [P, 2, 2])
        lg = sb("lg", [P, NB, E_N])
        lmax = sb("lmax", [P, NB])
        top8 = sb("top8", [E_N, 8])
        pos_rows = sb("pos_rows", [P, NB, E_N])
        cur = sb("cur", [P, NB, 2])
        sel = sb("sel", [E_N, 2, CAP])
        selx = sb("selx", [E_N, 2, CAPX])

        def region(at, *dims):
            n = int(np.prod(dims))
            v = arena[:, at:at + n]
            if len(dims) == 2:
                v = v.rearrange("p (a b) -> p a b", a=dims[0])
            if len(dims) == 3:
                v = v.rearrange("p (a b c) -> p a b c", a=dims[0], b=dims[1])
            return v

        qT = region(0, HEADS, TOK)
        kT = region(2560, HEADS, CTX + KEYS)
        v_rows = region(5632, NB, HEADS * P)
        vm_rows = region(5632, NB + 1, HEADS * VDIM)
        ckvT = region(8192, CTX + KEYS)
        kpeT = region(8960, CTX + KEYS)
        y_mla = region(9728, 2, TOK)
        probs = region(11008, 2, 2, TOK)
        cqT = region(11008, 2, TOK)
        chan_rows = region(11008, NB, 2, 2 * P)
        probsT = region(13568, 2, NB, P)
        zfT = region(13568, 2, TOK)
        yT = hT
        h_rows = region(0, NB, D)
        pick = region(5120, 2, 4 * CAP + CAPX)
        xs = region(5664, 2, KD, SLOT_TOK)
        hm = region(6944, 2, KD, SLOT_TOK)
        ye = region(8224, KD, 2 * CAP)
        yex = region(9248, KD, 2 * CAPX)
        ye_rows = region(9504, D)
        yex_rows = region(10528, D)
        back = region(11552, LAT)
        backx = region(12064, CTX)
        aff = region(12192, TOK)
        work = region(12832, TOK)
        pos = region(13472, TOK)
        mask = region(14112, TOK)
        x_rows = hT[:, :, :].rearrange("p a b -> p (a b)").rearrange("p (b d) -> p b d", b=NB)

        ident = consts[:, K_ID:K_ID + P]
        rot_diff = consts[:, K_ROTD:K_ROTD + P]
        rot_mla = consts[:, K_ROTM:K_ROTM + QM]
        cos_d, sin_d = consts[:, K_ROPED:K_ROPED + LAT], consts[:, K_ROPED + LAT:K_ROPED + 2 * LAT]
        cos_m, sin_m = consts[:, K_ROPEM:K_ROPEM + LAT], consts[:, K_ROPEM + LAT:K_ROPEM + 2 * LAT]
        iota = consts[:, K_IOTA:K_IOTA + CAP]
        eps = consts[:, K_EPS:K_EPS + 1]

        S = [ctx.enter_context(nc.psum_tensor(f"S{i}", [P, 1024], F32)) for i in range(2)]
        T = ctx.enter_context(nc.psum_tensor("T", [P, 1024], F32))
        U = ctx.enter_context(nc.psum_tensor("U", [P, 1024], F32))
        lat_bank = [T[:, 0:512], T[:, 512:1024]]
        ctx_bank = [U[:, 0:512], U[:, 512:1024]]
        sum_lat, sum_ctx = S[0][:, 0:512], S[0][:, 512:512 + CTX]
        rot_bank = S[1][:, 0:512]
        misc_bank = S[1][:, 512:1024]

        const_in = signal("const_in", 0, 4, 16)
        x_in = signal("x_in", 0, 2, 16)
        fill_done = signal("fill_done", 0, 3)
        xt_ps, xt_sb = signal("xt_ps", 0, KD), signal("xt_sb", 0, KD)
        cond_exp, cond_silu = signal("cond_exp", 0, 1), signal("cond_silu", 0, 1)
        cond_ps, cond_sb = signal("cond_ps", 0, 1), signal("cond_sb", 0, 1)
        slot_in = [signal(f"slot_in{i}", LAYER_CHUNKS // RING, 0, 16) for i in range(RING)]
        small_in = signal("small_in", SMALL, 0, 16)
        vec_ps, vec_sb = signal("vec_ps", 1), signal("vec_sb", 1)
        ada_ps, ada_sb = signal("ada_ps", ADA_CHUNKS), signal("ada_sb", ADA_CHUNKS)
        gain_sb = signal("gain_sb", 1)
        sq_done, sq_used = signal("sq_done", 2 * KD), signal("sq_used", 2 * KD)
        rms_done = signal("rms_done", 2)
        xn_done, h_done = signal("xn_done", 2 * KD), signal("h_done", 2 * KD)
        unit_ps = signal("unit_ps", UNITS)
        unit_lat, unit_ctx = signal("unit_lat", UNITS), signal("unit_ctx", UNITS)
        rope_ps, rope_sb = signal("rope_ps", ROPES), signal("rope_sb", ROPES)
        nsq_done, nsum_ps = signal("nsq_done", 7), signal("nsum_ps", 6)
        nrms_done, nscaled = signal("nrms_done", 6), signal("nscaled", 6)
        tr_ps, tr_sb = signal("tr_ps", 4), signal("tr_sb", 4)
        kpe_spread = signal("kpe_spread", 1)
        vm_ps, vm_sb = signal("vm_ps", NB + 1), signal("vm_sb", NB + 1)
        v_ps, v_sb = signal("v_ps", NB), signal("v_sb", NB)
        sc_ps, negm_done, exp_done = signal("sc_ps", GROUPS), signal("negm_done", GROUPS), signal("exp_done", GROUPS)
        probs_done = signal("probs_done", 2 * ATT_IT)
        pt_ps, pt_sb = signal("pt_ps", 2 * ATT_IT), signal("pt_sb", 2 * ATT_IT)
        o_ps, o_sb = signal("o_ps", 2 * ATT_IT), signal("o_sb", 2 * ATT_IT)
        lam_prod, lam_exp, lam_done = signal("lam_prod", 1), signal("lam_exp", 1), signal("lam_done", 1)
        cw_ps, cw_sb = signal("cw_ps", 2), signal("cw_sb", 2)
        fa_ps, fa_sb = signal("fa_ps", NB), signal("fa_sb", NB)
        fb_ps, fb_sb = signal("fb_ps", 2), signal("fb_sb", 2)
        mix_ps, mix_sb = signal("mix_ps", KD), signal("mix_sb", KD)
        outs_done = signal("outs_done", OUTS, 0, 16)
        lg_ps, lg_shift, lg_exp, aff_rows = (signal(n, 1) for n in ("lg_ps", "lg_shift", "lg_exp", "aff_rows"))
        aff_ps, pos_done, pr_ps = (signal(n, 1) for n in ("aff_ps", "pos_done", "pr_ps"))
        pr_sb = signal("pr_sb", 1, 1)
        hr_ps, hr_v, hr_a = signal("hr_ps", NB), signal("hr_v", NB), signal("hr_a", NB)
        sel_done, gate_sb, back_done = signal("sel_done", 1), signal("gate_sb", 1), signal("back_done", 1)
        sel_ps = signal("sel_ps", 1)
        pick_done, xs_ps = signal("pick_done", 2), signal("xs_ps", 2)
        xs_v, xs_a = signal("xs_v", 2), signal("xs_a", 2)
        gu_ps, silu_done, hm_done = signal("gu_ps", 8, 2), signal("silu_done", 4), signal("hm_done", 4)
        ye_ps, ye_sb = signal("ye_ps", 4, 2), signal("ye_sb", 4)
        yr_ps, yr_v, yr_a = signal("yr_ps", 2), signal("yr_v", 2), signal("yr_a", 2)
        add_ps, add_sb = signal("add_ps", KD), signal("add_sb", KD, 1)
        fin_ps, fin_v, fin_a = signal("fin_ps", NB), signal("fin_v", NB), signal("fin_a", NB)
        y_out = signal("y_out", 2, 0, 16)
        step_v = ctx.enter_context(nc.semaphore("step_v"))
        step_vp = signal("step_vp", 1)
        step_a = signal("step_a", 8, 0)

        block = ctx.enter_context(nc.Block())

        @block.sync
        def _(sp):
            sp.dma_start(consts[:, :], a["consts"]).then_inc(const_in.sem, 16)
            sp.dma_start(cond_rows[0:KD, :], a["c_ctx"].rearrange("(k p) -> k p", p=P)).then_inc(const_in.sem, 16)
            sp.dma_start(cond_rows[KD:2 * KD, :], a["c"].rearrange("b (k p) -> (b k) p", p=P)).then_inc(const_in.sem, 16)
            sp.dma_start(cond_rows[2 * KD:3 * KD, :], a["g_final"].rearrange("(k p) -> k p", p=P)).then_inc(const_in.sem, 16)
            sp.dma_start(x_rows[:, 0, :], a["x_prompt"].rearrange("b n d -> (b n) d")).then_inc(x_in.sem, 16)
            sp.dma_start(x_rows[:, 1:NB, :], a["x_sample"].rearrange("b (j p) d -> p (b j) d", p=P)).then_inc(x_in.sem, 16)

            sp.wait_ge(fill_done.sem, 3)
            with sp.Fori(0, DEPTH) as l:
                def small(dst, src):
                    sp.dma_start(dst, src).then_inc(small_in.sem, 16)

                sp.wait_ge(pr_sb.sem, pr_sb.at(l, 0))
                r = N_MOD * KD
                small(vec_rows[0:r, :], a["b_ada"][l].rearrange("(k p) -> k p", p=P))
                small(vec_rows[r:r + KD, :], a["g_attn"][l].rearrange("(k p) -> k p", p=P))
                small(vec_rows[r + KD:r + 2 * KD, :], a["g_ffn"][l].rearrange("(k p) -> k p", p=P))
                r += 2 * KD
                small(vec_rows[r:r + 2, :], a["g_mla_q"][l].rearrange("(k p) -> k p", p=P))
                small(vec_rows[r + 2:r + 3, :], a["g_mla_kv"][l].rearrange("(k p) -> k p", p=P))
                small(vec_rows[r + 3:r + 4, :], a["g_subln"][l].rearrange("(k p) -> k p", p=P))
                small(dlam[:, :, :], a["diff_lambda"][l].partition_broadcast(P))
                small(lamt[:, :], a["lam_init"][l].partition_broadcast(P))
                small(wuq[:, :, :], a["w_mla_uq"][l].rearrange("(k p) n -> p k n", p=P))
                small(wukv[:, :], a["w_mla_ukv"][l])
                small(cache_ckv[:, :], a["cache_mla_ckv"][0, l])
                small(cache_kpe[:, NOPE:QM], a["cache_mla_kpe"][0, l])
                small(cache_k[:, :], a["cache_diff_k"][0, l].rearrange("t h d -> t (h d)"))
                small(cache_v[:, :], a["cache_diff_v"][0, l].rearrange("t h d -> t (h d)"))
                for j in range(4):
                    half = (j % 2) * F_CH
                    small(wfour[half:half + F_CH, j // 2, half:half + F_CH], a["w_four"][l, j])
                small(wrt[:, :, :], a["w_router"][l].rearrange("(k p) e -> p k e", p=P))

                def load(i, src, last_read):
                    if last_read:
                        done, value = last_read
                        sp.wait_ge(done.sem, value)
                    rows = src.rearrange("(k p) n -> p k n", p=P)
                    n = rows.shape[2]
                    sp.dma_start(ring[:, i % RING, :, 0:n], rows).then_inc(slot_in[i % RING].sem, 16)

                def dense_read(c):
                    if c < ADA_CHUNKS:
                        return ada_ps, ada_ps.at(l, c + 1)
                    return {CH_MLA: (unit_ps, unit_ps.at(l, 4)), CH_Q: (unit_ps, unit_ps.at(l, 16)),
                            CH_K: (unit_ps, unit_ps.at(l, 20)), CH_V: (v_ps, v_ps.at(l, NB)),
                            CH_F: (unit_ps, unit_ps.at(l, UNITS)), CH_DFT: (fb_ps, fb_ps.at(l, 2)),
                            CH_OUT: (mix_ps, mix_ps.at(l, 4)), CH_OUT + 1: (mix_ps, mix_ps.at(l, KD))}[c]

                def pair_read(t, j):
                    i, part = divmod(j, 6)
                    if part < 4:
                        return gu_ps, gu_ps.at(t, 4 * i + part + 1)
                    return ye_ps, ye_ps.at(t, 2 * i + part - 3)

                def dense(c, src):
                    load(c, src, dense_read(c - RING) if c >= RING else pair_read(l * PAIRS, c - RING))

                for c in range(ADA_CHUNKS):
                    dense(c, a["w_ada"][l, :, c * 512:(c + 1) * 512])
                dense(CH_MLA, a["w_in"][l, :, C_CQ:C_END])
                dense(CH_Q, a["w_in"][l, :, C_Q:C_K])
                dense(CH_K, a["w_in"][l, :, C_K:C_V])
                load(CH_V, a["w_in"][l, :, C_V:C_CQ], dense_read(CH_MLA))
                load(CH_F, a["w_in"][l, :, C_F:C_Q], None)
                dense(CH_DFT, a["dft"])
                for c in range(2):
                    dense(CH_OUT + c, a["w_out"][l, :, c * 512:(c + 1) * 512])
                def expert_piece(pair, j):
                    i, part = divmod(j, 6)
                    if part < 4:
                        name, half = ("w_e_gate", "w_e_up")[part % 2], part // 2
                    else:
                        name, half = "w_e_down", part - 4
                    return a[name][l, pair * 2 + i, :, half * 512:(half + 1) * 512]

                for j in range(RING):
                    load(j, expert_piece(0, j), dense_read(DENSE_CHUNKS + j - RING))
                with sp.Fori(0, PAIRS - 1) as pair:
                    for j in range(RING, RING + PAIR_CHUNKS):
                        load(j, expert_piece(pair, j), pair_read(l * PAIRS + pair, j - RING))
                for j in range(RING, PAIR_CHUNKS):
                    load(j, expert_piece(PAIRS - 1, j), pair_read(l * PAIRS + PAIRS - 1, j - RING))

            sp.wait_ge(fin_v.sem, NB)
            sp.wait_ge(fin_a.sem, NB)
            out_rows = arena[:, 0:NB * D].rearrange("p (b d) -> p b d", b=NB)
            sp.dma_start(a["y_prompt"].rearrange("b n d -> (b n) d"), out_rows[:, 0, :]).then_inc(y_out.sem, 16)
            sp.dma_start(a["y_sample"].rearrange("b (j p) d -> p (b j) d", p=P), out_rows[:, 1:NB, :]).then_inc(y_out.sem, 16)
            sp.wait_ge(y_out.sem, y_out.at(1, 0))

        @block.gpsimd
        def _(g):
            g.memset(ones[:, :], 1.0).then_inc(fill_done.sem, 1)
            g.memset(wfour[:, :, :], 0.0).then_inc(fill_done.sem, 1)
            g.memset(cache_kpe[:, :], 0.0).then_inc(fill_done.sem, 1)


        def iterations(kind):
            return [(kind, h, b) for h in range(HEADS) for b in range(NB)]

        ITS = iterations("mla") + iterations("diff")

        def groups(it):
            if it < ATT_IT:
                return [it]
            return [ATT_IT + 2 * (it - ATT_IT), ATT_IT + 2 * (it - ATT_IT) + 1]

        def key_cols(b):
            return (0, CTX) if b == 0 else (CTX, KEYS)

        @block.tensor
        def _(pe):
            pe.wait_ge(const_in.sem, const_in.at(0, 0))
            pe.wait_ge(fill_done.sem, 3)
            pe.wait_ge(x_in.sem, x_in.at(0, 0))
            pe.sem_inc(gu_ps.sem, 2)
            pe.sem_inc(ye_ps.sem, 2)
            for k in range(KD):
                if k >= 2:
                    pe.wait_ge(xt_sb.sem, k - 1)
                for b in range(NB):
                    dst = ctx_bank[k % 2][:, 0:P] if b == 0 else lat_bank[k % 2][:, (b - 1) * P:b * P]
                    mm = pe.transpose(dst, x_rows[:, b, k * P:(k + 1) * P], ident)
                mm.then_inc(xt_ps.sem, 1)
            pe.wait_ge(cond_silu.sem, 1)
            pe.transpose(misc_bank[:, 0:3 * KD], cond_rows[:, :], ident[0:3 * KD, 0:3 * KD]).then_inc(cond_ps.sem, 1)
            pe.wait_ge(cond_sb.sem, 1)
            pe.wait_ge(xt_sb.sem, KD)
            cond = condT[:, 0:2 * KD].rearrange("p (s k) -> p k s", s=2)

            def slot(turn, i):
                pe.wait_ge(slot_in[i % RING].sem, turn + (i // RING) * 16 + 16)
                return ring[:, i % RING, :, :]

            def product(lat, ctx_out, weights, rhs, steps):
                for k in range(steps):
                    w = weights(k)
                    x = rhs(k)
                    flags = dict(start=(k == 0), stop=(k == steps - 1))
                    pe.matmul(lat, w, x[:, CTX:TOK], **flags)
                    mm = pe.matmul(ctx_out, w, x[:, 0:CTX], **flags)
                return mm

            def wide_norm(l, which):
                for k in range(KD):
                    pe.wait_ge(sq_done.sem, sq_done.at(l, which * KD + k + 1))
                    flags = dict(start=(k == 0), stop=(k == KD - 1))
                    pe.matmul(sum_lat, ones[:, :], scr[:, k % 2, CTX:TOK], **flags)
                    pe.matmul(sum_ctx, ones[:, :], scr[:, k % 2, 0:CTX], **flags).then_inc(sq_used.sem, 1)

            with pe.Fori(0, DEPTH) as l:
                turn = l * (LAYER_CHUNKS // RING * 16)

                pe.wait_ge(small_in.sem, small_in.at(l + 1, 0))
                pe.transpose(misc_bank[:, 0:N_VEC], vec_rows[:, :], ident[0:N_VEC, 0:N_VEC]).then_inc(vec_ps.sem, 1)

                for c in range(ADA_CHUNKS):
                    w = slot(turn, c)
                    if c >= 2:
                        pe.wait_ge(ada_sb.sem, ada_sb.at(l, c - 1))
                    for m in range(4):
                        for k in range(KD):
                            mm = pe.matmul(lat_bank[c % 2][:, 2 * m:2 * m + 2], w[:, k, m * P:(m + 1) * P], cond[:, k, :],
                                           start=(k == 0), stop=(k == KD - 1))
                    mm.then_inc(ada_ps.sem, 1)

                wide_norm(l, 0)
                pe.wait_ge(ada_sb.sem, ada_sb.at(l, ADA_CHUNKS))

                def unit_banks(u):
                    if u >= 2:
                        pe.wait_ge(unit_lat.sem, unit_lat.at(l, u - 1))
                        pe.wait_ge(unit_ctx.sem, unit_ctx.at(l, u - 1))
                    return lat_bank[u % 2], ctx_bank[u % 2][:, 0:CTX]

                def turn_pairs(r, rows, unit):
                    pe.wait_ge(unit_lat.sem, unit_lat.at(l, unit + 1))
                    if r >= 1:
                        pe.wait_ge(rope_sb.sem, rope_sb.at(l, r))
                    m = rot_diff if rows == slice(0, P) else rot_mla
                    pe.matmul(rot_bank[rows, :], m[rows, rows], rope_a[rows, r % 2, :], start=True, stop=True)\
                      .then_inc(rope_ps.sem, 1)


                w = slot(turn, CH_MLA)
                pe.wait_ge(h_done.sem, h_done.at(l, KD))
                for u, c0, m in ((0, 0, P), (1, P, P), (2, 2 * P, P), (3, C_END - C_CQ - QM, QM)):
                    lat, cx = unit_banks(u)
                    product(lat[0:m, :], cx[0:m, :], lambda k: w[:, k, c0:c0 + m], lambda k: hT[:, k, :], KD)\
                        .then_inc(unit_ps.sem, 1)

                def narrow_sum(n, first_sq, blocks):
                    for j in range(blocks):
                        pe.wait_ge(nsq_done.sem, nsq_done.at(l, first_sq + j + 1))
                        flags = dict(start=(j == 0), stop=(j == blocks - 1))
                        s = (first_sq + j) % 2
                        pe.matmul(sum_lat, ones[:, :], scr[:, s, CTX:TOK], **flags)
                        mm = pe.matmul(sum_ctx, ones[:, :], scr[:, s, 0:CTX], **flags)
                    mm.then_inc(nsum_ps.sem, 1)

                narrow_sum(0, 0, 2)
                pe.wait_ge(unit_lat.sem, unit_lat.at(l, 4))
                pe.transpose(misc_bank[:, 0:P], cache_ckv[:, :], ident)
                pe.transpose(misc_bank[0:QM, P:2 * P], cache_kpe[:, :], ident).then_inc(tr_ps.sem, 1)
                kpe_at = slice(NOPE, QM)
                pe.matmul(rot_bank[kpe_at, :], rot_mla[kpe_at, kpe_at], rope_a[kpe_at, 0, :], start=True, stop=True)\
                  .then_inc(rope_ps.sem, 1)
                pe.wait_ge(nrms_done.sem, nrms_done.at(l, 1))
                narrow_sum(1, 2, 1)

                pe.wait_ge(nscaled.sem, nscaled.at(l, 1))
                for h in range(HEADS):
                    u = 4 + h
                    lat, cx = unit_banks(u)
                    product(lat[0:QM, :], cx[0:QM, :], lambda k: wuq[:, k, h * QM:(h + 1) * QM], lambda k: cqT[:, k, :], 2)\
                        .then_inc(unit_ps.sem, 1)
                    if h >= 1:
                        turn_pairs(h, slice(0, QM), u - 1)
                pe.wait_ge(nscaled.sem, nscaled.at(l, 2))
                pe.wait_ge(tr_sb.sem, tr_sb.at(l, 1))
                for h in range(HEADS):
                    u = 8 + h
                    lat, _ = unit_banks(u)
                    w0 = wukv[:, h * (NOPE + VDIM):h * (NOPE + VDIM) + NOPE]
                    pe.matmul(lat[0:NOPE, :], w0, ckvT[:, 0:512], start=True, stop=True)
                    pe.matmul(ctx_bank[u % 2][0:NOPE, 0:256], w0, ckvT[:, 512:768], start=True, stop=True)\
                      .then_inc(unit_ps.sem, 1)
                    if h == 0:
                        turn_pairs(4, slice(0, QM), u - 1)
                wv = wukv[:, :].rearrange("p (h c) -> p h c", h=HEADS)[:, :, NOPE:NOPE + VDIM]
                for b in range(NB + 1):
                    if b >= 2:
                        pe.wait_ge(vm_sb.sem, vm_sb.at(l, b - 1))
                    dst = S[0][:, (b % 2) * 512:(b % 2) * 512 + HEADS * VDIM]
                    if b == 0:
                        pe.wait_ge(nrms_done.sem, nrms_done.at(l, 2))
                    pe.matmul(dst, ckvT[:, b * P:(b + 1) * P], wv, start=True, stop=True).then_inc(vm_ps.sem, 1)
                pe.wait_ge(kpe_spread.sem, kpe_spread.at(l, 1))
                pe.transpose(misc_bank[:, 0:P], ckvT[:, 0:P], ident)
                pe.transpose(misc_bank[:, P:P + ROPE], kpeT[NOPE:QM, 0:P], ident[NOPE:QM, NOPE:QM]).then_inc(tr_ps.sem, 1)
                pe.wait_ge(tr_sb.sem, tr_sb.at(l, 2))
                pe.wait_ge(rope_sb.sem, rope_sb.at(l, 5))
                pe.wait_ge(vm_sb.sem, vm_sb.at(l, NB + 1))

                def scores(it):
                    kind, h, b = ITS[it]
                    k0, nk = key_cols(b)
                    for comp, g in enumerate(groups(it)):
                        if g % GROUPS >= 2:
                            pe.wait_ge(exp_done.sem, exp_done.at(l, g - 1))
                        rows = slice(0, QM) if kind == "mla" else slice(comp * DH, (comp + 1) * DH)
                        q = qT[rows, h, b * P:(b + 1) * P]
                        bank = S[g % 2]
                        n = min(nk, 512)
                        mm = pe.matmul(bank[:, 0:n], q, kT[rows, h, k0:k0 + n], start=True, stop=True)
                        if nk > n:
                            mm = pe.matmul(bank[:, n:nk], q, kT[rows, h, k0 + n:k0 + nk], start=True, stop=True)
                        mm.then_inc(sc_ps.sem, 1)

                def turn_probs(it):
                    _, h, b = ITS[it]
                    pe.wait_ge(probs_done.sem, probs_done.at(l, it + 1))
                    if it >= 1:
                        pe.wait_ge(pt_sb.sem, pt_sb.at(l, it))
                    for j in range(1 if b == 0 else NB):
                        mm = pe.transpose(T[:, j * P:(j + 1) * P], probs[:, it % 2, 0, j * P:(j + 1) * P], ident)
                    mm.then_inc(pt_ps.sem, 1)

                def apply_probs(it):
                    kind, h, b = ITS[it]
                    pe.wait_ge(pt_sb.sem, pt_sb.at(l, it + 1))
                    if it >= 2:
                        pe.wait_ge(o_sb.sem, o_sb.at(l, it - 1))
                    blocks = [0] if b == 0 else [1, 2, 3, 4, 5]
                    c0 = (it % 2) * 512
                    for j, kb in enumerate(blocks):
                        if kind == "mla":
                            half = (h % 2) * VDIM
                            out = U[half:half + VDIM, c0:c0 + P]
                            v = vm_rows[:, kb, h * VDIM:(h + 1) * VDIM]
                        else:
                            out = U[:, c0:c0 + P]
                            v = (v_rows[:, kb, h * P:(h + 1) * P] if kb < NB else cache_v[:, h * P:(h + 1) * P])
                        mm = pe.matmul(out, v, probsT[:, it % 2, j, :], start=(j == 0), stop=(j == len(blocks) - 1))
                    mm.then_inc(o_ps.sem, 1)

                def attention(first, last):
                    for i in range(first, last + 2):
                        if i < last:
                            scores(i)
                        if first <= i - 1 < last:
                            turn_probs(i - 1)
                        if i - 2 >= first:
                            apply_probs(i - 2)

                pe.wait_ge(unit_lat.sem, unit_lat.at(l, 12))
                pe.wait_ge(unit_ctx.sem, unit_ctx.at(l, 12))
                attention(0, ATT_IT)
                pe.wait_ge(o_sb.sem, o_sb.at(l, ATT_IT))

                for c, u0 in ((CH_Q, 12), (CH_K, 16)):
                    w = slot(turn, c)
                    for h in range(HEADS):
                        u = u0 + h
                        lat, cx = unit_banks(u)
                        product(lat, cx, lambda k: w[:, k, h * P:(h + 1) * P], lambda k: hT[:, k, :], KD)\
                            .then_inc(unit_ps.sem, 1)
                        if u > 12:
                            turn_pairs(4 + u - 12, slice(0, P), u - 1)
                w = slot(turn, CH_V)
                for b in range(NB):
                    if b >= 2:
                        pe.wait_ge(v_sb.sem, v_sb.at(l, b - 1))
                    dst = S[0][:, (b % 2) * 512:(b % 2 + 1) * 512]
                    for k in range(KD):
                        mm = pe.matmul(dst, hT[:, k, b * P:(b + 1) * P], w[:, k, :], start=(k == 0), stop=(k == KD - 1))
                    mm.then_inc(v_ps.sem, 1)
                    if b == 0:
                        turn_pairs(12, slice(0, P), 19)
                w = slot(turn, CH_F)
                for j in range(2):
                    lat, cx = unit_banks(20 + j)
                    product(lat, cx, lambda k: w[:, k, j * P:(j + 1) * P], lambda k: hT[:, k, :], KD)\
                        .then_inc(unit_ps.sem, 1)

                for h in range(HEADS):
                    mm = pe.transpose(misc_bank[:, h * P:(h + 1) * P], cache_k[:, h * P:(h + 1) * P], ident)
                mm.then_inc(tr_ps.sem, 1)
                pe.wait_ge(tr_sb.sem, tr_sb.at(l, 3))
                for h in range(HEADS):
                    mm = pe.transpose(misc_bank[:, h * P:(h + 1) * P], kT[:, h, 0:P], ident)
                mm.then_inc(tr_ps.sem, 1)

                pe.wait_ge(v_sb.sem, v_sb.at(l, NB))
                for j in range(2):
                    for part in range(2):
                        mm = pe.matmul(S[0][:, j * 512 + part * P:j * 512 + (part + 1) * P],
                                       consts[:, K_CHAN + part * P:K_CHAN + (part + 1) * P], wfour[:, j, :],
                                       start=True, stop=True)
                    mm.then_inc(cw_ps.sem, 1)
                pe.wait_ge(cw_sb.sem, cw_sb.at(l, 2))
                pe.wait_ge(unit_lat.sem, unit_lat.at(l, UNITS))
                pe.wait_ge(unit_ctx.sem, unit_ctx.at(l, UNITS))
                for b in range(NB):
                    if b >= 2:
                        pe.wait_ge(fa_sb.sem, fa_sb.at(l, b - 1))
                    for j in range(2):
                        mm = pe.matmul(lat_bank[b % 2][:, j * 256:(j + 1) * 256], zfT[:, j, b * P:(b + 1) * P],
                                       chanw[:, j, :, :], start=True, stop=True)
                    mm.then_inc(fa_ps.sem, 1)
                w = slot(turn, CH_DFT)
                for j in range(2):
                    lat, cx = S[0][:, 0:512], ctx_bank[1][:, 0:CTX]
                    if j == 0:
                        lat, cx = U[:, 0:512], S[0][:, 512:512 + CTX]
                    pe.wait_ge(fa_sb.sem, fa_sb.at(l, NB))
                    for part in range(2):
                        cols = slice(part * P, (part + 1) * P)
                        for b in range(4):
                            pe.matmul(lat, chan_rows[:, b + 1, j, cols], w[:, 4 * part + b, :],
                                      start=(part == 0 and b == 0), stop=(part == 1 and b == 3))
                    for part in range(2):
                        cols = slice(part * P, (part + 1) * P)
                        mm = pe.matmul(cx, chan_rows[:, 0, j, cols], consts[:, K_SEQX + part * CTX:K_SEQX + (part + 1) * CTX],
                                       start=(part == 0), stop=(part == 1))
                    mm.then_inc(fb_ps.sem, 1)

                pe.wait_ge(fb_sb.sem, fb_sb.at(l, 2))
                pe.wait_ge(rope_sb.sem, rope_sb.at(l, ROPES))
                pe.wait_ge(tr_sb.sem, tr_sb.at(l, 4))
                attention(ATT_IT, 2 * ATT_IT)
                pe.wait_ge(exp_done.sem, exp_done.at(l, GROUPS))
                for h in range(HEADS):
                    if h >= 1:
                        pe.wait_ge(nrms_done.sem, nrms_done.at(l, 2 + h))
                    narrow_sum(2 + h, 3 + h, 1)

                pe.wait_ge(nscaled.sem, nscaled.at(l, 6))
                pe.wait_ge(o_sb.sem, o_sb.at(l, 2 * ATT_IT))
                for c in range(2):
                    w = slot(turn, CH_OUT + c)
                    for m in range(4):
                        n = 4 * c + m
                        if n >= 2:
                            pe.wait_ge(mix_sb.sem, mix_sb.at(l, n - 1))
                        product(lat_bank[n % 2], ctx_bank[n % 2][:, 0:CTX], lambda k: w[:, k, m * P:(m + 1) * P],
                                lambda k: yT[:, k, :] if k < 6 else y_mla[:, k - 6, :], KD).then_inc(mix_ps.sem, 1)

                wide_norm(l, 1)
                pe.wait_ge(h_done.sem, h_done.at(l, 2 * KD))
                pe.wait_ge(mix_sb.sem, mix_sb.at(l, KD))
                for b in range(NB):
                    for k in range(KD):
                        mm = pe.matmul(T[:, b * E_N:(b + 1) * E_N], hT[:, k, b * P:(b + 1) * P], wrt[:, k, :],
                                       start=(k == 0), stop=(k == KD - 1))
                mm.then_inc(lg_ps.sem, 1)
                pe.wait_ge(rms_done.sem, rms_done.at(l, 2))
                def rows_of_h(b):
                    if b >= 2:
                        pe.wait_ge(hr_v.sem, hr_v.at(l, b - 1))
                        pe.wait_ge(hr_a.sem, hr_a.at(l, b - 1))
                    for k in range(KD):
                        mm = pe.transpose(S[b % 2][:, k * P:(k + 1) * P], hT[:, k, b * P:(b + 1) * P], ident)
                    mm.then_inc(hr_ps.sem, 1)

                for b in range(NB - 1):
                    rows_of_h(b)
                pe.wait_ge(aff_rows.sem, aff_rows.at(l, 1))
                for b in range(NB):
                    dst = U[0:E_N, 512:512 + P] if b == 0 else U[0:E_N, (b - 1) * P:b * P]
                    mm = pe.transpose(dst, lg[:, b, :], ident)
                mm.then_inc(aff_ps.sem, 1)
                pe.wait_ge(pos_done.sem, pos_done.at(l, 1))
                rows_of_h(NB - 1)
                for b in range(NB):
                    mm = pe.transpose(T[:, b * E_N:(b + 1) * E_N], pos[0:E_N, b * P:(b + 1) * P], ident[0:E_N, 0:E_N])
                mm.then_inc(pr_ps.sem, 1)
                with pe.Fori(0, PAIRS) as pair:
                    t = l * PAIRS + pair
                    pturn = turn + (DENSE_CHUNKS // RING * 16) + pair * (PAIR_CHUNKS // RING * 16)
                    pe.wait_ge(hr_v.sem, hr_v.at(l, NB))
                    pe.wait_ge(hr_a.sem, hr_a.at(l, NB))
                    for i in range(2):
                        pe.wait_ge(pick_done.sem, pick_done.at(t, i + 1))
                        if i == 1:
                            pe.wait_ge(xs_v.sem, xs_v.at(t, 1))
                            pe.wait_ge(xs_a.sem, xs_a.at(t, 1))
                        for k in range(KD):
                            c0 = (k // 4) * 512 + (k % 4) * SLOT_TOK
                            for b in range(4):
                                pe.matmul(S[0][:, c0:c0 + CAP], h_rows[:, b + 1, k * P:(k + 1) * P],
                                          pick[:, i, b * CAP:(b + 1) * CAP], start=(b == 0), stop=(b == 3))
                            mm = pe.matmul(S[0][:, c0 + CAP:c0 + SLOT_TOK], h_rows[:, 0, k * P:(k + 1) * P],
                                           pick[:, i, 4 * CAP:4 * CAP + CAPX], start=True, stop=True)
                        mm.then_inc(xs_ps.sem, 1)
                        pe.wait_ge(xs_v.sem, xs_v.at(t, i + 1))
                        pe.wait_ge(xs_a.sem, xs_a.at(t, i + 1))
                        for half in range(2):
                            gu = (S[1], T)[half]
                            if i == 1:
                                pe.wait_ge(hm_done.sem, hm_done.at(t, half + 1))
                            for part in range(2):
                                w = slot(pturn, 6 * i + 2 * half + part)
                                for m in range(4):
                                    c0 = part * 512 + m * SLOT_TOK
                                    for k in range(KD):
                                        mm = pe.matmul(gu[:, c0:c0 + SLOT_TOK], w[:, k, m * P:(m + 1) * P], xs[:, i, k, :],
                                                       start=(k == 0), stop=(k == KD - 1))
                                mm.then_inc(gu_ps.sem, 1)
                        pe.wait_ge(hm_done.sem, hm_done.at(t, 2 * i + 2))
                        for half in range(2):
                            w = slot(pturn, 6 * i + 4 + half)
                            if i == 1:
                                pe.wait_ge(ye_sb.sem, ye_sb.at(t, half + 1))
                            for m in range(4):
                                c0 = half * 512 + m * SLOT_TOK
                                for k in range(KD):
                                    mm = pe.matmul(U[:, c0:c0 + SLOT_TOK], w[:, k, m * P:(m + 1) * P], hm[:, i, k, :],
                                                   start=(k == 0), stop=(k == KD - 1))
                            mm.then_inc(ye_ps.sem, 1)
                    pe.wait_ge(sel_done.sem, sel_done.at(t, 1))
                    lat_sel = sel[:, :, :].rearrange("e i c -> e (i c)")
                    ctx_sel = selx[:, :, :].rearrange("e i c -> e (i c)")
                    pe.matmul(T[:, 0:LAT], lat_sel, pos[0:E_N, CTX:TOK], start=True, stop=True)
                    pe.matmul(T[:, 512:512 + LAT], lat_sel, aff[0:E_N, CTX:TOK], start=True, stop=True)
                    pe.matmul(S[1][0:2 * CAPX, 0:CTX], ctx_sel, pos[0:E_N, 0:CTX], start=True, stop=True)
                    pe.matmul(S[1][0:2 * CAPX, 512:512 + CTX], ctx_sel, aff[0:E_N, 0:CTX], start=True, stop=True)\
                      .then_inc(sel_ps.sem, 1)
                    pe.wait_ge(ye_sb.sem, ye_sb.at(t, 4))
                    for k in range(KD):
                        mm = pe.transpose(S[0][:, k * P:(k + 1) * P], ye[:, k, :], ident)
                    mm.then_inc(yr_ps.sem, 1)
                    for k in range(KD):
                        mm = pe.transpose(U[0:2 * CAPX, k * P:(k + 1) * P], yex[:, k, :], ident)
                    mm.then_inc(yr_ps.sem, 1)
                    pe.wait_ge(back_done.sem, back_done.at(t, 1))
                    pe.wait_ge(yr_v.sem, yr_v.at(t, 2))
                    pe.wait_ge(yr_a.sem, yr_a.at(t, 2))
                    for n in range(KD):
                        if n >= 2:
                            pe.wait_ge(add_sb.sem, add_sb.at(t, n - 1))
                        pe.matmul(lat_bank[n % 2], ye_rows[:, n * P:(n + 1) * P], back[:, :], start=True, stop=True)
                        pe.matmul(ctx_bank[n % 2][:, 0:CTX], yex_rows[0:2 * CAPX, n * P:(n + 1) * P], backx[0:2 * CAPX, :],
                                  start=True, stop=True).then_inc(add_ps.sem, 1)
                    pe.wait_ge(add_sb.sem, add_sb.at(t, KD))

            wide_norm(DEPTH, 0)
            pe.wait_ge(xn_done.sem, xn_done.at(DEPTH, KD))
            for b in range(NB):
                if b >= 2:
                    pe.wait_ge(fin_v.sem, b - 1)
                    pe.wait_ge(fin_a.sem, b - 1)
                if b == 0:
                    pe.wait_ge(rms_done.sem, rms_done.at(DEPTH, 1))
                for k in range(KD):
                    mm = pe.transpose(S[b % 2][:, k * P:(k + 1) * P], hT[:, k, b * P:(b + 1) * P], ident)
                mm.then_inc(fin_ps.sem, 1)

        @block.scalar
        def _(act):
            act.wait_ge(const_in.sem, const_in.at(0, 0))
            act.activation(cond_e[:, :], cond_rows[0:2 * KD, :], ACT.Exp, scale=-1.0).then_inc(cond_exp.sem, 1)

            def root(n_feat, ready, value, l, s, done):
                act.wait_ge(ready, value)
                act.activation(rstd[:, CTX:TOK], sum_lat, ACT.Ln, bias=eps, scale=1.0 / n_feat)
                act.activation(rstd[:, 0:CTX], sum_ctx, ACT.Ln, bias=eps, scale=1.0 / n_feat).then_inc(step_a.sem, 1)
                act.wait_ge(step_a.sem, step_a.at(l, s))
                act.activation(rstd[:, :], rstd[:, :], ACT.Exp, scale=-0.5).then_inc(done, 1)

            def squares(l, which):
                for k in range(KD):
                    if k >= 2:
                        act.wait_ge(sq_used.sem, sq_used.at(l, which * KD + k - 1))
                    if which == 1:
                        act.wait_ge(mix_sb.sem, mix_sb.at(l, k + 1))
                    act.activation(scr[:, k % 2, :], xT[:, k, :], ACT.Square).then_inc(sq_done.sem, 1)

            def modulate(l, which):
                for k in range(KD):
                    act.wait_ge(xn_done.sem, xn_done.at(l, which * KD + k + 1))
                    sh = 3 * which * KD + k
                    act.activation(hT[:, k, 0:CTX], hT[:, k, 0:CTX], ACT.Identity, bias=mod[:, sh, 0:1],
                                   scale=gain[:, which, k, 0:1])
                    act.activation(hT[:, k, CTX:TOK], hT[:, k, CTX:TOK], ACT.Identity, bias=mod[:, sh, 1:2],
                                   scale=gain[:, which, k, 1:2]).then_inc(h_done.sem, 1)

            act.wait_ge(xt_sb.sem, KD)
            with act.Fori(0, DEPTH) as l:
                act.wait_ge(lam_prod.sem, lam_prod.at(l, 1))
                act.activation(lamw[:, 0:2], lamw[:, 0:2], ACT.Exp).then_inc(lam_exp.sem, 1)
                act.wait_ge(add_sb.sem, add_sb.at(l * PAIRS, 0))
                squares(l, 0)
                root(D, sq_used.sem, sq_used.at(l, KD), l, 1, rms_done.sem)
                act.wait_ge(gain_sb.sem, gain_sb.at(l, 1))
                modulate(l, 0)

                def ctx_copy(u, dst):
                    act.wait_ge(unit_ps.sem, unit_ps.at(l, u + 1))
                    m = dst.shape[0]
                    act.activation(dst, ctx_bank[u % 2][0:m, 0:dst.shape[1]], ACT.Copy).then_inc(unit_ctx.sem, 1)

                def narrow_square(n, src, lat_ready):
                    act.wait_ge(*lat_ready)
                    act.activation(scr[:, n % 2, :], src, ACT.Square).then_inc(nsq_done.sem, 1)

                ctx_copy(0, cqT[:, 0, 0:CTX])
                ctx_copy(1, cqT[:, 1, 0:CTX])
                act.wait_ge(unit_ctx.sem, unit_ctx.at(l, 2))
                narrow_square(0, cqT[:, 0, :], (unit_lat.sem, unit_lat.at(l, 1)))
                narrow_square(1, cqT[:, 1, :], (unit_lat.sem, unit_lat.at(l, 2)))
                ctx_copy(2, ckvT[:, 0:CTX])
                act.wait_ge(unit_ps.sem, unit_ps.at(l, 4))
                act.activation(kpeT[NOPE:QM, 0:CTX], ctx_bank[1][NOPE:QM, 0:CTX], ACT.Copy).then_inc(unit_ctx.sem, 1)
                root(2 * P, nsum_ps.sem, nsum_ps.at(l, 1), l, 2, nrms_done.sem)
                act.wait_ge(unit_ctx.sem, unit_ctx.at(l, 3))
                narrow_square(2, ckvT[:, 0:TOK], (unit_lat.sem, unit_lat.at(l, 3)))
                act.wait_ge(tr_ps.sem, tr_ps.at(l, 1))
                act.activation(ckvT[:, TOK:TOK + PAST], misc_bank[:, 0:P], ACT.Copy)
                act.activation(kpeT[NOPE:QM, TOK:TOK + PAST], misc_bank[NOPE:QM, P:2 * P], ACT.Copy).then_inc(tr_sb.sem, 1)
                act.wait_ge(nscaled.sem, nscaled.at(l, 1))
                root(P, nsum_ps.sem, nsum_ps.at(l, 2), l, 3, nrms_done.sem)
                for h in range(HEADS):
                    ctx_copy(4 + h, qT[0:QM, h, 0:CTX])
                for h in range(HEADS):
                    ctx_copy(8 + h, kT[0:NOPE, h, 512:768])
                for b in range(NB + 1):
                    act.wait_ge(vm_ps.sem, vm_ps.at(l, b + 1))
                    act.activation(vm_rows[:, b, :], S[0][:, (b % 2) * 512:(b % 2) * 512 + HEADS * VDIM], ACT.Copy)\
                       .then_inc(vm_sb.sem, 1)
                act.wait_ge(tr_ps.sem, tr_ps.at(l, 2))
                act.activation(ckv_rows[:, :], misc_bank[:, 0:P], ACT.Copy)
                act.activation(kpe_rows[:, :], misc_bank[:, P:P + ROPE], ACT.Copy).then_inc(tr_sb.sem, 1)
                act.wait_ge(tr_sb.sem, tr_sb.at(l, 2))
                act.dma_start(a["new_mla_ckv"][0, l], ckv_rows[:, :]).then_inc(outs_done.sem, 16)
                act.dma_start(a["new_mla_kpe"][0, l], kpe_rows[:, :]).then_inc(outs_done.sem, 16)

                def attention(first, last):
                    for i in range(first, last + 1):
                        if i < last:
                            kind, h, b = ITS[i]
                            nk = key_cols(b)[1]
                            for comp, g in enumerate(groups(i)):
                                act.wait_ge(negm_done.sem, negm_done.at(l, g + 1))
                                act.activation(probs[:, i % 2, comp, 0:nk], S[g % 2][:, 0:nk], ACT.Exp, bias=negm[:, g % 2:g % 2 + 1],
                                               scale=MLA_SCALE if kind == "mla" else DIFF_SCALE,
                                               accum_out=ssum[:, i % 2, comp:comp + 1]).then_inc(exp_done.sem, 1)
                        if i > first:
                            it = i - 1
                            _, h, b = ITS[it]
                            n = P if b == 0 else KEYS
                            act.wait_ge(pt_ps.sem, pt_ps.at(l, it + 1))
                            if it - 2 >= 0:
                                act.wait_ge(o_ps.sem, o_ps.at(l, it - 1))
                            act.activation(probsT[:, it % 2, :, :].rearrange("p j q -> p (j q)")[:, 0:n], T[:, 0:n], ACT.Copy)\
                               .then_inc(pt_sb.sem, 1)

                attention(0, ATT_IT)
                for h in range(HEADS):
                    ctx_copy(12 + h, qT[:, h, 0:CTX])
                for h in range(HEADS):
                    ctx_copy(16 + h, kT[:, h, 0:CTX])
                for b in range(NB):
                    act.wait_ge(v_ps.sem, v_ps.at(l, b + 1))
                    act.activation(v_rows[:, b, :], S[0][:, (b % 2) * 512:(b % 2 + 1) * 512], ACT.Copy).then_inc(v_sb.sem, 1)
                for j in range(2):
                    ctx_copy(20 + j, zfT[:, j, 0:CTX])
                act.wait_ge(v_sb.sem, v_sb.at(l, 1))
                act.dma_start(a["new_diff_v"][0, l].rearrange("t h d -> t (h d)"), v_rows[:, 0, :]).then_inc(outs_done.sem, 16)
                act.wait_ge(tr_ps.sem, tr_ps.at(l, 3))
                act.activation(kT[:, :, TOK:TOK + PAST], misc_bank.rearrange("p (h t) -> p h t", h=HEADS), ACT.Copy)\
                   .then_inc(tr_sb.sem, 1)
                act.wait_ge(tr_ps.sem, tr_ps.at(l, 4))
                act.activation(k_rows[:, :], misc_bank, ACT.Copy).then_inc(tr_sb.sem, 1)
                act.wait_ge(tr_sb.sem, tr_sb.at(l, 4))
                act.dma_start(a["new_diff_k"][0, l].rearrange("t h d -> t (h d)"), k_rows[:, :]).then_inc(outs_done.sem, 16)
                for j in range(2):
                    act.wait_ge(cw_ps.sem, cw_ps.at(l, j + 1))
                    act.activation(chanw[:, j, :, :].rearrange("p a e -> p (a e)"), S[0][:, j * 512:j * 512 + 2 * P], ACT.Copy)\
                       .then_inc(cw_sb.sem, 1)
                for b in range(NB):
                    act.wait_ge(fa_ps.sem, fa_ps.at(l, b + 1))
                    act.activation(chan_rows[:, b, :, :].rearrange("p j e -> p (j e)"), lat_bank[b % 2], ACT.Copy)\
                       .then_inc(fa_sb.sem, 1)
                attention(ATT_IT, 2 * ATT_IT)
                act.wait_ge(o_sb.sem, o_sb.at(l, 2 * ATT_IT))
                for h in range(HEADS):
                    if h >= 1:
                        act.wait_ge(nsum_ps.sem, nsum_ps.at(l, 2 + h))
                    narrow_square(3 + h, yT[:, 2 + h, :], (o_sb.sem, o_sb.at(l, 2 * ATT_IT)))
                    if h >= 1:
                        act.wait_ge(nscaled.sem, nscaled.at(l, 2 + h))
                    root(P, nsum_ps.sem, nsum_ps.at(l, 3 + h), l, 4 + h, nrms_done.sem)

                squares(l, 1)
                act.wait_ge(nscaled.sem, nscaled.at(l, 6))
                root(D, sq_used.sem, sq_used.at(l, 2 * KD), l, 8, rms_done.sem)
                modulate(l, 1)
                act.wait_ge(lg_shift.sem, lg_shift.at(l, 1))
                act.activation(lg[:, :, :], lg[:, :, :], ACT.Exp).then_inc(lg_exp.sem, 1)
                act.wait_ge(outs_done.sem, outs_done.at(l + 1, 0))
                for b in range(NB):
                    act.wait_ge(hr_ps.sem, hr_ps.at(l, b + 1))
                    act.activation(h_rows[:, b, 512:1024], S[b % 2][:, 512:1024], ACT.Copy).then_inc(hr_a.sem, 1)
                with act.Fori(0, PAIRS) as pair:
                    t = l * PAIRS + pair
                    for i in range(2):
                        act.wait_ge(xs_ps.sem, xs_ps.at(t, i + 1))
                        act.activation(xs[:, i, 4:8, :].rearrange("p k c -> p (k c)"), S[0][:, 512:512 + 4 * SLOT_TOK], ACT.Copy)\
                           .then_inc(xs_a.sem, 1)
                        for half in range(2):
                            act.wait_ge(gu_ps.sem, gu_ps.at(t, 4 * i + 2 * half + 1))
                            if 2 * i + half >= 2:
                                act.wait_ge(hm_done.sem, hm_done.at(t, 2 * i + half - 1))
                            act.activation(scr[:, half, 0:4 * SLOT_TOK], (S[1], T)[half][:, 0:4 * SLOT_TOK], ACT.Silu)\
                               .then_inc(silu_done.sem, 1)
                    act.wait_ge(sel_ps.sem, sel_ps.at(t, 1))
                    act.activation(rope_a[:, 0, :], T[:, 512:1024], ACT.Copy)
                    act.activation(rope_a[0:2 * CAPX, 1, 0:CTX], S[1][0:2 * CAPX, 512:512 + CTX], ACT.Copy).then_inc(gate_sb.sem, 1)
                    act.wait_ge(yr_ps.sem, yr_ps.at(t, 1))
                    act.activation(ye_rows[:, 512:1024], S[0][:, 512:1024], ACT.Copy).then_inc(yr_a.sem, 1)
                    act.wait_ge(yr_ps.sem, yr_ps.at(t, 2))
                    act.activation(yex_rows[0:2 * CAPX, 512:1024], U[0:2 * CAPX, 512:1024], ACT.Copy).then_inc(yr_a.sem, 1)

            act.wait_ge(add_sb.sem, add_sb.at(DEPTH * PAIRS, 0))
            squares(DEPTH, 0)
            root(D, sq_used.sem, sq_used.at(DEPTH, KD), DEPTH, 1, rms_done.sem)
            for b in range(NB):
                act.wait_ge(fin_ps.sem, b + 1)
                act.activation(arena[:, b * D + 512:(b + 1) * D], S[b % 2][:, 512:1024], ACT.Copy).then_inc(fin_a.sem, 1)

        @block.vector
        def _(ve):
            count = [0]

            def link(ins):
                count[0] += 1
                ins.then_inc(step_v, 1)
                ve.wait_ge(step_v, count[0])

            ve.wait_ge(cond_exp.sem, 1)
            link(ve.tensor_scalar(cond_e[:, :], cond_e[:, :], 1.0, None, ALU.add))
            link(ve.reciprocal(cond_e[:, :], cond_e[:, :]))
            ve.tensor_tensor(cond_rows[0:2 * KD, :], cond_rows[0:2 * KD, :], cond_e[:, :], ALU.mult).then_inc(cond_silu.sem, 1)
            for k in range(KD):
                ve.wait_ge(xt_ps.sem, k + 1)
                ve.tensor_copy(xT[:, k, 0:CTX], ctx_bank[k % 2][:, 0:CTX])
                ve.tensor_copy(xT[:, k, CTX:TOK], lat_bank[k % 2]).then_inc(xt_sb.sem, 1)
            ve.wait_ge(cond_ps.sem, 1)
            ve.tensor_copy(condT[:, :], misc_bank[:, 0:3 * KD]).then_inc(cond_sb.sem, 1)
            ve.sem_inc(add_sb.sem, 1)
            ve.sem_inc(pr_sb.sem, 1)

            def normalise(l, which):
                ve.wait_ge(rms_done.sem, rms_done.at(l, which + 1))
                for k in range(KD):
                    ve.tensor_tensor(hT[:, k, :], xT[:, k, :], rstd[:, :], ALU.mult).then_inc(xn_done.sem, 1)

            with ve.Fori(0, DEPTH) as l:
                ve.sem_clear(step_v)
                count[0] = 0
                ve.wait_ge(small_in.sem, small_in.at(l + 1, 0))
                pairs = dlam[:, :, :].rearrange("p (a b) d -> p a b d", b=2)
                link(ve.tensor_tensor(dprod[:, :, :], pairs[:, :, 0, :], pairs[:, :, 1, :], ALU.mult))
                ve.reduce_sum(lamw[:, 0:2], dprod[:, :, :], AX.X).then_inc(lam_prod.sem, 1)
                ve.wait_ge(vec_ps.sem, vec_ps.at(l, 1))
                ve.tensor_copy(vecT[:, :], misc_bank[:, 0:N_VEC]).then_inc(vec_sb.sem, 1)
                ve.wait_ge(vec_sb.sem, vec_sb.at(l, 1))
                for c in range(ADA_CHUNKS):
                    ve.wait_ge(ada_ps.sem, ada_ps.at(l, c + 1))
                    ve.tensor_tensor(mod[:, 4 * c:4 * c + 4, :], lat_bank[c % 2][:, 0:8].rearrange("p (m s) -> p m s", s=2),
                                     vecT[:, 4 * c:4 * c + 4].unsqueeze(2).broadcast_to([P, 4, 2]), ALU.add)\
                      .then_inc(ada_sb.sem, 1)
                ve.wait_ge(ada_sb.sem, ada_sb.at(l, ADA_CHUNKS))
                for which in range(2):
                    g0 = N_MOD * KD + which * KD
                    s0 = (3 * which + 1) * KD
                    ins = ve.scalar_tensor_tensor(out=gain[:, which, :, :], in0=mod[:, s0:s0 + KD, :], scalar=1.0,
                                                  in1=vecT[:, g0:g0 + KD].unsqueeze(2).broadcast_to([P, KD, 2]),
                                                  op0=ALU.add, op1=ALU.mult)
                ins.then_inc(gain_sb.sem, 1)
                ve.wait_ge(lam_exp.sem, lam_exp.at(l, 1))
                link(ve.scalar_tensor_tensor(out=lamw[:, 2:3], in0=lamw[:, 1:2], scalar=lamw[:, 0:1], in1=lamt[:, 0:1],
                                                op0=ALU.subtract, op1=ALU.subtract))
                ve.tensor_tensor(gsub[:, :], vecT[:, N_VEC - 1:N_VEC], lamt[:, 1:2], ALU.mult).then_inc(lam_done.sem, 1)
                ve.wait_ge(lam_done.sem, lam_done.at(l, 1))
                normalise(l, 0)

                rope_n = [0]

                def lat_copy(u, dst):
                    ve.wait_ge(unit_ps.sem, unit_ps.at(l, u + 1))
                    ve.tensor_copy(dst, lat_bank[u % 2][0:dst.shape[0], :]).then_inc(unit_lat.sem, 1)

                def rope_parts(u, dst, rows, cos, sin):
                    r = rope_n[0]
                    ve.wait_ge(unit_ps.sem, unit_ps.at(l, u + 1))
                    if r >= 2:
                        ve.wait_ge(rope_ps.sem, rope_ps.at(l, r - 1))
                    z = lat_bank[u % 2][rows, :]
                    ve.tensor_tensor(dst, z, cos[rows, :], ALU.mult)
                    ve.tensor_tensor(rope_a[rows, r % 2, :], z, sin[rows, :], ALU.mult).then_inc(unit_lat.sem, 1)
                    rope_n[0] += 1

                def rope_add(r, dst, rows):
                    ve.wait_ge(rope_ps.sem, rope_ps.at(l, r + 1))
                    ve.tensor_tensor(dst, rot_bank[rows, :], dst, ALU.add).then_inc(rope_sb.sem, 1)

                def narrow_scale(n, dst, g_col):
                    ve.wait_ge(nrms_done.sem, nrms_done.at(l, n + 1))
                    for j, blk in enumerate(dst):
                        ins = ve.scalar_tensor_tensor(out=blk, in0=blk, scalar=g_col[:, j:j + 1], in1=rstd[:, :],
                                                      op0=ALU.mult, op1=ALU.mult)
                    ins.then_inc(nscaled.sem, 1)

                lat_copy(0, cqT[:, 0, CTX:TOK])
                lat_copy(1, cqT[:, 1, CTX:TOK])
                lat_copy(2, ckvT[:, CTX:TOK])
                kpe_rows_at = slice(NOPE, QM)
                rope_parts(3, kpeT[NOPE:QM, CTX:TOK], kpe_rows_at, cos_m, sin_m)
                gq = N_VEC - 4
                narrow_scale(0, [cqT[:, 0, :], cqT[:, 1, :]], vecT[:, gq:gq + 2])
                rope_add(0, kpeT[NOPE:QM, CTX:TOK], kpe_rows_at)
                ve.wait_ge(rope_sb.sem, rope_sb.at(l, 1))
                ve.wait_ge(unit_ctx.sem, unit_ctx.at(l, 4))
                ve.wait_ge(tr_sb.sem, tr_sb.at(l, 1))
                for h in range(HEADS):
                    ins = ve.tensor_copy(kT[NOPE:QM, h, :], kpeT[NOPE:QM, :])
                ins.then_inc(kpe_spread.sem, 1)
                narrow_scale(1, [ckvT[:, 0:TOK]], vecT[:, gq + 2:gq + 3])
                q_rows_at = slice(0, QM)
                for h in range(HEADS):
                    rope_parts(4 + h, qT[0:QM, h, CTX:TOK], q_rows_at, cos_m, sin_m)
                    if h >= 1:
                        rope_add(h, qT[0:QM, h - 1, CTX:TOK], q_rows_at)
                lat_copy(8, kT[0:NOPE, 0, 0:512])
                rope_add(4, qT[0:QM, HEADS - 1, CTX:TOK], q_rows_at)
                for h in range(1, HEADS):
                    lat_copy(8 + h, kT[0:NOPE, h, 0:512])

                def attention(first, last):
                    for i in range(first, last + 3):
                        if i < last:
                            kind, h, b = ITS[i]
                            nk = key_cols(b)[1]
                            for g in groups(i):
                                c = slice(g % 2, g % 2 + 1)
                                ve.wait_ge(sc_ps.sem, sc_ps.at(l, g + 1))
                                link(ve.reduce_max(smax[:, c], S[g % 2][:, 0:nk], AX.X))
                                ve.tensor_scalar(negm[:, c], smax[:, c], -(MLA_SCALE if kind == "mla" else DIFF_SCALE), None,
                                                 ALU.mult).then_inc(negm_done.sem, 1)
                        if first <= i - 1 < last:
                            it = i - 1
                            kind, h, b = ITS[it]
                            n = key_cols(b)[1]
                            s = it % 2
                            ve.wait_ge(exp_done.sem, exp_done.at(l, groups(it)[-1] + 1))
                            if kind == "mla":
                                link(ve.reciprocal(srec[:, s, 0:1], ssum[:, s, 0:1]))
                                ve.tensor_scalar(probs[:, s, 0, 0:n], probs[:, s, 0, 0:n], srec[:, s, 0:1], None, ALU.mult)\
                                  .then_inc(probs_done.sem, 1)
                            else:
                                link(ve.reciprocal(srec[:, s, :], ssum[:, s, :]))
                                ve.tensor_scalar(probs[:, s, 0, 0:n], probs[:, s, 0, 0:n], srec[:, s, 0:1], None, ALU.mult)
                                link(ve.tensor_scalar(srec[:, s, 1:2], srec[:, s, 1:2], lamw[:, 2:3], None, ALU.mult))
                                ve.scalar_tensor_tensor(out=probs[:, s, 0, 0:n], in0=probs[:, s, 1, 0:n], scalar=srec[:, s, 1:2],
                                                        in1=probs[:, s, 0, 0:n], op0=ALU.mult, op1=ALU.add)\
                                  .then_inc(probs_done.sem, 1)
                        if i - 3 >= first:
                            it = i - 3
                            kind, h, b = ITS[it]
                            c0 = (it % 2) * 512
                            ve.wait_ge(o_ps.sem, o_ps.at(l, it + 1))
                            if kind == "mla":
                                half = slice((h % 2) * VDIM, (h % 2 + 1) * VDIM)
                                ins = ve.tensor_copy(y_mla[half, h // 2, b * P:(b + 1) * P], U[half, c0:c0 + P])
                            else:
                                ins = ve.tensor_copy(yT[:, 2 + h, b * P:(b + 1) * P], U[:, c0:c0 + P])
                            ins.then_inc(o_sb.sem, 1)

                attention(0, ATT_IT)
                all_rows = slice(0, P)
                for j in range(8):
                    dst = qT if j < 4 else kT
                    rope_parts(12 + j, dst[:, j % 4, CTX:TOK], all_rows, cos_d, sin_d)
                    if j >= 1:
                        prev = qT if j - 1 < 4 else kT
                        rope_add(4 + j, prev[:, (j - 1) % 4, CTX:TOK], all_rows)
                rope_add(12, kT[:, 3, CTX:TOK], all_rows)
                for j in range(2):
                    lat_copy(20 + j, zfT[:, j, CTX:TOK])
                for j in range(2):
                    lat, cx = (U[:, 0:512], S[0][:, 512:512 + CTX]) if j == 0 else (S[0][:, 0:512], ctx_bank[1][:, 0:CTX])
                    ve.wait_ge(fb_ps.sem, fb_ps.at(l, j + 1))
                    ve.tensor_copy(yT[:, j, CTX:TOK], lat)
                    ve.tensor_copy(yT[:, j, 0:CTX], cx).then_inc(fb_sb.sem, 1)
                attention(ATT_IT, 2 * ATT_IT)
                ve.wait_ge(o_sb.sem, o_sb.at(l, 2 * ATT_IT))
                for h in range(HEADS):
                    narrow_scale(2 + h, [yT[:, 2 + h, :]], gsub)

                def residual(n, gate_block):
                    ve.scalar_tensor_tensor(out=xT[:, n, CTX:TOK], in0=lat_bank[n % 2], scalar=mod[:, gate_block + n, 1:2],
                                            in1=xT[:, n, CTX:TOK], op0=ALU.mult, op1=ALU.add)
                    return ve.scalar_tensor_tensor(out=xT[:, n, 0:CTX], in0=ctx_bank[n % 2][:, 0:CTX],
                                                   scalar=mod[:, gate_block + n, 0:1], in1=xT[:, n, 0:CTX],
                                                   op0=ALU.mult, op1=ALU.add)

                for n in range(KD):
                    ve.wait_ge(mix_ps.sem, mix_ps.at(l, n + 1))
                    residual(n, 2 * KD).then_inc(mix_sb.sem, 1)

                ve.wait_ge(mix_sb.sem, mix_sb.at(l, KD))
                normalise(l, 1)
                ve.wait_ge(lg_ps.sem, lg_ps.at(l, 1))
                logits = T[:, 0:NB * E_N].rearrange("p (b e) -> p b e", b=NB)
                link(ve.reduce_max(lmax[:, :], logits, AX.X))
                ve.tensor_tensor(lg[:, :, :], logits, lmax[:, :].unsqueeze(2).broadcast_to([P, NB, E_N]), ALU.subtract)\
                  .then_inc(lg_shift.sem, 1)
                ve.wait_ge(outs_done.sem, outs_done.at(l + 1, 0))
                ve.wait_ge(lg_exp.sem, lg_exp.at(l, 1))
                link(ve.reduce_sum(lmax[:, :], lg[:, :, :], AX.X))
                link(ve.reciprocal(lmax[:, :], lmax[:, :]))
                ve.tensor_tensor(lg[:, :, :], lg[:, :, :], lmax[:, :].unsqueeze(2).broadcast_to([P, NB, E_N]), ALU.mult)\
                  .then_inc(aff_rows.sem, 1)
                def rows_of_h(b):
                    ve.wait_ge(hr_ps.sem, hr_ps.at(l, b + 1))
                    ve.tensor_copy(h_rows[:, b, 0:512], S[b % 2][:, 0:512]).then_inc(hr_v.sem, 1)

                for b in range(NB - 1):
                    rows_of_h(b)
                ve.wait_ge(aff_ps.sem, aff_ps.at(l, 1))
                ve.tensor_copy(aff[0:E_N, 0:CTX], U[0:E_N, 512:512 + CTX])
                link(ve.tensor_copy(aff[0:E_N, CTX:TOK], U[0:E_N, 0:LAT]))
                link(ve.tensor_copy(work[0:E_N, :], aff[0:E_N, :]))
                for cols, cap in ((slice(0, CTX), CAPX), (slice(CTX, TOK), CAP)):
                    for _ in range(cap // 8):
                        link(ve.max(top8[:, :], work[0:E_N, cols]))
                        link(ve.match_replace(work[0:E_N, cols], top8[:, :], work[0:E_N, cols], -1.0))
                link(ve.tensor_scalar(mask[0:E_N, :], work[0:E_N, :], 0.0, None, ALU.is_lt))
                for cols in (slice(0, CTX), slice(CTX, TOK)):
                    link(ve.tensor_tensor_scan(pos[0:E_N, cols], mask[0:E_N, cols], mask[0:E_N, cols], 0.0, ALU.add, ALU.max))
                link(ve.tensor_tensor(pos[0:E_N, :], pos[0:E_N, :], mask[0:E_N, :], ALU.mult))
                ve.tensor_scalar(pos[0:E_N, :], pos[0:E_N, :], -1.0, None, ALU.add).then_inc(pos_done.sem, 1)
                rows_of_h(NB - 1)
                ve.wait_ge(pr_ps.sem, pr_ps.at(l, 1))
                ve.tensor_copy(pos_rows[:, :, :], T[:, 0:NB * E_N].rearrange("p (b e) -> p b e", b=NB)).then_inc(pr_sb.sem, 1)

                with ve.Fori(0, PAIRS) as pair:
                    t = l * PAIRS + pair
                    ve.wait_ge(pr_sb.sem, pr_sb.at(l, 1))
                    ve.tensor_copy(cur[:, :, :], pos_rows[:, :, bass.ds(pair * 2, 2)]).then_inc(step_vp.sem, 1)
                    ve.tensor_copy(selx[:, :, :], ident[0:E_N, bass.ds(pair * 2, 2)].unsqueeze(2).broadcast_to([E_N, 2, CAPX]))
                    ve.tensor_copy(sel[:, :, :], ident[0:E_N, bass.ds(pair * 2, 2)].unsqueeze(2).broadcast_to([E_N, 2, CAP]))\
                      .then_inc(sel_done.sem, 1)
                    ve.wait_ge(step_vp.sem, step_vp.at(t, 1))
                    for i in range(2):
                        ve.tensor_tensor(pick[:, i, 0:4 * CAP].rearrange("p (b c) -> p b c", b=4),
                                         iota.unsqueeze(1).broadcast_to([P, 4, CAP]),
                                         cur[:, 1:NB, i].unsqueeze(2).broadcast_to([P, 4, CAP]), ALU.is_equal)
                        ve.tensor_tensor(pick[:, i, 4 * CAP:4 * CAP + CAPX], iota[:, 0:CAPX],
                                         cur[:, 0, i:i + 1].broadcast_to([P, CAPX]), ALU.is_equal).then_inc(pick_done.sem, 1)
                    for i in range(2):
                        ve.wait_ge(xs_ps.sem, xs_ps.at(t, i + 1))
                        ve.tensor_copy(xs[:, i, 0:4, :].rearrange("p k c -> p (k c)"), S[0][:, 0:4 * SLOT_TOK]).then_inc(xs_v.sem, 1)
                        for half in range(2):
                            ve.wait_ge(silu_done.sem, silu_done.at(t, 2 * i + half + 1))
                            ve.wait_ge(gu_ps.sem, gu_ps.at(t, 4 * i + 2 * half + 2))
                            ve.tensor_tensor(hm[:, i, 4 * half:4 * half + 4, :].rearrange("p k c -> p (k c)"),
                                             (S[1], T)[half][:, 512:512 + 4 * SLOT_TOK], scr[:, half, 0:4 * SLOT_TOK], ALU.mult)\
                              .then_inc(hm_done.sem, 1)
                        for half in range(2):
                            ve.wait_ge(ye_ps.sem, ye_ps.at(t, 2 * i + half + 1))
                            out = U[:, half * 512:half * 512 + 4 * SLOT_TOK].rearrange("p (m c) -> p m c", m=4)
                            ve.tensor_copy(ye[:, 4 * half:4 * half + 4, i * CAP:(i + 1) * CAP], out[:, :, 0:CAP])
                            ve.tensor_copy(yex[:, 4 * half:4 * half + 4, i * CAPX:(i + 1) * CAPX], out[:, :, CAP:SLOT_TOK])\
                              .then_inc(ye_sb.sem, 1)
                    ve.wait_ge(gate_sb.sem, gate_sb.at(t, 1))
                    ve.scalar_tensor_tensor(out=back[:, :], in0=T[:, 0:LAT], scalar=consts[:, K_SLOT:K_SLOT + 1],
                                            in1=rope_a[:, 0, :], op0=ALU.is_equal, op1=ALU.mult)
                    ve.scalar_tensor_tensor(out=backx[0:2 * CAPX, :], in0=S[1][0:2 * CAPX, 0:CTX],
                                            scalar=consts[0:2 * CAPX, K_SLOTX:K_SLOTX + 1],
                                            in1=rope_a[0:2 * CAPX, 1, 0:CTX], op0=ALU.is_equal, op1=ALU.mult)\
                      .then_inc(back_done.sem, 1)
                    ve.wait_ge(yr_ps.sem, yr_ps.at(t, 1))
                    ve.tensor_copy(ye_rows[:, 0:512], S[0][:, 0:512]).then_inc(yr_v.sem, 1)
                    ve.wait_ge(yr_ps.sem, yr_ps.at(t, 2))
                    ve.tensor_copy(yex_rows[0:2 * CAPX, 0:512], U[0:2 * CAPX, 0:512]).then_inc(yr_v.sem, 1)
                    for n in range(KD):
                        ve.wait_ge(add_ps.sem, add_ps.at(t, n + 1))
                        residual(n, 5 * KD).then_inc(add_sb.sem, 1)
                    ve.wait_ge(add_sb.sem, add_sb.at(t, KD))

            ve.wait_ge(rms_done.sem, rms_done.at(DEPTH, 1))
            for k in range(KD):
                ve.scalar_tensor_tensor(out=hT[:, k, :], in0=xT[:, k, :], scalar=condT[:, 2 * KD + k:2 * KD + k + 1],
                                        in1=rstd[:, :], op0=ALU.mult, op1=ALU.mult).then_inc(xn_done.sem, 1)
            for b in range(NB):
                ve.wait_ge(fin_ps.sem, b + 1)
                ve.tensor_copy(arena[:, b * D:b * D + 512], S[b % 2][:, 0:512]).then_inc(fin_v.sem, 1)


_INS = ["x_prompt", "x_sample", "cache_diff_k", "cache_diff_v", "cache_mla_ckv", "cache_mla_kpe", "c", "c_ctx", "w_ada",
        "b_ada", "g_attn", "g_ffn", "w_in", "w_four", "diff_lambda", "g_subln", "g_mla_q", "w_mla_uq", "g_mla_kv",
        "w_mla_ukv", "w_out", "w_router", "w_e_gate", "w_e_up", "w_e_down", "g_final"]
_OUTS = [("y_prompt", (1, CTX, D)), ("y_sample", (1, LAT, D)), ("new_diff_k", (1, DEPTH, CTX, HEADS, 2 * DH)),
         ("new_diff_v", (1, DEPTH, CTX, HEADS, 2 * DH)), ("new_mla_ckv", (1, DEPTH, CTX, P)),
         ("new_mla_kpe", (1, DEPTH, CTX, ROPE))]


def _rope_tables(dim):
    rows = LAT // GRID_W
    row = np.repeat(np.arange(rows, dtype=np.float32), GRID_W)
    col = np.tile(np.arange(GRID_W, dtype=np.float32), rows)
    nf = dim // 4
    inv = (np.float32(ROPE_BASE) ** (-np.arange(nf, dtype=np.float32) / np.float32(nf))).astype(np.float32)
    ang = np.concatenate([row[:, None] * inv, col[:, None] * inv], axis=-1)
    return np.cos(ang).astype(np.float32).T, np.sin(ang).astype(np.float32).T


def _constants():
    c = np.zeros((P, K_W), np.float32)
    c[:, K_ID:K_ID + P] = np.eye(P)
    def rot(m, at, half):
        for i in range(half):
            m[at + half + i, at + i] = -1.0
            m[at + i, at + half + i] = 1.0
    rot(c[:, K_ROTD:K_ROTD + P], 0, DH // 2)
    rot(c[:, K_ROTD:K_ROTD + P], DH, DH // 2)
    rot(c[:, K_ROTM:K_ROTM + QM], NOPE, ROPE // 2)
    cos, sin = _rope_tables(DH)
    c[:, K_ROPED:K_ROPED + LAT] = np.tile(cos, (4, 1))
    c[:, K_ROPED + LAT:K_ROPED + 2 * LAT] = np.tile(sin, (4, 1))
    cos, sin = _rope_tables(ROPE)
    c[0:NOPE, K_ROPEM:K_ROPEM + LAT] = 1.0
    c[NOPE:QM, K_ROPEM:K_ROPEM + LAT] = np.tile(cos, (2, 1))
    c[NOPE:QM, K_ROPEM + LAT:K_ROPEM + 2 * LAT] = np.tile(sin, (2, 1))

    def dft(n):
        turn = 2.0 * np.pi * (np.outer(np.arange(n), np.arange(n)) % n) / n
        return np.cos(turn) / np.sqrt(n), np.sin(turn) / np.sqrt(n)

    for part, m in enumerate(dft(F_CH)):
        for j in range(2):
            c[j * F_CH:(j + 1) * F_CH, K_CHAN + part * P + j * F_CH:K_CHAN + part * P + (j + 1) * F_CH] = m
    co, si = dft(CTX)
    c[:, K_SEQX:K_SEQX + CTX], c[:, K_SEQX + CTX:K_SEQX + 2 * CTX] = co, -si
    c[:, K_IOTA:K_IOTA + CAP] = np.arange(CAP)
    c[:, K_SLOT] = np.arange(P) % CAP
    c[:, K_SLOTX] = np.arange(P) % CAPX
    c[:, K_EPS] = EPS
    co, si = dft(LAT)
    seq = np.concatenate([co, -si]).astype(np.float32)
    init = 0.8 - 0.6 * np.exp(-0.3 * np.arange(DEPTH))
    lam = np.stack([init, 1.0 - init], axis=1).astype(np.float32)
    return c, seq, lam


def kernel(**inputs):
    import concourse.bacc as bacc
    from concourse.bass_utils import run_bass_kernel_spmd

    nc = bacc.Bacc("TRN2", target_bir_lowering=False, num_devices=1)
    arrays, aps = {}, {}
    consts, seq, lam = _constants()
    given = [(n, inputs[n]) for n in _INS] + [("consts", consts), ("dft", seq), ("lam_init", lam)]
    for name, value in given:
        v = np.ascontiguousarray(value)
        arrays[f"in_{name}_dram"] = v
        aps[name] = nc.dram_tensor(f"in_{name}_dram", v.shape, mybir.dt.from_np(v.dtype), kind="ExternalInput").ap()
    for name, shape in _OUTS:
        aps[name] = nc.dram_tensor(f"out_{name}_dram", shape, F32, kind="ExternalOutput").ap()
    build(nc, aps)
    r = run_bass_kernel_spmd(nc, [arrays], core_ids=[0])
    return tuple(r.results[0][f"out_{name}_dram"] for name, _ in _OUTS)
```

```python
from contextlib import ExitStack

import numpy as np

import concourse.bass as bass
from concourse import mybir

F32 = mybir.dt.float32
F32R = mybir.dt.float32r
ALU = mybir.AluOpType
ACT = mybir.ActivationFunctionType
AX = mybir.AxisListType

P = 128
D = 1024
KD = D // P
DEPTH = 2
CTX, LAT, PAST = 128, 512, 128
TOK = CTX + LAT
NB = TOK // P
KEYS = LAT + PAST
GRID_W = 64
ROPE_BASE = 10000.0
EPS = 1e-6
HEADS = 4
DH = 64
NOPE, ROPE, VDIM = 64, 32, 64
QM = NOPE + ROPE
F_CH = 64
E_N = 16
PAIRS = E_N // 2
CAP = 2 * LAT // E_N
CAPX = 2 * CTX // E_N
SLOT_TOK = CAP + CAPX
N_MOD = 6
N_VEC = N_MOD * KD + 2 * KD + 2 + 1 + 1
DIFF_SCALE = float(DH) ** -0.5
MLA_SCALE = float(QM) ** -0.5

C_F, C_Q, C_K, C_V, C_CQ, C_CKV, C_KPE, C_END = 0, 256, 768, 1280, 1792, 2048, 2176, 2208

RING = 4
ADA_CHUNKS = 12
CH_MLA, CH_Q, CH_K, CH_V, CH_F, CH_DFT, CH_OUT = 12, 13, 14, 15, 16, 17, 18
DENSE_CHUNKS = 20
PAIR_CHUNKS = 12
LAYER_CHUNKS = DENSE_CHUNKS + PAIRS * PAIR_CHUNKS
assert LAYER_CHUNKS % RING == 0 and DENSE_CHUNKS % RING == 0 and PAIR_CHUNKS % RING == 0

K_ID, K_ROTD, K_ROTM = 0, 128, 256
K_ROPED = K_ROTM + QM
K_ROPEM = K_ROPED + 2 * LAT
K_CHAN = K_ROPEM + 2 * LAT
K_SEQX = K_CHAN + 2 * P
K_IOTA = K_SEQX + 2 * CTX
K_SLOT = K_IOTA + CAP
K_SLOTX = K_SLOT + 1
K_EPS = K_SLOTX + 1
K_FOLD = K_EPS + 1
K_W = K_FOLD + 2

GATE, UP, DOWN = range(3)
GROUPS_OF_PAIR = [(0, GATE, 0), (0, UP, 0), (0, GATE, 1), (0, UP, 1), (1, GATE, 0), (1, UP, 0), (1, GATE, 1), (1, UP, 1),
                  (0, DOWN, 0), (0, DOWN, 1), (1, DOWN, 0), (1, DOWN, 1)]
PIECES = 4
YE_AT = 5664
SPLIT_AT = 10144
ARENA = SPLIT_AT + 4 * KD * 2 * SLOT_TOK
XROW = 32

UNITS = 22
ROPES = 13
ATT_IT = HEADS * NB
GROUPS = 3 * ATT_IT
VECS, SMALL = 6, 13
OUTS = 4


class Signal:

    def __init__(self, sem, per, setup=0, step=1):
        self.sem, self.per, self.setup, self.step = sem, per, setup, step

    def at(self, turn, k):
        return turn * (self.per * self.step) + (self.setup + k) * self.step


def build(nc, a):
    ctx = ExitStack()
    with ctx:
        def sb(name, shape):
            return ctx.enter_context(nc.sbuf_tensor(name, shape, F32))

        def signal(name, per, setup=0, step=1):
            return Signal(ctx.enter_context(nc.semaphore(name)), per, setup, step)

        def reused(first, *later):
            for name, shape, dt in (first, *later):
                with nc.sbuf_tensor(name, shape, dt) as t:
                    yield t

        xT = sb("xT", [P, KD, TOK])
        consts = sb("consts", [P, K_W])
        ones = sb("ones", [P, P])
        scr = sb("scr", [P, 2, TOK])
        rstd, back = reused(("rstd", [P, TOK], F32), ("back", [P, LAT], F32R))
        ctx.enter_context(nc.sbuf_tensor("rstd_place", [P, TOK], F32))
        rope_a = sb("rope_a", [P, 2, LAT])
        vec_rows = sb("vec_rows", [N_VEC, P])
        vecT = sb("vecT", [P, N_VEC])
        mod = sb("mod", [P, N_MOD * KD, 2])
        gain = sb("gain", [P, 2, KD, 2])
        condT = sb("condT", [P, 3 * KD])
        condP = sb("condP", [P, KD, 32])
        wuq = sb("wuq", [P, 2, HEADS * QM])
        wukv = sb("wukv", [P, HEADS * (NOPE + VDIM)])
        wfour = sb("wfour", [P, 2, P])
        wrt = sb("wrt", [P, KD, E_N])
        dlam = sb("dlam", [P, 4, DH])
        lamt = sb("lamt", [P, 2])
        lamw = sb("lamw", [P, 4])
        gsub = sb("gsub", [P, 1])
        cache_k = sb("cache_k", [P, HEADS * P])
        cache_v = sb("cache_v", [P, HEADS * P])
        cache_ckv = sb("cache_ckv", [P, P])
        cache_kpe = sb("cache_kpe", [P, QM])
        chanw = sb("chanw", [P, 2, 2, P])
        k_rows = sb("k_rows", [P, HEADS * P])
        smax = sb("smax", [P, 2])
        negm = sb("negm", [P, 2])
        ssum = sb("ssum", [P, 2, 2])
        srec = sb("srec", [P, 2, 2])
        lg = sb("lg", [P, NB, E_N])
        lmax = sb("lmax", [P, NB])
        top8 = sb("top8", [E_N, 8])
        pos_rows = sb("pos_rows", [P, NB, E_N + 2])
        cur = sb("cur", [P, NB, 2])
        cur_gate = sb("cur_gate", [P, NB, 2])
        gates = sb("gates", [SLOT_TOK, 2])

        ring, ring_lo = reused(("ring", [P, RING, KD, 512], F32), ("ring_lo", [P, RING, KD, 512], F32R))
        ctx.enter_context(nc.sbuf_tensor("ring_place", [P, RING, KD, 512], F32))
        hT, w_hi = reused(("hT", [P, KD, TOK], F32), ("w_hi", [P, PIECES, 2, 512], F32R))
        ctx.enter_context(nc.sbuf_tensor("hT_place", [P, KD, TOK], F32))
        with nc.sbuf_tensor("arena", [P, ARENA], F32) as arena:
            pass
        ctx.enter_context(nc.sbuf_tensor("arena_front", [P, YE_AT], F32))
        ye_hi, yex, ye_lo = (ctx.enter_context(nc.sbuf_tensor(n, [P, D], F32R)) for n in ("ye_hi", "yex", "ye_lo"))
        backx = ctx.enter_context(nc.sbuf_tensor("backx", [P, CTX], F32R))
        ctx.enter_context(nc.sbuf_tensor("arena_middle", [P, SPLIT_AT - YE_AT - 3 * D - CTX], F32))
        xs_hi, xs_lo = (ctx.enter_context(nc.sbuf_tensor(n, [P, KD, 2, SLOT_TOK], F32R)) for n in ("xs_hi", "xs_lo"))
        hm_hi, hm_lo = (ctx.enter_context(nc.sbuf_tensor(n, [P, 2, KD, SLOT_TOK], F32R)) for n in ("hm_hi", "hm_lo"))

        def region(at, *dims):
            n = int(np.prod(dims))
            v = arena[:, at:at + n]
            if len(dims) == 2:
                v = v.rearrange("p (a b) -> p a b", a=dims[0])
            if len(dims) == 3:
                v = v.rearrange("p (a b c) -> p a b c", a=dims[0], b=dims[1])
            return v

        qT = region(0, HEADS, TOK)
        kT = region(2560, HEADS, CTX + KEYS)
        v_rows = region(5632, NB, HEADS * P)
        vm_rows = region(5632, NB + 1, HEADS * VDIM)
        ckvT = region(8192, CTX + KEYS)
        kpeT = region(8960, CTX + KEYS)
        y_mla = region(9728, 2, TOK)
        probs = region(11008, 2, 2, TOK)
        cqT = region(11008, 2, TOK)
        chan_rows = region(11008, NB, 2, 2 * P)
        probsT = region(13568, 2, NB, P)
        zfT = region(13568, 2, TOK)
        ckv_rows = region(14848, P)
        kpe_rows = region(14976, ROPE)
        dprod = region(15008, 2, DH)
        yT = hT
        h_rows = region(0, NB, D)
        pick = region(5120, 4, 2 * CAP)
        pickx = region(5632, 2 * CAPX)
        slot_rows = hT[:, :, :].rearrange("p a b -> p (a b)")[:, 2 * PIECES * 512:2 * PIECES * 512 + D]
        slotx_rows = [chanw[:, :, :, :].rearrange("p a b c -> p (a b c)"), k_rows[:, :]]
        hm_rows = [scr[:, :, :].rearrange("p a b -> p (a b)")[:, 0:D], rope_a[:, :, :].rearrange("p a b -> p (a b)")]
        aff = region(8864, TOK)
        scr_end = scr[:, :, :].rearrange("p a b -> p (a b)")[0:E_N, D:D + 256]
        sel = scr_end[:, 0:2 * CAP].rearrange("e (i c) -> e i c", i=2)
        selx = scr_end[:, 2 * CAP:2 * CAP + 4 * XROW].rearrange("e (a i c) -> e a i c", a=2, i=2)
        pos = region(9504, TOK)[0:E_N, :]
        work = region(7840, TOK)
        mask = region(5792, TOK)
        cond_rows = region(0, P)[0:3 * KD, :]
        cond_e = region(P, P)[0:2 * KD, :]
        x_rows = hT[:, :, :].rearrange("p a b -> p (a b)").rearrange("p (b d) -> p b d", b=NB)

        ident = consts[:, K_ID:K_ID + P]
        rot_diff = consts[:, K_ROTD:K_ROTD + P]
        rot_mla = consts[:, K_ROTM:K_ROTM + QM]
        cos_d, sin_d = consts[:, K_ROPED:K_ROPED + LAT], consts[:, K_ROPED + LAT:K_ROPED + 2 * LAT]
        cos_m, sin_m = consts[:, K_ROPEM:K_ROPEM + LAT], consts[:, K_ROPEM + LAT:K_ROPEM + 2 * LAT]
        iota = consts[:, K_IOTA:K_IOTA + CAP]
        eps = consts[:, K_EPS:K_EPS + 1]

        S = [ctx.enter_context(nc.psum_tensor(f"S{i}", [P, 1024], F32)) for i in range(2)]
        T = ctx.enter_context(nc.psum_tensor("T", [P, 1024], F32))
        U = ctx.enter_context(nc.psum_tensor("U", [P, 1024], F32))
        lat_bank = [T[:, 0:512], T[:, 512:1024]]
        ctx_bank = [U[:, 0:512], U[:, 512:1024]]
        sum_lat, sum_ctx = S[0][:, 0:512], S[0][:, 512:512 + CTX]
        rot_bank = S[1][:, 0:512]
        misc_bank = S[1][:, 512:1024]

        const_in = signal("const_in", 0, 4, 16)
        x_in = signal("x_in", 0, 2, 16)
        fill_done = signal("fill_done", 0, 5)
        xt_ps, xt_sb = signal("xt_ps", 0, KD), signal("xt_sb", 0, KD)
        cond_exp, cond_silu = signal("cond_exp", 0, 1), signal("cond_silu", 0, 1)
        cond_ps, cond_sb = signal("cond_ps", 0, 1), signal("cond_sb", 0, 1)
        slot_in = [signal(f"slot_in{i}", LAYER_CHUNKS // RING, 0, 16) for i in range(RING)]
        vec_in, small_in = signal("vec_in", VECS, 0, 16), signal("small_in", SMALL, 0, 16)
        vec_ps, vec_sb = signal("vec_ps", 1), signal("vec_sb", 1)
        adar_ps, adar_sb = signal("adar_ps", ADA_CHUNKS), signal("adar_sb", ADA_CHUNKS)
        ada_ps, ada_sb = signal("ada_ps", ADA_CHUNKS), signal("ada_sb", ADA_CHUNKS)
        gain_sb = signal("gain_sb", 1)
        sq_done, sq_used = signal("sq_done", 2 * KD), signal("sq_used", 2 * KD)
        rms_done = signal("rms_done", 2)
        xn_done, h_done = signal("xn_done", 2 * KD), signal("h_done", 2 * KD)
        unit_ps = signal("unit_ps", UNITS)
        unit_lat, unit_ctx = signal("unit_lat", UNITS), signal("unit_ctx", UNITS)
        rope_ps, rope_sb = signal("rope_ps", ROPES), signal("rope_sb", ROPES)
        nsq_done, nsum_ps = signal("nsq_done", 7), signal("nsum_ps", 6)
        nrms_done, nscaled = signal("nrms_done", 6), signal("nscaled", 6)
        tr_ps, tr_sb = signal("tr_ps", 4), signal("tr_sb", 4)
        kpe_spread = signal("kpe_spread", 1)
        vm_ps, vm_sb = signal("vm_ps", NB + 1), signal("vm_sb", NB + 1)
        v_ps, v_sb = signal("v_ps", NB), signal("v_sb", NB)
        sc_ps, negm_done, exp_done = signal("sc_ps", GROUPS), signal("negm_done", GROUPS), signal("exp_done", GROUPS)
        probs_done = signal("probs_done", 2 * ATT_IT)
        pt_ps, pt_sb = signal("pt_ps", 2 * ATT_IT), signal("pt_sb", 2 * ATT_IT)
        o_ps, o_sb = signal("o_ps", 2 * ATT_IT), signal("o_sb", 2 * ATT_IT)
        lam_prod, lam_exp, lam_done = signal("lam_prod", 1), signal("lam_exp", 1), signal("lam_done", 1)
        cw_ps, cw_sb = signal("cw_ps", 2), signal("cw_sb", 2)
        fa_ps, fa_sb = signal("fa_ps", NB), signal("fa_sb", NB)
        fb_ps, fb_sb = signal("fb_ps", 2), signal("fb_sb", 2)
        mix_ps, mix_sb = signal("mix_ps", KD), signal("mix_sb", KD)
        outs_done = signal("outs_done", OUTS, 0, 16)
        lg_ps, lg_shift, lg_exp, aff_rows = (signal(n, 1) for n in ("lg_ps", "lg_shift", "lg_exp", "aff_rows"))
        aff_ps, pos_done, pr_ps = (signal(n, 1) for n in ("aff_ps", "pos_done", "pr_ps"))
        pr_sb = signal("pr_sb", 1, 1)
        hr_ps, hr_v, hr_a = signal("hr_ps", NB), signal("hr_v", NB), signal("hr_a", NB)
        pick_done, lg_rows, xg_rows = (signal(n, 1) for n in ("pick_done", "lat_rows_sb", "ctx_rows_sb"))
        gl_ps, gx_ps, tl_ps, tx_ps = (signal(n, 1) for n in ("gl_ps", "gx_ps", "tl_ps", "tx_ps"))
        xl_hi, xl_lo, xx_hi, xx_lo = (signal(n, 1) for n in ("xl_hi", "xl_lo", "xx_hi", "xx_lo"))
        gate_cols, gate_ps, gate_sb = (signal(n, 1) for n in ("gate_cols", "gate_ps", "gate_sb"))
        sel_done, place_ps = (signal(n, 1) for n in ("sel_done", "place_ps"))
        back_done = signal("back_done", 1, 1)
        hi_done, lo_done = (signal(n, 12 * PIECES) for n in ("hi_done", "lo_done"))
        piece_ps = signal("piece_ps", 12 * (PIECES - 1), PIECES - 1)
        gr_ps = signal("gr_ps", 12, RING)
        silu_done, hm_done = signal("silu_done", 4), signal("hm_done", 4)
        th_ps, hh_done, hl_done = signal("th_ps", 2), signal("hh_done", 2), signal("hl_done", 2)
        t_clear = signal("t_clear", 1)
        ye0_hi, ye0_lo = signal("ye0_hi", 2), signal("ye0_lo", 2)
        ye1_hi, rows_done = signal("ye1_hi", 2), signal("rows_done", 1)
        add_ps, add_sb = signal("add_ps", KD), signal("add_sb", KD, 1)
        fin_ps, fin_v, fin_a = signal("fin_ps", NB), signal("fin_v", NB), signal("fin_a", NB)
        y_out = signal("y_out", 2, 0, 16)
        step_v = ctx.enter_context(nc.semaphore("step_v"))
        step_a = signal("step_a", 8, 0)

        block = ctx.enter_context(nc.Block())

        @block.sync
        def _(sp):
            sp.dma_start(consts[:, :], a["consts"]).then_inc(const_in.sem, 16)
            sp.dma_start(cond_rows[0:KD, :], a["c_ctx"].rearrange("(k p) -> k p", p=P)).then_inc(const_in.sem, 16)
            sp.dma_start(cond_rows[KD:2 * KD, :], a["c"].rearrange("b (k p) -> (b k) p", p=P)).then_inc(const_in.sem, 16)
            sp.dma_start(cond_rows[2 * KD:3 * KD, :], a["g_final"].rearrange("(k p) -> k p", p=P)).then_inc(const_in.sem, 16)
            sp.dma_start(x_rows[:, 0, :], a["x_prompt"].rearrange("b n d -> (b n) d")).then_inc(x_in.sem, 16)
            sp.dma_start(x_rows[:, 1:NB, :], a["x_sample"].rearrange("b (j p) d -> p (b j) d", p=P)).then_inc(x_in.sem, 16)

            sp.wait_ge(fill_done.sem, 5)
            with sp.Fori(0, DEPTH) as l:
                def vec(dst, src):
                    sp.dma_start(dst, src).then_inc(vec_in.sem, 16)

                def small(dst, src):
                    sp.dma_start(dst, src).then_inc(small_in.sem, 16)

                sp.wait_ge(pr_sb.sem, pr_sb.at(l, 0))
                r = N_MOD * KD
                vec(vec_rows[0:r, :], a["b_ada"][l].rearrange("(k p) -> k p", p=P))
                vec(vec_rows[r:r + KD, :], a["g_attn"][l].rearrange("(k p) -> k p", p=P))
                vec(vec_rows[r + KD:r + 2 * KD, :], a["g_ffn"][l].rearrange("(k p) -> k p", p=P))
                r += 2 * KD
                vec(vec_rows[r:r + 2, :], a["g_mla_q"][l].rearrange("(k p) -> k p", p=P))
                vec(vec_rows[r + 2:r + 3, :], a["g_mla_kv"][l].rearrange("(k p) -> k p", p=P))
                vec(vec_rows[r + 3:r + 4, :], a["g_subln"][l].rearrange("(k p) -> k p", p=P))

                def load(i, src, last_read):
                    if last_read:
                        done, value = last_read
                        sp.wait_ge(done.sem, value)
                    rows = src.rearrange("(k p) n -> p k n", p=P)
                    n = rows.shape[2]
                    sp.dma_start(ring[:, i % RING, :, 0:n], rows).then_inc(slot_in[i % RING].sem, 16)

                def dense_read(c):
                    if c < ADA_CHUNKS:
                        return adar_ps, adar_ps.at(l, c + 1)
                    return {CH_MLA: (unit_ps, unit_ps.at(l, 4)), CH_Q: (unit_ps, unit_ps.at(l, 16)),
                            CH_K: (unit_ps, unit_ps.at(l, 20)), CH_V: (v_ps, v_ps.at(l, NB)),
                            CH_F: (unit_ps, unit_ps.at(l, UNITS)), CH_DFT: (fb_ps, fb_ps.at(l, 2)),
                            CH_OUT: (mix_ps, mix_ps.at(l, 4)), CH_OUT + 1: (mix_ps, mix_ps.at(l, KD))}[c]

                def pair_read(t, j):
                    return gr_ps, gr_ps.at(t, j + 1)

                def dense(c, src):
                    load(c, src, dense_read(c - RING) if c >= RING else pair_read(l * PAIRS, c - RING))

                def small_weights():
                    small(dlam[:, :, :], a["diff_lambda"][l].partition_broadcast(P))
                    small(lamt[:, :], a["lam_init"][l].partition_broadcast(P))
                    small(wuq[:, :, :], a["w_mla_uq"][l].rearrange("(k p) n -> p k n", p=P))
                    small(wukv[:, :], a["w_mla_ukv"][l])
                    small(cache_ckv[:, :], a["cache_mla_ckv"][0, l])
                    small(cache_kpe[:, NOPE:QM], a["cache_mla_kpe"][0, l])
                    small(cache_k[:, :], a["cache_diff_k"][0, l].rearrange("t h d -> t (h d)"))
                    small(cache_v[:, :], a["cache_diff_v"][0, l].rearrange("t h d -> t (h d)"))
                    for j in range(4):
                        half = (j % 2) * F_CH
                        small(wfour[half:half + F_CH, j // 2, half:half + F_CH], a["w_four"][l, j])
                    small(wrt[:, :, :], a["w_router"][l].rearrange("(k p) e -> p k e", p=P))

                for c in range(ADA_CHUNKS):
                    dense(c, a["w_ada"][l, :, c * 512:(c + 1) * 512])
                    if c == RING - 1:
                        small_weights()
                dense(CH_MLA, a["w_in"][l, :, C_CQ:C_END])
                dense(CH_Q, a["w_in"][l, :, C_Q:C_K])
                dense(CH_K, a["w_in"][l, :, C_K:C_V])
                load(CH_V, a["w_in"][l, :, C_V:C_CQ], dense_read(CH_MLA))
                load(CH_F, a["w_in"][l, :, C_F:C_Q], None)
                dense(CH_DFT, a["dft"])
                for c in range(2):
                    dense(CH_OUT + c, a["w_out"][l, :, c * 512:(c + 1) * 512])
                def expert_piece(pair, j):
                    later, j = divmod(j, PAIR_CHUNKS)
                    i, matrix, half = GROUPS_OF_PAIR[j]
                    name = ("w_e_gate", "w_e_up", "w_e_down")[matrix]
                    return a[name][l, pair * 2 + (2 * later + i), :, half * 512:(half + 1) * 512]

                for j in range(RING):
                    load(j, expert_piece(0, j), dense_read(DENSE_CHUNKS + j - RING))
                with sp.Fori(0, PAIRS - 1) as pair:
                    for j in range(RING, RING + PAIR_CHUNKS):
                        load(j, expert_piece(pair, j), pair_read(l * PAIRS + pair, j - RING))
                for j in range(RING, PAIR_CHUNKS):
                    load(j, expert_piece(PAIRS - 1, j), pair_read(l * PAIRS + PAIRS - 1, j - RING))

            sp.wait_ge(fin_v.sem, NB)
            sp.wait_ge(fin_a.sem, NB)
            out_rows = arena[:, 0:NB * D].rearrange("p (b d) -> p b d", b=NB)
            sp.dma_start(a["y_prompt"].rearrange("b n d -> (b n) d"), out_rows[:, 0, :]).then_inc(y_out.sem, 16)
            sp.dma_start(a["y_sample"].rearrange("b (j p) d -> p (b j) d", p=P), out_rows[:, 1:NB, :]).then_inc(y_out.sem, 16)
            sp.wait_ge(y_out.sem, y_out.at(1, 0))

        @block.gpsimd
        def _(g):
            g.memset(ones[:, :], 1.0).then_inc(fill_done.sem, 1)
            g.memset(wfour[:, :, :], 0.0).then_inc(fill_done.sem, 1)
            g.memset(cache_kpe[:, :], 0.0).then_inc(fill_done.sem, 1)
            g.memset(condP[:, :, :], 0.0).then_inc(fill_done.sem, 1)
            g.memset(pos_rows[:, :, E_N:E_N + 2], -1.0).then_inc(fill_done.sem, 1)


        def iterations(kind):
            return [(kind, h, b) for h in range(HEADS) for b in range(NB)]

        ITS = iterations("mla") + iterations("diff")

        def groups(it):
            if it < ATT_IT:
                return [it]
            return [ATT_IT + 2 * (it - ATT_IT), ATT_IT + 2 * (it - ATT_IT) + 1]

        def key_cols(b):
            return (0, CTX) if b == 0 else (CTX, KEYS)

        @block.tensor
        def _(pe):
            pe.wait_ge(const_in.sem, const_in.at(0, 0))
            pe.wait_ge(fill_done.sem, 5)
            pe.wait_ge(x_in.sem, x_in.at(0, 0))
            pe.sem_inc(gr_ps.sem, RING)
            pe.sem_inc(piece_ps.sem, PIECES - 1)
            for k in range(KD):
                if k >= 2:
                    pe.wait_ge(xt_sb.sem, k - 1)
                for b in range(NB):
                    dst = ctx_bank[k % 2][:, 0:P] if b == 0 else lat_bank[k % 2][:, (b - 1) * P:b * P]
                    mm = pe.transpose(dst, x_rows[:, b, k * P:(k + 1) * P], ident)
                mm.then_inc(xt_ps.sem, 1)
            pe.wait_ge(cond_silu.sem, 1)
            pe.transpose(misc_bank[:, 0:3 * KD], cond_rows[:, :], ident[0:3 * KD, 0:3 * KD]).then_inc(cond_ps.sem, 1)
            pe.wait_ge(cond_sb.sem, 1)
            pe.wait_ge(xt_sb.sem, KD)

            def slot(turn, i):
                pe.wait_ge(slot_in[i % RING].sem, turn + (i // RING) * 16 + 16)
                return ring[:, i % RING, :, :]

            def product(lat, ctx_out, weights, rhs, steps):
                for k in range(steps):
                    w = weights(k)
                    x = rhs(k)
                    flags = dict(start=(k == 0), stop=(k == steps - 1))
                    pe.matmul(lat, w, x[:, CTX:TOK], **flags)
                    mm = pe.matmul(ctx_out, w, x[:, 0:CTX], **flags)
                return mm

            def wide_norm(l, which):
                for k in range(KD):
                    pe.wait_ge(sq_done.sem, sq_done.at(l, which * KD + k + 1))
                    flags = dict(start=(k == 0), stop=(k == KD - 1))
                    pe.matmul(sum_lat, ones[:, :], scr[:, k % 2, CTX:TOK], **flags)
                    pe.matmul(sum_ctx, ones[:, :], scr[:, k % 2, 0:CTX], **flags).then_inc(sq_used.sem, 1)

            with pe.Fori(0, DEPTH) as l:
                turn = l * (LAYER_CHUNKS // RING * 16)

                pe.wait_ge(vec_in.sem, vec_in.at(l + 1, 0))
                pe.transpose(misc_bank[:, 0:N_VEC], vec_rows[:, :], ident[0:N_VEC, 0:N_VEC]).then_inc(vec_ps.sem, 1)

                wide_norm(l, 0)

                def fold(c):
                    pe.wait_ge(adar_sb.sem, adar_sb.at(l, c + 1))
                    if c >= 2:
                        pe.wait_ge(ada_sb.sem, ada_sb.at(l, c - 1))
                    for m in range(4):
                        mm = pe.matmul(ctx_bank[c % 2][:, 2 * m:2 * m + 2], scr[:, c % 2, m * P:(m + 1) * P],
                                       consts[:, K_FOLD:K_FOLD + 2], start=True, stop=True)
                    mm.then_inc(ada_ps.sem, 1)

                pe.wait_ge(rms_done.sem, rms_done.at(l, 1))
                for c in range(ADA_CHUNKS):
                    w = slot(turn, c)
                    if c >= 2:
                        pe.wait_ge(adar_sb.sem, adar_sb.at(l, c - 1))
                    for k in range(KD):
                        q = 32 * (k % 4)
                        mm = pe.matmul(lat_bank[c % 2][q:q + 32, :], condP[:, k, :], w[:, k, :],
                                       start=(k < 4), stop=(k >= 4))
                    mm.then_inc(adar_ps.sem, 1)
                    if c >= 1:
                        fold(c - 1)
                fold(ADA_CHUNKS - 1)
                pe.wait_ge(ada_sb.sem, ada_sb.at(l, ADA_CHUNKS))

                def unit_banks(u):
                    if u >= 2:
                        pe.wait_ge(unit_lat.sem, unit_lat.at(l, u - 1))
                        pe.wait_ge(unit_ctx.sem, unit_ctx.at(l, u - 1))
                    return lat_bank[u % 2], ctx_bank[u % 2][:, 0:CTX]

                def turn_pairs(r, rows, unit):
                    pe.wait_ge(unit_lat.sem, unit_lat.at(l, unit + 1))
                    if r >= 1:
                        pe.wait_ge(rope_sb.sem, rope_sb.at(l, r))
                    m = rot_diff if rows == slice(0, P) else rot_mla
                    pe.matmul(rot_bank[rows, :], m[rows, rows], rope_a[rows, r % 2, :], start=True, stop=True)\
                      .then_inc(rope_ps.sem, 1)


                pe.wait_ge(small_in.sem, small_in.at(l + 1, 0))
                w = slot(turn, CH_MLA)
                pe.wait_ge(h_done.sem, h_done.at(l, KD))
                for u, c0, m in ((0, 0, P), (1, P, P), (2, 2 * P, P), (3, C_END - C_CQ - QM, QM)):
                    lat, cx = unit_banks(u)
                    product(lat[0:m, :], cx[0:m, :], lambda k: w[:, k, c0:c0 + m], lambda k: hT[:, k, :], KD)\
                        .then_inc(unit_ps.sem, 1)

                def narrow_sum(n, first_sq, blocks):
                    for j in range(blocks):
                        pe.wait_ge(nsq_done.sem, nsq_done.at(l, first_sq + j + 1))
                        flags = dict(start=(j == 0), stop=(j == blocks - 1))
                        s = (first_sq + j) % 2
                        pe.matmul(sum_lat, ones[:, :], scr[:, s, CTX:TOK], **flags)
                        mm = pe.matmul(sum_ctx, ones[:, :], scr[:, s, 0:CTX], **flags)
                    mm.then_inc(nsum_ps.sem, 1)

                narrow_sum(0, 0, 2)
                pe.wait_ge(unit_lat.sem, unit_lat.at(l, 4))
                pe.transpose(misc_bank[:, 0:P], cache_ckv[:, :], ident)
                pe.transpose(misc_bank[0:QM, P:2 * P], cache_kpe[:, :], ident).then_inc(tr_ps.sem, 1)
                kpe_at = slice(NOPE, QM)
                pe.matmul(rot_bank[kpe_at, :], rot_mla[kpe_at, kpe_at], rope_a[kpe_at, 0, :], start=True, stop=True)\
                  .then_inc(rope_ps.sem, 1)
                pe.wait_ge(nrms_done.sem, nrms_done.at(l, 1))
                narrow_sum(1, 2, 1)

                pe.wait_ge(nscaled.sem, nscaled.at(l, 1))
                for h in range(HEADS):
                    u = 4 + h
                    lat, cx = unit_banks(u)
                    product(lat[0:QM, :], cx[0:QM, :], lambda k: wuq[:, k, h * QM:(h + 1) * QM], lambda k: cqT[:, k, :], 2)\
                        .then_inc(unit_ps.sem, 1)
                    if h >= 1:
                        turn_pairs(h, slice(0, QM), u - 1)
                pe.wait_ge(nscaled.sem, nscaled.at(l, 2))
                pe.wait_ge(tr_sb.sem, tr_sb.at(l, 1))
                for h in range(HEADS):
                    u = 8 + h
                    lat, _ = unit_banks(u)
                    w0 = wukv[:, h * (NOPE + VDIM):h * (NOPE + VDIM) + NOPE]
                    pe.matmul(lat[0:NOPE, :], w0, ckvT[:, 0:512], start=True, stop=True)
                    pe.matmul(ctx_bank[u % 2][0:NOPE, 0:256], w0, ckvT[:, 512:768], start=True, stop=True)\
                      .then_inc(unit_ps.sem, 1)
                    if h == 0:
                        turn_pairs(4, slice(0, QM), u - 1)
                wv = wukv[:, :].rearrange("p (h c) -> p h c", h=HEADS)[:, :, NOPE:NOPE + VDIM]
                for b in range(NB + 1):
                    if b >= 2:
                        pe.wait_ge(vm_sb.sem, vm_sb.at(l, b - 1))
                    dst = S[0][:, (b % 2) * 512:(b % 2) * 512 + HEADS * VDIM]
                    if b == 0:
                        pe.wait_ge(nrms_done.sem, nrms_done.at(l, 2))
                    pe.matmul(dst, ckvT[:, b * P:(b + 1) * P], wv, start=True, stop=True).then_inc(vm_ps.sem, 1)
                pe.wait_ge(kpe_spread.sem, kpe_spread.at(l, 1))
                pe.transpose(misc_bank[:, 0:P], ckvT[:, 0:P], ident)
                pe.transpose(misc_bank[:, P:P + ROPE], kpeT[NOPE:QM, 0:P], ident[NOPE:QM, NOPE:QM]).then_inc(tr_ps.sem, 1)
                pe.wait_ge(tr_sb.sem, tr_sb.at(l, 2))
                pe.wait_ge(rope_sb.sem, rope_sb.at(l, 5))
                pe.wait_ge(vm_sb.sem, vm_sb.at(l, NB + 1))

                def scores(it):
                    kind, h, b = ITS[it]
                    k0, nk = key_cols(b)
                    for comp, g in enumerate(groups(it)):
                        if g % GROUPS >= 2:
                            pe.wait_ge(exp_done.sem, exp_done.at(l, g - 1))
                        rows = slice(0, QM) if kind == "mla" else slice(comp * DH, (comp + 1) * DH)
                        q = qT[rows, h, b * P:(b + 1) * P]
                        bank = S[g % 2]
                        n = min(nk, 512)
                        mm = pe.matmul(bank[:, 0:n], q, kT[rows, h, k0:k0 + n], start=True, stop=True)
                        if nk > n:
                            mm = pe.matmul(bank[:, n:nk], q, kT[rows, h, k0 + n:k0 + nk], start=True, stop=True)
                        mm.then_inc(sc_ps.sem, 1)

                def turn_probs(it):
                    _, h, b = ITS[it]
                    pe.wait_ge(probs_done.sem, probs_done.at(l, it + 1))
                    if it >= 1:
                        pe.wait_ge(pt_sb.sem, pt_sb.at(l, it))
                    for j in range(1 if b == 0 else NB):
                        mm = pe.transpose(T[:, j * P:(j + 1) * P], probs[:, it % 2, 0, j * P:(j + 1) * P], ident)
                    mm.then_inc(pt_ps.sem, 1)

                def apply_probs(it):
                    kind, h, b = ITS[it]
                    pe.wait_ge(pt_sb.sem, pt_sb.at(l, it + 1))
                    if it >= 2:
                        pe.wait_ge(o_sb.sem, o_sb.at(l, it - 1))
                    blocks = [0] if b == 0 else [1, 2, 3, 4, 5]
                    c0 = (it % 2) * 512
                    for j, kb in enumerate(blocks):
                        if kind == "mla":
                            half = (h % 2) * VDIM
                            out = U[half:half + VDIM, c0:c0 + P]
                            v = vm_rows[:, kb, h * VDIM:(h + 1) * VDIM]
                        else:
                            out = U[:, c0:c0 + P]
                            v = (v_rows[:, kb, h * P:(h + 1) * P] if kb < NB else cache_v[:, h * P:(h + 1) * P])
                        mm = pe.matmul(out, v, probsT[:, it % 2, j, :], start=(j == 0), stop=(j == len(blocks) - 1))
                    mm.then_inc(o_ps.sem, 1)

                def attention(first, last):
                    for i in range(first, last + 2):
                        if i < last:
                            scores(i)
                        if first <= i - 1 < last:
                            turn_probs(i - 1)
                        if i - 2 >= first:
                            apply_probs(i - 2)

                pe.wait_ge(unit_lat.sem, unit_lat.at(l, 12))
                pe.wait_ge(unit_ctx.sem, unit_ctx.at(l, 12))
                attention(0, ATT_IT)
                pe.wait_ge(o_sb.sem, o_sb.at(l, ATT_IT))

                for c, u0 in ((CH_Q, 12), (CH_K, 16)):
                    w = slot(turn, c)
                    for h in range(HEADS):
                        u = u0 + h
                        lat, cx = unit_banks(u)
                        product(lat, cx, lambda k: w[:, k, h * P:(h + 1) * P], lambda k: hT[:, k, :], KD)\
                            .then_inc(unit_ps.sem, 1)
                        if u > 12:
                            turn_pairs(4 + u - 12, slice(0, P), u - 1)
                w = slot(turn, CH_V)
                for b in range(NB):
                    if b >= 2:
                        pe.wait_ge(v_sb.sem, v_sb.at(l, b - 1))
                    dst = S[0][:, (b % 2) * 512:(b % 2 + 1) * 512]
                    for k in range(KD):
                        mm = pe.matmul(dst, hT[:, k, b * P:(b + 1) * P], w[:, k, :], start=(k == 0), stop=(k == KD - 1))
                    mm.then_inc(v_ps.sem, 1)
                    if b == 0:
                        turn_pairs(12, slice(0, P), 19)
                w = slot(turn, CH_F)
                for j in range(2):
                    lat, cx = unit_banks(20 + j)
                    product(lat, cx, lambda k: w[:, k, j * P:(j + 1) * P], lambda k: hT[:, k, :], KD)\
                        .then_inc(unit_ps.sem, 1)

                for h in range(HEADS):
                    mm = pe.transpose(misc_bank[:, h * P:(h + 1) * P], cache_k[:, h * P:(h + 1) * P], ident)
                mm.then_inc(tr_ps.sem, 1)
                pe.wait_ge(tr_sb.sem, tr_sb.at(l, 3))
                for h in range(HEADS):
                    mm = pe.transpose(misc_bank[:, h * P:(h + 1) * P], kT[:, h, 0:P], ident)
                mm.then_inc(tr_ps.sem, 1)

                pe.wait_ge(v_sb.sem, v_sb.at(l, NB))
                for j in range(2):
                    for part in range(2):
                        mm = pe.matmul(S[0][:, j * 512 + part * P:j * 512 + (part + 1) * P],
                                       consts[:, K_CHAN + part * P:K_CHAN + (part + 1) * P], wfour[:, j, :],
                                       start=True, stop=True)
                    mm.then_inc(cw_ps.sem, 1)
                pe.wait_ge(cw_sb.sem, cw_sb.at(l, 2))
                pe.wait_ge(unit_lat.sem, unit_lat.at(l, UNITS))
                pe.wait_ge(unit_ctx.sem, unit_ctx.at(l, UNITS))
                for b in range(NB):
                    if b >= 2:
                        pe.wait_ge(fa_sb.sem, fa_sb.at(l, b - 1))
                    for j in range(2):
                        mm = pe.matmul(lat_bank[b % 2][:, j * 256:(j + 1) * 256], zfT[:, j, b * P:(b + 1) * P],
                                       chanw[:, j, :, :], start=True, stop=True)
                    mm.then_inc(fa_ps.sem, 1)
                w = slot(turn, CH_DFT)
                for j in range(2):
                    lat, cx = S[0][:, 0:512], ctx_bank[1][:, 0:CTX]
                    if j == 0:
                        lat, cx = U[:, 0:512], S[0][:, 512:512 + CTX]
                    pe.wait_ge(fa_sb.sem, fa_sb.at(l, NB))
                    for part in range(2):
                        cols = slice(part * P, (part + 1) * P)
                        for b in range(4):
                            pe.matmul(lat, chan_rows[:, b + 1, j, cols], w[:, 4 * part + b, :],
                                      start=(part == 0 and b == 0), stop=(part == 1 and b == 3))
                    for part in range(2):
                        cols = slice(part * P, (part + 1) * P)
                        mm = pe.matmul(cx, chan_rows[:, 0, j, cols], consts[:, K_SEQX + part * CTX:K_SEQX + (part + 1) * CTX],
                                       start=(part == 0), stop=(part == 1))
                    mm.then_inc(fb_ps.sem, 1)

                pe.wait_ge(fb_sb.sem, fb_sb.at(l, 2))
                pe.wait_ge(rope_sb.sem, rope_sb.at(l, ROPES))
                pe.wait_ge(tr_sb.sem, tr_sb.at(l, 4))
                attention(ATT_IT, 2 * ATT_IT)
                pe.wait_ge(exp_done.sem, exp_done.at(l, GROUPS))
                for h in range(HEADS):
                    if h >= 1:
                        pe.wait_ge(nrms_done.sem, nrms_done.at(l, 2 + h))
                    narrow_sum(2 + h, 3 + h, 1)

                pe.wait_ge(nscaled.sem, nscaled.at(l, 6))
                pe.wait_ge(o_sb.sem, o_sb.at(l, 2 * ATT_IT))
                for c in range(2):
                    w = slot(turn, CH_OUT + c)
                    for m in range(4):
                        n = 4 * c + m
                        if n >= 2:
                            pe.wait_ge(mix_sb.sem, mix_sb.at(l, n - 1))
                        product(lat_bank[n % 2], ctx_bank[n % 2][:, 0:CTX], lambda k: w[:, k, m * P:(m + 1) * P],
                                lambda k: yT[:, k, :] if k < 6 else y_mla[:, k - 6, :], KD).then_inc(mix_ps.sem, 1)

                wide_norm(l, 1)
                pe.wait_ge(h_done.sem, h_done.at(l, 2 * KD))
                pe.wait_ge(mix_sb.sem, mix_sb.at(l, KD))
                for b in range(NB):
                    for k in range(KD):
                        mm = pe.matmul(T[:, b * E_N:(b + 1) * E_N], hT[:, k, b * P:(b + 1) * P], wrt[:, k, :],
                                       start=(k == 0), stop=(k == KD - 1))
                mm.then_inc(lg_ps.sem, 1)
                pe.wait_ge(rms_done.sem, rms_done.at(l, 2))
                def rows_of_h(b):
                    if b >= 2:
                        pe.wait_ge(hr_v.sem, hr_v.at(l, b - 1))
                        pe.wait_ge(hr_a.sem, hr_a.at(l, b - 1))
                    for k in range(KD):
                        mm = pe.transpose(S[b % 2][:, k * P:(k + 1) * P], hT[:, k, b * P:(b + 1) * P], ident)
                    mm.then_inc(hr_ps.sem, 1)

                for b in range(NB - 1):
                    rows_of_h(b)
                pe.wait_ge(aff_rows.sem, aff_rows.at(l, 1))
                for b in range(NB):
                    dst = U[0:E_N, 512:512 + P] if b == 0 else U[0:E_N, (b - 1) * P:b * P]
                    mm = pe.transpose(dst, lg[:, b, :], ident)
                mm.then_inc(aff_ps.sem, 1)
                pe.wait_ge(pos_done.sem, pos_done.at(l, 1))
                rows_of_h(NB - 1)
                for b in range(NB):
                    mm = pe.transpose(T[:, b * E_N:(b + 1) * E_N], pos[:, b * P:(b + 1) * P], ident[0:E_N, 0:E_N])
                mm.then_inc(pr_ps.sem, 1)
                def gather_lat(u):
                    pe.wait_ge(pick_done.sem, pick_done.at(u, 1))
                    for half in range(2):
                        for b in range(4):
                            mm = pe.matmul(U[:, half * 512:(half + 1) * 512], pick[:, b, :],
                                           h_rows[:, b + 1, half * 512:(half + 1) * 512], start=(b == 0), stop=(b == 3))
                    mm.then_inc(gl_ps.sem, 1)

                def gather_ctx(u):
                    pe.wait_ge(lg_rows.sem, lg_rows.at(u, 1))
                    for half in range(2):
                        mm = pe.matmul(U[0:2 * CAPX, half * 512:(half + 1) * 512], pickx[:, :],
                                       h_rows[:, 0, half * 512:(half + 1) * 512], start=True, stop=True)
                    mm.then_inc(gx_ps.sem, 1)

                def turn_lat(u):
                    pe.wait_ge(xg_rows.sem, xg_rows.at(u, 1))
                    for k in range(KD):
                        mm = pe.transpose(U[:, k * P:(k + 1) * P], slot_rows[:, k * P:(k + 1) * P], ident)
                    mm.then_inc(tl_ps.sem, 1)

                def turn_ctx(u):
                    n = 2 * CAPX
                    for k in range(KD):
                        rows = slotx_rows[k // 4][0:n, k % 4 * P:(k % 4 + 1) * P]
                        mm = pe.transpose(S[0][:, k * n:(k + 1) * n], rows, ident[0:n, 0:n])
                    mm.then_inc(tx_ps.sem, 1)

                u = l * (PAIRS + 1)
                pe.wait_ge(hr_v.sem, hr_v.at(l, NB))
                pe.wait_ge(hr_a.sem, hr_a.at(l, NB))
                gather_lat(u)
                gather_ctx(u)
                turn_lat(u)
                turn_ctx(u)

                def scatter(v, n, lat, cx, ahead):
                    if n >= ahead:
                        pe.wait_ge(add_sb.sem, add_sb.at(v, n - ahead + 1))
                    cols = slice(n * P, (n + 1) * P)
                    pe.matmul(lat, ye_hi[:, cols], back[:, :], start=True, stop=False)
                    pe.matmul(lat, ye_lo[:, cols], back[:, :], start=False, stop=True)
                    pe.matmul(cx, yex[:, cols], backx[:, :], start=True, stop=True).then_inc(add_ps.sem, 1)

                with pe.Fori(0, PAIRS) as pair:
                    t = l * PAIRS + pair
                    u = l * (PAIRS + 1) + pair + 1

                    def group(g, between={}):
                        i, matrix, half = GROUPS_OF_PAIR[g]
                        if matrix == DOWN:
                            out = T[0:SLOT_TOK, half * 512:(half + 1) * 512]
                        else:
                            out = S[half][0:SLOT_TOK, matrix * 512:(matrix + 1) * 512]
                        for piece in range(PIECES):
                            n = g * PIECES + piece
                            pe.wait_ge(lo_done.sem, lo_done.at(t, n + 1))
                            for kk in range(2):
                                k = 2 * piece + kk
                                x_hi = hm_hi[:, i, k, :] if matrix == DOWN else xs_hi[:, k, i, :]
                                x_lo = hm_lo[:, i, k, :] if matrix == DOWN else xs_lo[:, k, i, :]
                                w_low = ring_lo[:, g % RING, k, :]
                                pe.matmul(out, x_lo, w_hi[:, piece, kk, :], start=(k == 0), stop=False)
                                pe.matmul(out, x_hi, w_hi[:, piece, kk, :], start=False, stop=False)
                                mm = pe.matmul(out, x_hi, w_low, start=False, stop=(k == KD - 1))
                            mm.then_inc(piece_ps.sem if piece < PIECES - 1 else gr_ps.sem, 1)
                            if piece in between:
                                scatter(u - 1, between[piece], T[:, 0:LAT], T[:, 512:512 + CTX], 1)

                    def turn_middle(i):
                        pe.wait_ge(hm_done.sem, hm_done.at(t, 2 * i + 2))
                        for j in range(KD):
                            c0 = (j // 4) * 512 + (j % 4) * SLOT_TOK
                            mm = pe.transpose(U[:, c0:c0 + SLOT_TOK], hm_rows[i][0:SLOT_TOK, j * P:(j + 1) * P],
                                              ident[0:SLOT_TOK, 0:SLOT_TOK])
                        mm.then_inc(th_ps.sem, 1)

                    pe.wait_ge(back_done.sem, back_done.at(t, 0))
                    pe.wait_ge(gate_cols.sem, gate_cols.at(t, 1))
                    for i in range(2):
                        out = U[:, 256 + i:257 + i]
                        for b in range(4):
                            pe.matmul(out[0:CAP, :], pick[:, b, i * CAP:(i + 1) * CAP], cur_gate[:, b + 1, i:i + 1],
                                      start=(b == 0), stop=(b == 3))
                        mm = pe.matmul(out[CAP:SLOT_TOK, :], pickx[:, i * CAPX:(i + 1) * CAPX], cur_gate[:, 0, i:i + 1],
                                       start=True, stop=True)
                    mm.then_inc(gate_ps.sem, 1)
                    pe.wait_ge(xx_lo.sem, xx_lo.at(u - 1, 1))
                    group(0)
                    pe.wait_ge(rows_done.sem, rows_done.at(u - 1, 1))
                    group(1, {1: 0, 3: 1})
                    group(2, {2: 2})
                    group(3, {1: 3})
                    pe.wait_ge(hm_done.sem, hm_done.at(t, 1))
                    group(4, {1: 4})
                    pe.wait_ge(gate_sb.sem, gate_sb.at(t, 1))
                    turn_middle(0)
                    group(5, {1: 5})
                    pe.wait_ge(hl_done.sem, hl_done.at(t, 1))
                    gather_lat(u)
                    group(6, {1: 6})
                    gather_ctx(u)
                    group(7, {0: 7})
                    turn_lat(u)
                    pe.wait_ge(add_sb.sem, add_sb.at(u - 1, KD))
                    group(8)
                    pe.wait_ge(xl_lo.sem, xl_lo.at(u, 1))
                    turn_middle(1)
                    turn_ctx(u)
                    group(9)
                    pe.wait_ge(hl_done.sem, hl_done.at(t, 2))
                    pe.wait_ge(ye0_lo.sem, ye0_lo.at(t, 1))
                    group(10)
                    pe.wait_ge(sel_done.sem, sel_done.at(t, 1))
                    pe.matmul(U[:, 0:LAT], sel[:, :, :].rearrange("e i c -> e (i c)"), pos[:, CTX:TOK], start=True, stop=True)
                    pe.matmul(U[:, 512:512 + CTX], selx[:, :, :, :].rearrange("e a i c -> e (a i c)"), pos[:, 0:CTX],
                              start=True, stop=True).then_inc(place_ps.sem, 1)
                    pe.wait_ge(ye0_lo.sem, ye0_lo.at(t, 2))
                    group(11)
                u = l * (PAIRS + 1) + PAIRS
                pe.wait_ge(rows_done.sem, rows_done.at(u, 1))
                for n in range(KD):
                    scatter(u, n, lat_bank[n % 2], ctx_bank[n % 2][:, 0:CTX], 2)
                pe.wait_ge(add_sb.sem, add_sb.at(u, KD))

            wide_norm(DEPTH, 0)
            pe.wait_ge(xn_done.sem, xn_done.at(DEPTH, KD))
            for b in range(NB):
                if b >= 2:
                    pe.wait_ge(fin_v.sem, b - 1)
                    pe.wait_ge(fin_a.sem, b - 1)
                if b == 0:
                    pe.wait_ge(rms_done.sem, rms_done.at(DEPTH, 1))
                for k in range(KD):
                    mm = pe.transpose(S[b % 2][:, k * P:(k + 1) * P], hT[:, k, b * P:(b + 1) * P], ident)
                mm.then_inc(fin_ps.sem, 1)

        @block.scalar
        def _(act):
            act.wait_ge(const_in.sem, const_in.at(0, 0))
            act.activation(cond_e[:, :], cond_rows[0:2 * KD, :], ACT.Exp, scale=-1.0).then_inc(cond_exp.sem, 1)

            def root(n_feat, ready, value, l, s, done):
                act.wait_ge(ready, value)
                act.activation(rstd[:, CTX:TOK], sum_lat, ACT.Ln, bias=eps, scale=1.0 / n_feat)
                act.activation(rstd[:, 0:CTX], sum_ctx, ACT.Ln, bias=eps, scale=1.0 / n_feat).then_inc(step_a.sem, 1)
                act.wait_ge(step_a.sem, step_a.at(l, s))
                act.activation(rstd[:, :], rstd[:, :], ACT.Exp, scale=-0.5).then_inc(done, 1)

            def squares(l, which):
                for k in range(KD):
                    if k >= 2:
                        act.wait_ge(sq_used.sem, sq_used.at(l, which * KD + k - 1))
                    if which == 1:
                        act.wait_ge(mix_sb.sem, mix_sb.at(l, k + 1))
                    act.activation(scr[:, k % 2, :], xT[:, k, :], ACT.Square).then_inc(sq_done.sem, 1)

            def modulate(l, which):
                for k in range(KD):
                    act.wait_ge(xn_done.sem, xn_done.at(l, which * KD + k + 1))
                    sh = 3 * which * KD + k
                    act.activation(hT[:, k, 0:CTX], hT[:, k, 0:CTX], ACT.Identity, bias=mod[:, sh, 0:1],
                                   scale=gain[:, which, k, 0:1])
                    act.activation(hT[:, k, CTX:TOK], hT[:, k, CTX:TOK], ACT.Identity, bias=mod[:, sh, 1:2],
                                   scale=gain[:, which, k, 1:2]).then_inc(h_done.sem, 1)

            act.wait_ge(xt_sb.sem, KD)
            with act.Fori(0, DEPTH) as l:
                act.wait_ge(add_sb.sem, add_sb.at(l * (PAIRS + 1), 0))
                squares(l, 0)
                root(D, sq_used.sem, sq_used.at(l, KD), l, 1, rms_done.sem)
                for c in range(ADA_CHUNKS):
                    act.wait_ge(adar_ps.sem, adar_ps.at(l, c + 1))
                    if c >= 2:
                        act.wait_ge(ada_ps.sem, ada_ps.at(l, c - 1))
                    act.activation(scr[:, c % 2, 0:512], lat_bank[c % 2], ACT.Copy).then_inc(adar_sb.sem, 1)
                act.wait_ge(lam_prod.sem, lam_prod.at(l, 1))
                act.activation(lamw[:, 0:2], lamw[:, 0:2], ACT.Exp).then_inc(lam_exp.sem, 1)
                act.wait_ge(gain_sb.sem, gain_sb.at(l, 1))
                modulate(l, 0)

                def ctx_copy(u, dst):
                    act.wait_ge(unit_ps.sem, unit_ps.at(l, u + 1))
                    m = dst.shape[0]
                    act.activation(dst, ctx_bank[u % 2][0:m, 0:dst.shape[1]], ACT.Copy).then_inc(unit_ctx.sem, 1)

                def narrow_square(n, src, lat_ready):
                    act.wait_ge(*lat_ready)
                    act.activation(scr[:, n % 2, :], src, ACT.Square).then_inc(nsq_done.sem, 1)

                ctx_copy(0, cqT[:, 0, 0:CTX])
                ctx_copy(1, cqT[:, 1, 0:CTX])
                act.wait_ge(unit_ctx.sem, unit_ctx.at(l, 2))
                narrow_square(0, cqT[:, 0, :], (unit_lat.sem, unit_lat.at(l, 1)))
                narrow_square(1, cqT[:, 1, :], (unit_lat.sem, unit_lat.at(l, 2)))
                ctx_copy(2, ckvT[:, 0:CTX])
                act.wait_ge(unit_ps.sem, unit_ps.at(l, 4))
                act.activation(kpeT[NOPE:QM, 0:CTX], ctx_bank[1][NOPE:QM, 0:CTX], ACT.Copy).then_inc(unit_ctx.sem, 1)
                root(2 * P, nsum_ps.sem, nsum_ps.at(l, 1), l, 2, nrms_done.sem)
                act.wait_ge(unit_ctx.sem, unit_ctx.at(l, 3))
                narrow_square(2, ckvT[:, 0:TOK], (unit_lat.sem, unit_lat.at(l, 3)))
                act.wait_ge(tr_ps.sem, tr_ps.at(l, 1))
                act.activation(ckvT[:, TOK:TOK + PAST], misc_bank[:, 0:P], ACT.Copy)
                act.activation(kpeT[NOPE:QM, TOK:TOK + PAST], misc_bank[NOPE:QM, P:2 * P], ACT.Copy).then_inc(tr_sb.sem, 1)
                act.wait_ge(nscaled.sem, nscaled.at(l, 1))
                root(P, nsum_ps.sem, nsum_ps.at(l, 2), l, 3, nrms_done.sem)
                for h in range(HEADS):
                    ctx_copy(4 + h, qT[0:QM, h, 0:CTX])
                for h in range(HEADS):
                    ctx_copy(8 + h, kT[0:NOPE, h, 512:768])
                for b in range(NB + 1):
                    act.wait_ge(vm_ps.sem, vm_ps.at(l, b + 1))
                    act.activation(vm_rows[:, b, :], S[0][:, (b % 2) * 512:(b % 2) * 512 + HEADS * VDIM], ACT.Copy)\
                       .then_inc(vm_sb.sem, 1)
                act.wait_ge(tr_ps.sem, tr_ps.at(l, 2))
                act.activation(ckv_rows[:, :], misc_bank[:, 0:P], ACT.Copy)
                act.activation(kpe_rows[:, :], misc_bank[:, P:P + ROPE], ACT.Copy).then_inc(tr_sb.sem, 1)
                act.wait_ge(tr_sb.sem, tr_sb.at(l, 2))
                act.dma_start(a["new_mla_ckv"][0, l], ckv_rows[:, :]).then_inc(outs_done.sem, 16)
                act.dma_start(a["new_mla_kpe"][0, l], kpe_rows[:, :]).then_inc(outs_done.sem, 16)

                def attention(first, last):
                    for i in range(first, last + 1):
                        if i < last:
                            kind, h, b = ITS[i]
                            nk = key_cols(b)[1]
                            for comp, g in enumerate(groups(i)):
                                act.wait_ge(negm_done.sem, negm_done.at(l, g + 1))
                                act.activation(probs[:, i % 2, comp, 0:nk], S[g % 2][:, 0:nk], ACT.Exp, bias=negm[:, g % 2:g % 2 + 1],
                                               scale=MLA_SCALE if kind == "mla" else DIFF_SCALE,
                                               accum_out=ssum[:, i % 2, comp:comp + 1]).then_inc(exp_done.sem, 1)
                        if i > first:
                            it = i - 1
                            _, h, b = ITS[it]
                            n = P if b == 0 else KEYS
                            act.wait_ge(pt_ps.sem, pt_ps.at(l, it + 1))
                            if it - 2 >= 0:
                                act.wait_ge(o_ps.sem, o_ps.at(l, it - 1))
                            act.activation(probsT[:, it % 2, :, :].rearrange("p j q -> p (j q)")[:, 0:n], T[:, 0:n], ACT.Copy)\
                               .then_inc(pt_sb.sem, 1)

                attention(0, ATT_IT)
                for h in range(HEADS):
                    ctx_copy(12 + h, qT[:, h, 0:CTX])
                for h in range(HEADS):
                    ctx_copy(16 + h, kT[:, h, 0:CTX])
                for b in range(NB):
                    act.wait_ge(v_ps.sem, v_ps.at(l, b + 1))
                    act.activation(v_rows[:, b, :], S[0][:, (b % 2) * 512:(b % 2 + 1) * 512], ACT.Copy).then_inc(v_sb.sem, 1)
                for j in range(2):
                    ctx_copy(20 + j, zfT[:, j, 0:CTX])
                act.wait_ge(v_sb.sem, v_sb.at(l, 1))
                act.dma_start(a["new_diff_v"][0, l].rearrange("t h d -> t (h d)"), v_rows[:, 0, :]).then_inc(outs_done.sem, 16)
                act.wait_ge(tr_ps.sem, tr_ps.at(l, 3))
                act.activation(kT[:, :, TOK:TOK + PAST], misc_bank.rearrange("p (h t) -> p h t", h=HEADS), ACT.Copy)\
                   .then_inc(tr_sb.sem, 1)
                act.wait_ge(tr_ps.sem, tr_ps.at(l, 4))
                act.activation(k_rows[:, :], misc_bank, ACT.Copy).then_inc(tr_sb.sem, 1)
                act.wait_ge(tr_sb.sem, tr_sb.at(l, 4))
                act.dma_start(a["new_diff_k"][0, l].rearrange("t h d -> t (h d)"), k_rows[:, :]).then_inc(outs_done.sem, 16)
                for j in range(2):
                    act.wait_ge(cw_ps.sem, cw_ps.at(l, j + 1))
                    act.activation(chanw[:, j, :, :].rearrange("p a e -> p (a e)"), S[0][:, j * 512:j * 512 + 2 * P], ACT.Copy)\
                       .then_inc(cw_sb.sem, 1)
                for b in range(NB):
                    act.wait_ge(fa_ps.sem, fa_ps.at(l, b + 1))
                    act.activation(chan_rows[:, b, :, :].rearrange("p j e -> p (j e)"), lat_bank[b % 2], ACT.Copy)\
                       .then_inc(fa_sb.sem, 1)
                attention(ATT_IT, 2 * ATT_IT)
                act.wait_ge(o_sb.sem, o_sb.at(l, 2 * ATT_IT))
                for h in range(HEADS):
                    if h >= 1:
                        act.wait_ge(nsum_ps.sem, nsum_ps.at(l, 2 + h))
                    narrow_square(3 + h, yT[:, 2 + h, :], (o_sb.sem, o_sb.at(l, 2 * ATT_IT)))
                    if h >= 1:
                        act.wait_ge(nscaled.sem, nscaled.at(l, 2 + h))
                    root(P, nsum_ps.sem, nsum_ps.at(l, 3 + h), l, 4 + h, nrms_done.sem)

                squares(l, 1)
                act.wait_ge(nscaled.sem, nscaled.at(l, 6))
                root(D, sq_used.sem, sq_used.at(l, 2 * KD), l, 8, rms_done.sem)
                modulate(l, 1)
                act.wait_ge(lg_shift.sem, lg_shift.at(l, 1))
                act.activation(lg[:, :, :], lg[:, :, :], ACT.Exp).then_inc(lg_exp.sem, 1)
                act.wait_ge(outs_done.sem, outs_done.at(l + 1, 0))
                for b in range(NB):
                    act.wait_ge(hr_ps.sem, hr_ps.at(l, b + 1))
                    act.activation(h_rows[:, b, 512:1024], S[b % 2][:, 512:1024], ACT.Copy).then_inc(hr_a.sem, 1)
                def copy_lat_rows(u):
                    act.wait_ge(gl_ps.sem, gl_ps.at(u, 1))
                    act.activation(slot_rows, U[:, :], ACT.Copy).then_inc(lg_rows.sem, 1)

                def copy_ctx_rows(u):
                    act.wait_ge(gx_ps.sem, gx_ps.at(u, 1))
                    for half in range(2):
                        ins = act.activation(slotx_rows[half][0:2 * CAPX, :], U[0:2 * CAPX, half * 512:(half + 1) * 512], ACT.Copy)
                    ins.then_inc(xg_rows.sem, 1)

                def high_lat(u):
                    act.wait_ge(tl_ps.sem, tl_ps.at(u, 1))
                    act.activation(xs_hi[:, :, :, 0:CAP], U[:, :].rearrange("p (k i c) -> p k i c", k=KD, i=2), ACT.Copy)\
                       .then_inc(xl_hi.sem, 1)

                def high_ctx(u):
                    act.wait_ge(tx_ps.sem, tx_ps.at(u, 1))
                    act.activation(xs_hi[:, :, :, CAP:SLOT_TOK],
                                   S[0][:, 0:KD * 2 * CAPX].rearrange("p (k i c) -> p k i c", k=KD, i=2), ACT.Copy)\
                       .then_inc(xx_hi.sem, 1)

                u = l * (PAIRS + 1)
                copy_lat_rows(u)
                copy_ctx_rows(u)
                high_lat(u)
                high_ctx(u)

                def out_rows(i, half, done):
                    cols = slice(half * 512, (half + 1) * 512)
                    act.activation(ye_hi[i * CAP:(i + 1) * CAP, cols], T[0:CAP, cols], ACT.Copy)
                    act.activation(yex[i * XROW:i * XROW + CAPX, cols], T[CAP:SLOT_TOK, cols], ACT.Copy)\
                       .then_inc(done.sem, 1)

                with act.Fori(0, PAIRS) as pair:
                    t = l * PAIRS + pair
                    u = l * (PAIRS + 1) + pair + 1

                    def high_pieces(g):
                        act.wait_ge(slot_in[g % RING].sem,
                                    (l * LAYER_CHUNKS + DENSE_CHUNKS + pair * PAIR_CHUNKS) * (16 // RING) + (g // RING + 1) * 16)
                        for piece in range(PIECES):
                            if piece < PIECES - 1:
                                act.wait_ge(piece_ps.sem, piece_ps.at(t, (g - 1) * (PIECES - 1) + piece + 1))
                            else:
                                act.wait_ge(gr_ps.sem, gr_ps.at(t, g))
                            act.activation(w_hi[:, piece, :, :], ring[:, g % RING, 2 * piece:2 * piece + 2, :], ACT.Copy)\
                               .then_inc(hi_done.sem, 1)

                    def silu(i, half):
                        act.wait_ge(gr_ps.sem, gr_ps.at(t, 4 * i + 2 * half + 1))
                        act.activation(hm_rows[i][0:SLOT_TOK, half * 512:(half + 1) * 512], S[half][0:SLOT_TOK, 0:512], ACT.Silu)\
                           .then_inc(silu_done.sem, 1)

                    def high_middle(i):
                        act.wait_ge(th_ps.sem, th_ps.at(t, i + 1))
                        act.activation(hm_hi[:, i, :, :].rearrange("p (b j) c -> p b (j c)", b=2),
                                       U[:, :].rearrange("p (b n) -> p b n", b=2)[:, :, 0:4 * SLOT_TOK], ACT.Copy)\
                           .then_inc(hh_done.sem, 1)

                    high_pieces(0)
                    act.wait_ge(gate_ps.sem, gate_ps.at(t, 1))
                    act.activation(gates[:, :], U[0:SLOT_TOK, 256:258], ACT.Copy).then_inc(gate_sb.sem, 1)
                    act.wait_ge(gr_ps.sem, gr_ps.at(t, 0))
                    act.wait_ge(t_clear.sem, t_clear.at(l, 1))
                    out_rows(1, 0, ye1_hi)
                    out_rows(1, 1, ye1_hi)
                    high_pieces(1)
                    silu(0, 0)
                    high_pieces(2)
                    high_pieces(3)
                    silu(0, 1)
                    high_pieces(4)
                    high_pieces(5)
                    high_middle(0)
                    silu(1, 0)
                    high_pieces(6)
                    copy_lat_rows(u)
                    high_pieces(7)
                    copy_ctx_rows(u)
                    silu(1, 1)
                    high_pieces(8)
                    high_lat(u)
                    high_pieces(9)
                    high_middle(1)
                    high_ctx(u)
                    act.wait_ge(gr_ps.sem, gr_ps.at(t, 9))
                    out_rows(0, 0, ye0_hi)
                    high_pieces(10)
                    act.wait_ge(gr_ps.sem, gr_ps.at(t, 10))
                    out_rows(0, 1, ye0_hi)
                    high_pieces(11)
                act.wait_ge(gr_ps.sem, gr_ps.at((l + 1) * PAIRS, 0))
                out_rows(1, 0, ye1_hi)
                out_rows(1, 1, ye1_hi)

            act.wait_ge(add_sb.sem, add_sb.at(DEPTH * (PAIRS + 1), 0))
            squares(DEPTH, 0)
            root(D, sq_used.sem, sq_used.at(DEPTH, KD), DEPTH, 1, rms_done.sem)
            for b in range(NB):
                act.wait_ge(fin_ps.sem, b + 1)
                act.activation(arena[:, b * D + 512:(b + 1) * D], S[b % 2][:, 512:1024], ACT.Copy).then_inc(fin_a.sem, 1)

        @block.vector
        def _(ve):
            count = [0]

            def link(ins):
                count[0] += 1
                ins.then_inc(step_v, 1)
                ve.wait_ge(step_v, count[0])

            ve.wait_ge(cond_exp.sem, 1)
            link(ve.tensor_scalar(cond_e[:, :], cond_e[:, :], 1.0, None, ALU.add))
            link(ve.reciprocal(cond_e[:, :], cond_e[:, :]))
            ve.tensor_tensor(cond_rows[0:2 * KD, :], cond_rows[0:2 * KD, :], cond_e[:, :], ALU.mult).then_inc(cond_silu.sem, 1)
            for k in range(KD):
                ve.wait_ge(xt_ps.sem, k + 1)
                ve.tensor_copy(xT[:, k, 0:CTX], ctx_bank[k % 2][:, 0:CTX])
                ve.tensor_copy(xT[:, k, CTX:TOK], lat_bank[k % 2]).then_inc(xt_sb.sem, 1)
            ve.wait_ge(cond_ps.sem, 1)
            link(ve.tensor_copy(condT[:, :], misc_bank[:, 0:3 * KD]))
            ve.tensor_copy(condP[:, :, 0:2], condT[:, 0:2 * KD].rearrange("p (s k) -> p k s", s=2)).then_inc(cond_sb.sem, 1)
            ve.sem_inc(add_sb.sem, 1)
            ve.sem_inc(back_done.sem, 1)
            ve.sem_inc(pr_sb.sem, 1)

            def normalise(l, which):
                ve.wait_ge(rms_done.sem, rms_done.at(l, which + 1))
                for k in range(KD):
                    ve.tensor_tensor(hT[:, k, :], xT[:, k, :], rstd[:, :], ALU.mult).then_inc(xn_done.sem, 1)

            with ve.Fori(0, DEPTH) as l:
                ve.sem_clear(step_v)
                count[0] = 0
                ve.wait_ge(vec_ps.sem, vec_ps.at(l, 1))
                ve.tensor_copy(vecT[:, :], misc_bank[:, 0:N_VEC]).then_inc(vec_sb.sem, 1)
                ve.wait_ge(vec_sb.sem, vec_sb.at(l, 1))
                normalise(l, 0)
                for c in range(ADA_CHUNKS):
                    ve.wait_ge(ada_ps.sem, ada_ps.at(l, c + 1))
                    ve.tensor_tensor(mod[:, 4 * c:4 * c + 4, :], ctx_bank[c % 2][:, 0:8].rearrange("p (m s) -> p m s", s=2),
                                     vecT[:, 4 * c:4 * c + 4].unsqueeze(2).broadcast_to([P, 4, 2]), ALU.add)\
                      .then_inc(ada_sb.sem, 1)
                ve.wait_ge(ada_sb.sem, ada_sb.at(l, ADA_CHUNKS))
                for which in range(2):
                    g0 = N_MOD * KD + which * KD
                    s0 = (3 * which + 1) * KD
                    ins = ve.scalar_tensor_tensor(out=gain[:, which, :, :], in0=mod[:, s0:s0 + KD, :], scalar=1.0,
                                                  in1=vecT[:, g0:g0 + KD].unsqueeze(2).broadcast_to([P, KD, 2]),
                                                  op0=ALU.add, op1=ALU.mult)
                ins.then_inc(gain_sb.sem, 1)
                ve.wait_ge(small_in.sem, small_in.at(l + 1, 0))
                pairs = dlam[:, :, :].rearrange("p (a b) d -> p a b d", b=2)
                link(ve.tensor_tensor(dprod[:, :, :], pairs[:, :, 0, :], pairs[:, :, 1, :], ALU.mult))
                ve.reduce_sum(lamw[:, 0:2], dprod[:, :, :], AX.X).then_inc(lam_prod.sem, 1)
                ve.wait_ge(lam_exp.sem, lam_exp.at(l, 1))
                link(ve.scalar_tensor_tensor(out=lamw[:, 2:3], in0=lamw[:, 1:2], scalar=lamw[:, 0:1], in1=lamt[:, 0:1],
                                                op0=ALU.subtract, op1=ALU.subtract))
                ve.tensor_tensor(gsub[:, :], vecT[:, N_VEC - 1:N_VEC], lamt[:, 1:2], ALU.mult).then_inc(lam_done.sem, 1)
                ve.wait_ge(lam_done.sem, lam_done.at(l, 1))

                rope_n = [0]

                def lat_copy(u, dst):
                    ve.wait_ge(unit_ps.sem, unit_ps.at(l, u + 1))
                    ve.tensor_copy(dst, lat_bank[u % 2][0:dst.shape[0], :]).then_inc(unit_lat.sem, 1)

                def rope_parts(u, dst, rows, cos, sin):
                    r = rope_n[0]
                    ve.wait_ge(unit_ps.sem, unit_ps.at(l, u + 1))
                    if r >= 2:
                        ve.wait_ge(rope_ps.sem, rope_ps.at(l, r - 1))
                    z = lat_bank[u % 2][rows, :]
                    ve.tensor_tensor(dst, z, cos[rows, :], ALU.mult)
                    ve.tensor_tensor(rope_a[rows, r % 2, :], z, sin[rows, :], ALU.mult).then_inc(unit_lat.sem, 1)
                    rope_n[0] += 1

                def rope_add(r, dst, rows):
                    ve.wait_ge(rope_ps.sem, rope_ps.at(l, r + 1))
                    ve.tensor_tensor(dst, rot_bank[rows, :], dst, ALU.add).then_inc(rope_sb.sem, 1)

                def narrow_scale(n, dst, g_col):
                    ve.wait_ge(nrms_done.sem, nrms_done.at(l, n + 1))
                    for j, blk in enumerate(dst):
                        ins = ve.scalar_tensor_tensor(out=blk, in0=blk, scalar=g_col[:, j:j + 1], in1=rstd[:, :],
                                                      op0=ALU.mult, op1=ALU.mult)
                    ins.then_inc(nscaled.sem, 1)

                lat_copy(0, cqT[:, 0, CTX:TOK])
                lat_copy(1, cqT[:, 1, CTX:TOK])
                lat_copy(2, ckvT[:, CTX:TOK])
                kpe_rows_at = slice(NOPE, QM)
                rope_parts(3, kpeT[NOPE:QM, CTX:TOK], kpe_rows_at, cos_m, sin_m)
                gq = N_VEC - 4
                narrow_scale(0, [cqT[:, 0, :], cqT[:, 1, :]], vecT[:, gq:gq + 2])
                rope_add(0, kpeT[NOPE:QM, CTX:TOK], kpe_rows_at)
                ve.wait_ge(rope_sb.sem, rope_sb.at(l, 1))
                ve.wait_ge(unit_ctx.sem, unit_ctx.at(l, 4))
                ve.wait_ge(tr_sb.sem, tr_sb.at(l, 1))
                for h in range(HEADS):
                    ins = ve.tensor_copy(kT[NOPE:QM, h, :], kpeT[NOPE:QM, :])
                ins.then_inc(kpe_spread.sem, 1)
                narrow_scale(1, [ckvT[:, 0:TOK]], vecT[:, gq + 2:gq + 3])
                q_rows_at = slice(0, QM)
                for h in range(HEADS):
                    rope_parts(4 + h, qT[0:QM, h, CTX:TOK], q_rows_at, cos_m, sin_m)
                    if h >= 1:
                        rope_add(h, qT[0:QM, h - 1, CTX:TOK], q_rows_at)
                lat_copy(8, kT[0:NOPE, 0, 0:512])
                rope_add(4, qT[0:QM, HEADS - 1, CTX:TOK], q_rows_at)
                for h in range(1, HEADS):
                    lat_copy(8 + h, kT[0:NOPE, h, 0:512])

                def attention(first, last):
                    for i in range(first, last + 3):
                        if first <= i - 1 < last:
                            it = i - 1
                            kind, h, b = ITS[it]
                            n = key_cols(b)[1]
                            s = it % 2
                            ve.wait_ge(exp_done.sem, exp_done.at(l, groups(it)[-1] + 1))
                            if kind == "mla":
                                link(ve.reciprocal(srec[:, s, 0:1], ssum[:, s, 0:1]))
                                ve.tensor_scalar(probs[:, s, 0, 0:n], probs[:, s, 0, 0:n], srec[:, s, 0:1], None, ALU.mult)\
                                  .then_inc(probs_done.sem, 1)
                            else:
                                link(ve.reciprocal(srec[:, s, :], ssum[:, s, :]))
                                ve.tensor_scalar(probs[:, s, 0, 0:n], probs[:, s, 0, 0:n], srec[:, s, 0:1], None, ALU.mult)
                                link(ve.tensor_scalar(srec[:, s, 1:2], srec[:, s, 1:2], lamw[:, 2:3], None, ALU.mult))
                                ve.scalar_tensor_tensor(out=probs[:, s, 0, 0:n], in0=probs[:, s, 1, 0:n], scalar=srec[:, s, 1:2],
                                                        in1=probs[:, s, 0, 0:n], op0=ALU.mult, op1=ALU.add)\
                                  .then_inc(probs_done.sem, 1)
                        if i < last:
                            kind, h, b = ITS[i]
                            nk = key_cols(b)[1]
                            for g in groups(i):
                                c = slice(g % 2, g % 2 + 1)
                                ve.wait_ge(sc_ps.sem, sc_ps.at(l, g + 1))
                                link(ve.reduce_max(smax[:, c], S[g % 2][:, 0:nk], AX.X))
                                ve.tensor_scalar(negm[:, c], smax[:, c], -(MLA_SCALE if kind == "mla" else DIFF_SCALE), None,
                                                 ALU.mult).then_inc(negm_done.sem, 1)
                        if i - 3 >= first:
                            it = i - 3
                            kind, h, b = ITS[it]
                            c0 = (it % 2) * 512
                            ve.wait_ge(o_ps.sem, o_ps.at(l, it + 1))
                            if kind == "mla":
                                half = slice((h % 2) * VDIM, (h % 2 + 1) * VDIM)
                                ins = ve.tensor_copy(y_mla[half, h // 2, b * P:(b + 1) * P], U[half, c0:c0 + P])
                            else:
                                ins = ve.tensor_copy(yT[:, 2 + h, b * P:(b + 1) * P], U[:, c0:c0 + P])
                            ins.then_inc(o_sb.sem, 1)

                attention(0, ATT_IT)
                all_rows = slice(0, P)
                for j in range(8):
                    dst = qT if j < 4 else kT
                    rope_parts(12 + j, dst[:, j % 4, CTX:TOK], all_rows, cos_d, sin_d)
                    if j >= 1:
                        prev = qT if j - 1 < 4 else kT
                        rope_add(4 + j, prev[:, (j - 1) % 4, CTX:TOK], all_rows)
                rope_add(12, kT[:, 3, CTX:TOK], all_rows)
                for j in range(2):
                    lat_copy(20 + j, zfT[:, j, CTX:TOK])
                for j in range(2):
                    lat, cx = (U[:, 0:512], S[0][:, 512:512 + CTX]) if j == 0 else (S[0][:, 0:512], ctx_bank[1][:, 0:CTX])
                    ve.wait_ge(fb_ps.sem, fb_ps.at(l, j + 1))
                    ve.tensor_copy(yT[:, j, CTX:TOK], lat)
                    ve.tensor_copy(yT[:, j, 0:CTX], cx).then_inc(fb_sb.sem, 1)
                attention(ATT_IT, 2 * ATT_IT)
                ve.wait_ge(o_sb.sem, o_sb.at(l, 2 * ATT_IT))
                for h in range(HEADS):
                    narrow_scale(2 + h, [yT[:, 2 + h, :]], gsub)

                def residual(n, gate_block, lat, cx):
                    ve.scalar_tensor_tensor(out=xT[:, n, CTX:TOK], in0=lat, scalar=mod[:, gate_block + n, 1:2],
                                            in1=xT[:, n, CTX:TOK], op0=ALU.mult, op1=ALU.add)
                    return ve.scalar_tensor_tensor(out=xT[:, n, 0:CTX], in0=cx,
                                                   scalar=mod[:, gate_block + n, 0:1], in1=xT[:, n, 0:CTX],
                                                   op0=ALU.mult, op1=ALU.add)

                for n in range(KD):
                    ve.wait_ge(mix_ps.sem, mix_ps.at(l, n + 1))
                    residual(n, 2 * KD, lat_bank[n % 2], ctx_bank[n % 2][:, 0:CTX]).then_inc(mix_sb.sem, 1)

                ve.wait_ge(mix_sb.sem, mix_sb.at(l, KD))
                normalise(l, 1)
                ve.wait_ge(lg_ps.sem, lg_ps.at(l, 1))
                logits = T[:, 0:NB * E_N].rearrange("p (b e) -> p b e", b=NB)
                link(ve.reduce_max(lmax[:, :], logits, AX.X))
                ve.tensor_tensor(lg[:, :, :], logits, lmax[:, :].unsqueeze(2).broadcast_to([P, NB, E_N]), ALU.subtract)\
                  .then_inc(lg_shift.sem, 1)
                ve.wait_ge(outs_done.sem, outs_done.at(l + 1, 0))
                ve.wait_ge(lg_exp.sem, lg_exp.at(l, 1))
                link(ve.reduce_sum(lmax[:, :], lg[:, :, :], AX.X))
                link(ve.reciprocal(lmax[:, :], lmax[:, :]))
                ve.tensor_tensor(lg[:, :, :], lg[:, :, :], lmax[:, :].unsqueeze(2).broadcast_to([P, NB, E_N]), ALU.mult)\
                  .then_inc(aff_rows.sem, 1)
                def rows_of_h(b):
                    ve.wait_ge(hr_ps.sem, hr_ps.at(l, b + 1))
                    ve.tensor_copy(h_rows[:, b, 0:512], S[b % 2][:, 0:512]).then_inc(hr_v.sem, 1)

                for b in range(NB - 1):
                    rows_of_h(b)
                ve.wait_ge(aff_ps.sem, aff_ps.at(l, 1))
                ve.tensor_copy(aff[0:E_N, 0:CTX], U[0:E_N, 512:512 + CTX])
                link(ve.tensor_copy(aff[0:E_N, CTX:TOK], U[0:E_N, 0:LAT]))
                link(ve.tensor_copy(work[0:E_N, :], aff[0:E_N, :]))
                for cols, cap in ((slice(0, CTX), CAPX), (slice(CTX, TOK), CAP)):
                    for _ in range(cap // 8):
                        link(ve.max(top8[:, :], work[0:E_N, cols]))
                        link(ve.match_replace(work[0:E_N, cols], top8[:, :], work[0:E_N, cols], -1.0))
                link(ve.tensor_scalar(mask[0:E_N, :], work[0:E_N, :], 0.0, None, ALU.is_lt))
                for cols in (slice(0, CTX), slice(CTX, TOK)):
                    link(ve.tensor_tensor_scan(pos[:, cols], mask[0:E_N, cols], mask[0:E_N, cols], 0.0, ALU.add, ALU.max))
                link(ve.tensor_tensor(pos[:, :], pos[:, :], mask[0:E_N, :], ALU.mult))
                ve.tensor_scalar(pos[:, :], pos[:, :], -1.0, None, ALU.add).then_inc(pos_done.sem, 1)
                rows_of_h(NB - 1)
                ve.wait_ge(pr_ps.sem, pr_ps.at(l, 1))
                ve.tensor_copy(pos_rows[:, :, 0:E_N], T[:, 0:NB * E_N].rearrange("p (b e) -> p b e", b=NB)).then_inc(pr_sb.sem, 1)

                def choose(u, first):
                    ve.wait_ge(pr_sb.sem, pr_sb.at(l, 1))
                    link(ve.tensor_copy(cur[:, :, :], pos_rows[:, :, first]))
                    for i in range(2):
                        ve.tensor_tensor(pick[:, :, i * CAP:(i + 1) * CAP], iota.unsqueeze(1).broadcast_to([P, 4, CAP]),
                                         cur[:, 1:NB, i].unsqueeze(2).broadcast_to([P, 4, CAP]), ALU.is_equal)
                    ve.tensor_tensor(pickx[:, :].rearrange("p (i c) -> p i c", i=2),
                                     iota[:, 0:CAPX].unsqueeze(1).broadcast_to([P, 2, CAPX]),
                                     cur[:, 0, :].unsqueeze(2).broadcast_to([P, 2, CAPX]), ALU.is_equal)\
                      .then_inc(pick_done.sem, 1)

                def low_lat(u):
                    ve.wait_ge(xl_hi.sem, xl_hi.at(u, 1))
                    ve.tensor_tensor(xs_lo[:, :, :, 0:CAP], U[:, :].rearrange("p (k i c) -> p k i c", k=KD, i=2),
                                     xs_hi[:, :, :, 0:CAP].bitcast(F32), ALU.subtract).then_inc(xl_lo.sem, 1)

                def low_ctx(u):
                    ve.wait_ge(xx_hi.sem, xx_hi.at(u, 1))
                    ve.tensor_tensor(xs_lo[:, :, :, CAP:SLOT_TOK],
                                     S[0][:, 0:KD * 2 * CAPX].rearrange("p (k i c) -> p k i c", k=KD, i=2),
                                     xs_hi[:, :, :, CAP:SLOT_TOK].bitcast(F32), ALU.subtract).then_inc(xx_lo.sem, 1)

                def low_rows(i, half, hi_ready):
                    ve.wait_ge(*hi_ready)
                    cols = slice(half * 512, (half + 1) * 512)
                    ve.tensor_tensor(ye_lo[i * CAP:(i + 1) * CAP, cols], T[0:CAP, cols],
                                     ye_hi[i * CAP:(i + 1) * CAP, cols].bitcast(F32), ALU.subtract)
                    at = i * XROW
                    return ve.tensor_tensor(yex[2 * XROW + at:2 * XROW + at + CAPX, cols], T[CAP:SLOT_TOK, cols],
                                            yex[at:at + CAPX, cols].bitcast(F32), ALU.subtract)

                def add_back(v, n, lat, cx):
                    ve.wait_ge(add_ps.sem, add_ps.at(v, n + 1))
                    residual(n, 5 * KD, lat, cx).then_inc(add_sb.sem, 1)

                u = l * (PAIRS + 1)
                choose(u, slice(0, 2))
                low_lat(u)
                low_ctx(u)
                for zeros in (ye_hi, yex, ye_lo, back, backx):
                    ve.memset(zeros[:, :].bitcast(F32), 0.0)
                ve.memset(T[0:SLOT_TOK, :], 0.0).then_inc(t_clear.sem, 1)
                with ve.Fori(0, PAIRS) as pair:
                    t = l * PAIRS + pair
                    u = l * (PAIRS + 1) + pair + 1
                    ve.sem_clear(step_v)
                    count[0] = 0

                    def low_pieces(g, between={}):
                        for piece in range(PIECES):
                            ve.wait_ge(hi_done.sem, hi_done.at(t, g * PIECES + piece + 1))
                            k = slice(2 * piece, 2 * piece + 2)
                            ve.tensor_tensor(ring_lo[:, g % RING, k, :], ring[:, g % RING, k, :],
                                             w_hi[:, piece, :, :].bitcast(F32), ALU.subtract).then_inc(lo_done.sem, 1)
                            if piece in between:
                                add_back(u - 1, between[piece], T[:, 0:LAT], T[:, 512:512 + CTX])

                    def middle(i, half):
                        ve.wait_ge(silu_done.sem, silu_done.at(t, 2 * i + half + 1))
                        ve.wait_ge(gr_ps.sem, gr_ps.at(t, 4 * i + 2 * half + 2))
                        rows = hm_rows[i][0:SLOT_TOK, half * 512:(half + 1) * 512]
                        ve.scalar_tensor_tensor(out=rows, in0=S[half][0:SLOT_TOK, 512:1024], scalar=gates[:, i:i + 1], in1=rows,
                                                op0=ALU.mult, op1=ALU.mult).then_inc(hm_done.sem, 1)

                    def low_middle(i):
                        ve.wait_ge(hh_done.sem, hh_done.at(t, i + 1))
                        ve.tensor_tensor(hm_lo[:, i, :, :].rearrange("p (b j) c -> p b (j c)", b=2),
                                         U[:, :].rearrange("p (b n) -> p b n", b=2)[:, :, 0:4 * SLOT_TOK],
                                         hm_hi[:, i, :, :].bitcast(F32).rearrange("p (b j) c -> p b (j c)", b=2),
                                         ALU.subtract).then_inc(hl_done.sem, 1)

                    ve.wait_ge(aff_rows.sem, aff_rows.at(l, 1))
                    ve.tensor_copy(cur_gate[:, :, :], lg[:, :, bass.ds(pair * 2, 2)]).then_inc(gate_cols.sem, 1)
                    low_pieces(0)
                    low_rows(1, 0, (ye1_hi.sem, ye1_hi.at(u - 1, 1)))
                    low_rows(1, 1, (ye1_hi.sem, ye1_hi.at(u - 1, 2))).then_inc(rows_done.sem, 1)
                    low_pieces(1)
                    ve.wait_ge(gate_sb.sem, gate_sb.at(t, 1))
                    choose(u, bass.ds(pair * 2 + 2, 2))
                    for copy in range(2):
                        ve.tensor_copy(selx[:, copy, :, :],
                                       ident[0:E_N, bass.ds(pair * 2, 2)].unsqueeze(2).broadcast_to([E_N, 2, XROW]))
                    ve.tensor_copy(sel[:, :, :], ident[0:E_N, bass.ds(pair * 2, 2)].unsqueeze(2).broadcast_to([E_N, 2, CAP]))\
                      .then_inc(sel_done.sem, 1)
                    low_pieces(2, {1: 0, 3: 1})
                    middle(0, 0)
                    low_pieces(3, {2: 2})
                    low_pieces(4, {1: 3})
                    middle(0, 1)
                    low_pieces(5, {1: 4})
                    low_middle(0)
                    low_pieces(6, {1: 5})
                    middle(1, 0)
                    low_pieces(7, {1: 6})
                    low_pieces(8, {0: 7})
                    middle(1, 1)
                    low_lat(u)
                    low_pieces(9)
                    low_middle(1)
                    low_ctx(u)
                    low_rows(0, 0, (ye0_hi.sem, ye0_hi.at(t, 1))).then_inc(ye0_lo.sem, 1)
                    low_pieces(10)
                    low_rows(0, 1, (ye0_hi.sem, ye0_hi.at(t, 2))).then_inc(ye0_lo.sem, 1)
                    low_pieces(11)
                    ve.wait_ge(place_ps.sem, place_ps.at(t, 1))
                    ve.tensor_scalar(back[:, :], U[:, 0:LAT], consts[:, K_SLOT:K_SLOT + 1], None, ALU.is_equal)
                    ve.tensor_scalar(backx[:, :], U[:, 512:512 + CTX], consts[:, K_SLOTX:K_SLOTX + 1], None, ALU.is_equal)\
                      .then_inc(back_done.sem, 1)
                u = l * (PAIRS + 1) + PAIRS
                low_rows(1, 0, (ye1_hi.sem, ye1_hi.at(u, 1)))
                low_rows(1, 1, (ye1_hi.sem, ye1_hi.at(u, 2))).then_inc(rows_done.sem, 1)
                for n in range(KD):
                    add_back(u, n, lat_bank[n % 2], ctx_bank[n % 2][:, 0:CTX])
                ve.wait_ge(add_sb.sem, add_sb.at(u, KD))

            ve.wait_ge(rms_done.sem, rms_done.at(DEPTH, 1))
            for k in range(KD):
                ve.scalar_tensor_tensor(out=hT[:, k, :], in0=xT[:, k, :], scalar=condT[:, 2 * KD + k:2 * KD + k + 1],
                                        in1=rstd[:, :], op0=ALU.mult, op1=ALU.mult).then_inc(xn_done.sem, 1)
            for b in range(NB):
                ve.wait_ge(fin_ps.sem, b + 1)
                ve.tensor_copy(arena[:, b * D:b * D + 512], S[b % 2][:, 0:512]).then_inc(fin_v.sem, 1)


_INS = ["x_prompt", "x_sample", "cache_diff_k", "cache_diff_v", "cache_mla_ckv", "cache_mla_kpe", "c", "c_ctx", "w_ada",
        "b_ada", "g_attn", "g_ffn", "w_in", "w_four", "diff_lambda", "g_subln", "g_mla_q", "w_mla_uq", "g_mla_kv",
        "w_mla_ukv", "w_out", "w_router", "w_e_gate", "w_e_up", "w_e_down", "g_final"]
_OUTS = [("y_prompt", (1, CTX, D)), ("y_sample", (1, LAT, D)), ("new_diff_k", (1, DEPTH, CTX, HEADS, 2 * DH)),
         ("new_diff_v", (1, DEPTH, CTX, HEADS, 2 * DH)), ("new_mla_ckv", (1, DEPTH, CTX, P)),
         ("new_mla_kpe", (1, DEPTH, CTX, ROPE))]


def _rope_tables(dim):
    rows = LAT // GRID_W
    row = np.repeat(np.arange(rows, dtype=np.float32), GRID_W)
    col = np.tile(np.arange(GRID_W, dtype=np.float32), rows)
    nf = dim // 4
    inv = (np.float32(ROPE_BASE) ** (-np.arange(nf, dtype=np.float32) / np.float32(nf))).astype(np.float32)
    ang = np.concatenate([row[:, None] * inv, col[:, None] * inv], axis=-1)
    return np.cos(ang).astype(np.float32).T, np.sin(ang).astype(np.float32).T


def _constants():
    c = np.zeros((P, K_W), np.float32)
    c[:, K_ID:K_ID + P] = np.eye(P)
    def rot(m, at, half):
        for i in range(half):
            m[at + half + i, at + i] = -1.0
            m[at + i, at + half + i] = 1.0
    rot(c[:, K_ROTD:K_ROTD + P], 0, DH // 2)
    rot(c[:, K_ROTD:K_ROTD + P], DH, DH // 2)
    rot(c[:, K_ROTM:K_ROTM + QM], NOPE, ROPE // 2)
    cos, sin = _rope_tables(DH)
    c[:, K_ROPED:K_ROPED + LAT] = np.tile(cos, (4, 1))
    c[:, K_ROPED + LAT:K_ROPED + 2 * LAT] = np.tile(sin, (4, 1))
    cos, sin = _rope_tables(ROPE)
    c[0:NOPE, K_ROPEM:K_ROPEM + LAT] = 1.0
    c[NOPE:QM, K_ROPEM:K_ROPEM + LAT] = np.tile(cos, (2, 1))
    c[NOPE:QM, K_ROPEM + LAT:K_ROPEM + 2 * LAT] = np.tile(sin, (2, 1))

    def dft(n):
        turn = 2.0 * np.pi * (np.outer(np.arange(n), np.arange(n)) % n) / n
        return np.cos(turn) / np.sqrt(n), np.sin(turn) / np.sqrt(n)

    for part, m in enumerate(dft(F_CH)):
        for j in range(2):
            c[j * F_CH:(j + 1) * F_CH, K_CHAN + part * P + j * F_CH:K_CHAN + part * P + (j + 1) * F_CH] = m
    co, si = dft(CTX)
    c[:, K_SEQX:K_SEQX + CTX], c[:, K_SEQX + CTX:K_SEQX + 2 * CTX] = co, -si
    c[:, K_IOTA:K_IOTA + CAP] = np.arange(CAP)
    c[:, K_SLOT] = np.arange(P) % CAP
    c[:, K_SLOTX] = np.arange(P) % XROW
    c[:, K_FOLD:K_FOLD + 2] = np.arange(P)[:, None] % 32 == np.arange(2)[None, :]
    c[:, K_EPS] = EPS
    co, si = dft(LAT)
    seq = np.concatenate([co, -si]).astype(np.float32)
    init = 0.8 - 0.6 * np.exp(-0.3 * np.arange(DEPTH))
    lam = np.stack([init, 1.0 - init], axis=1).astype(np.float32)
    return c, seq, lam


def kernel(**inputs):
    import concourse.bacc as bacc
    from concourse.bass_utils import run_bass_kernel_spmd

    nc = bacc.Bacc("TRN2", target_bir_lowering=False, num_devices=1)
    arrays, aps = {}, {}
    consts, seq, lam = _constants()
    given = [(n, inputs[n]) for n in _INS] + [("consts", consts), ("dft", seq), ("lam_init", lam)]
    for name, value in given:
        v = np.ascontiguousarray(value)
        arrays[f"in_{name}_dram"] = v
        aps[name] = nc.dram_tensor(f"in_{name}_dram", v.shape, mybir.dt.from_np(v.dtype), kind="ExternalInput").ap()
    for name, shape in _OUTS:
        aps[name] = nc.dram_tensor(f"out_{name}_dram", shape, F32, kind="ExternalOutput").ap()
    build(nc, aps)
    r = run_bass_kernel_spmd(nc, [arrays], core_ids=[0])
    return tuple(r.results[0][f"out_{name}_dram"] for name, _ in _OUTS)
```

```python
from contextlib import ExitStack

import numpy as np

import concourse.bass as bass
from concourse import mybir

F32 = mybir.dt.float32
F32R = mybir.dt.float32r
ALU = mybir.AluOpType
ACT = mybir.ActivationFunctionType
AX = mybir.AxisListType

P = 128
D = 1024
KD = D // P
DEPTH = 2
CTX, LAT, PAST = 128, 512, 128
TOK = CTX + LAT
NB = TOK // P
KEYS = LAT + PAST
GRID_W = 64
ROPE_BASE = 10000.0
EPS = 1e-6
HEADS = 4
DH = 64
NOPE, ROPE, VDIM = 64, 32, 64
QM = NOPE + ROPE
F_CH = 64
E_N = 16
PAIRS = E_N // 2
CAP = 2 * LAT // E_N
CAPX = 2 * CTX // E_N
SLOT_TOK = CAP + CAPX
N_MOD = 6
N_VEC = N_MOD * KD + 2 * KD + 2 + 1 + 1
DIFF_SCALE = float(DH) ** -0.5
MLA_SCALE = float(QM) ** -0.5

C_F, C_Q, C_K, C_V, C_CQ, C_CKV, C_KPE, C_END = 0, 256, 768, 1280, 1792, 2048, 2176, 2208

RING = 4
ADA_CHUNKS = 12
CH_MLA, CH_Q, CH_K, CH_V, CH_F, CH_DFT, CH_OUT = 12, 13, 14, 15, 16, 17, 18
DENSE_CHUNKS = 20
PAIR_CHUNKS = 12
LAYER_CHUNKS = DENSE_CHUNKS + PAIRS * PAIR_CHUNKS
assert LAYER_CHUNKS % RING == 0 and DENSE_CHUNKS % RING == 0 and PAIR_CHUNKS % RING == 0

K_ID, K_ROTD, K_ROTM = 0, 128, 256
K_ROPED = K_ROTM + QM
K_ROPEM = K_ROPED + 2 * LAT
K_CHAN = K_ROPEM + 2 * LAT
K_SEQX = K_CHAN + 2 * P
K_IOTA = K_SEQX + 2 * CTX
K_SLOT = K_IOTA + CAP
K_SLOTX = K_SLOT + 1
K_EPS = K_SLOTX + 1
K_FOLD = K_EPS + 1
K_W = K_FOLD + E_N

GATE, UP, DOWN = range(3)
GROUPS_OF_PAIR = [(0, GATE, 0), (0, UP, 0), (0, GATE, 1), (0, UP, 1),
                  (1, GATE, 0), (1, UP, 0), (1, GATE, 1), (1, UP, 1),
                  (0, DOWN, 0), (0, DOWN, 1), (1, DOWN, 0), (1, DOWN, 1)]
PIECES = 4
ON_GPSIMD = [(g, 2) for g in (1, 2, 3, 4, 5, 7, 8, 9, 10)]
ON_VECTOR = [(g, p) for g in range(len(GROUPS_OF_PAIR)) for p in range(PIECES) if (g, p) not in ON_GPSIMD]
YE_AT = 5664
SPLIT_AT = 10144
ARENA = SPLIT_AT + 4 * KD * 2 * SLOT_TOK
XROW = 32

UNITS = 22
ROPES = 13
ATT_IT = HEADS * NB
GROUPS = 3 * ATT_IT
VECS, SMALL = 6, 13
OUTS = 4


class Signal:

    def __init__(self, sem, per, setup=0, step=1):
        self.sem, self.per, self.setup, self.step = sem, per, setup, step

    def at(self, turn, k):
        return turn * (self.per * self.step) + (self.setup + k) * self.step


def build(nc, a):
    ctx = ExitStack()
    with ctx:
        def sb(name, shape):
            return ctx.enter_context(nc.sbuf_tensor(name, shape, F32))

        def signal(name, per, setup=0, step=1):
            return Signal(ctx.enter_context(nc.semaphore(name)), per, setup, step)

        def reused(first, *later):
            for name, shape, dt in (first, *later):
                with nc.sbuf_tensor(name, shape, dt) as t:
                    yield t

        xT = sb("xT", [P, KD, TOK])
        consts = sb("consts", [P, K_W])
        ones = sb("ones", [P, P])
        scr = sb("scr", [P, 2, TOK])
        rstd, back = reused(("rstd", [P, TOK], F32), ("back", [P, LAT], F32R))
        ctx.enter_context(nc.sbuf_tensor("rstd_place", [P, TOK], F32))
        rope_a = sb("rope_a", [P, 2, LAT])
        vec_rows = sb("vec_rows", [N_VEC, P])
        vecT = sb("vecT", [P, N_VEC])
        mod = sb("mod", [P, N_MOD * KD, 2])
        gain = sb("gain", [P, 2, KD, 2])
        condT = sb("condT", [P, 3 * KD])
        condP = sb("condP", [P, KD, 32])
        wuq = sb("wuq", [P, 2, HEADS * QM])
        wukv = sb("wukv", [P, HEADS * (NOPE + VDIM)])
        wfour = sb("wfour", [P, 2, P])
        wrt = sb("wrt", [P, KD, 32])
        dlam = sb("dlam", [P, 4, DH])
        lamt = sb("lamt", [P, 2])
        lamw = sb("lamw", [P, 4])
        gsub = sb("gsub", [P, 1])
        cache_k = sb("cache_k", [P, HEADS * P])
        cache_v = sb("cache_v", [P, HEADS * P])
        cache_ckv = sb("cache_ckv", [P, P])
        cache_kpe = sb("cache_kpe", [P, QM])
        chanw = sb("chanw", [P, 2, 2, P])
        k_rows = sb("k_rows", [P, HEADS * P])
        smax = sb("smax", [P, 2])
        negm = sb("negm", [P, 2])
        ssum = sb("ssum", [P, 3, 2])
        srec = sb("srec", [P, 3, 2])
        lg = sb("lg", [P, NB, E_N])
        lmax = sb("lmax", [P, NB])
        top8 = sb("top8", [E_N, 8])
        pos_rows = sb("pos_rows", [P, NB, E_N + 2])
        cur = sb("cur", [P, NB, 2])
        cur_gate = sb("cur_gate", [P, NB, 2])
        gates = sb("gates", [SLOT_TOK, 2])

        ring, ring_lo = reused(("ring", [P, RING, KD, 512], F32), ("ring_lo", [P, RING, KD, 512], F32R))
        ctx.enter_context(nc.sbuf_tensor("ring_place", [P, RING, KD, 512], F32))
        hT, w_hi = reused(("hT", [P, KD, TOK], F32), ("w_hi", [P, PIECES, 2, 512], F32R))
        w_hi_size = PIECES * 2 * 512
        ctx.enter_context(nc.sbuf_tensor("w_hi_place", [P, w_hi_size], F32))
        sel = ctx.enter_context(nc.sbuf_tensor("sel", [E_N, 2, CAP], F32R))
        selx = ctx.enter_context(nc.sbuf_tensor("selx", [E_N, 2, 2, XROW], F32R))
        ctx.enter_context(nc.sbuf_tensor("hT_rest", [P, KD * TOK - w_hi_size - 2 * CAP - 4 * XROW], F32))
        with nc.sbuf_tensor("arena", [P, ARENA], F32) as arena:
            pass
        ctx.enter_context(nc.sbuf_tensor("arena_front", [P, YE_AT], F32))
        ye_hi, yex, ye_lo = (ctx.enter_context(nc.sbuf_tensor(n, [P, D], F32R)) for n in ("ye_hi", "yex", "ye_lo"))
        backx = ctx.enter_context(nc.sbuf_tensor("backx", [P, CTX], F32R))
        ctx.enter_context(nc.sbuf_tensor("logits_place", [P, TOK], F32))
        pos = ctx.enter_context(nc.sbuf_tensor("pos", [P, TOK], F32R))
        pos = pos[0:E_N, :]
        xs_hi, xs_lo = (ctx.enter_context(nc.sbuf_tensor(n, [P, KD, 2, SLOT_TOK], F32R)) for n in ("xs_hi", "xs_lo"))
        hm_hi, hm_lo = (ctx.enter_context(nc.sbuf_tensor(n, [P, 2, KD, SLOT_TOK], F32R)) for n in ("hm_hi", "hm_lo"))

        def region(at, *dims):
            n = int(np.prod(dims))
            v = arena[:, at:at + n]
            if len(dims) == 2:
                v = v.rearrange("p (a b) -> p a b", a=dims[0])
            if len(dims) == 3:
                v = v.rearrange("p (a b c) -> p a b c", a=dims[0], b=dims[1])
            return v

        qT = region(0, HEADS, TOK)
        kT = region(2560, HEADS, CTX + KEYS)
        v_rows = region(5632, NB, HEADS * P)
        vm_rows = region(5632, NB + 1, HEADS * VDIM)
        ckvT = region(8192, CTX + KEYS)
        kpeT = region(8960, CTX + KEYS)
        y_mla = region(9728, 2, TOK)
        probs = [region(11008, 2, TOK), region(11008 + 2 * TOK, 2, TOK), scr]
        cqT = region(11008, 2, TOK)
        chan_rows = region(11008, NB, 2, 2 * P)
        probsT = region(13568, 2, NB, P)
        zfT = region(13568, 2, TOK)
        ckv_rows = region(14848, P)
        kpe_rows = region(14976, ROPE)
        dprod = region(15008, 2, DH)
        sub_squares = region(0, HEADS, TOK)
        sub_rstd = region(11008, HEADS * TOK)
        sub_lat, sub_ctx = [0, 512, 1024, 2048], [1536 + h * CTX for h in range(HEADS)]
        ada_rows = region(0, 2, 512)
        yT = hT
        h_rows = region(0, NB, D)
        pick = region(5120, 4, 2 * CAP)
        pickx = region(5632, 2 * CAPX)
        hm_rows = [scr[:, :, :].rearrange("p a b -> p (a b)")[:, 0:D], rope_a[:, :, :].rearrange("p a b -> p (a b)")]
        logit_parts = region(8864, TOK)
        rank = region(9504, TOK)[0:E_N, :]
        work = region(SPLIT_AT, TOK)
        mask = region(SPLIT_AT + TOK, TOK)
        cond_rows = region(0, P)[0:3 * KD, :]
        cond_e = region(P, P)[0:2 * KD, :]
        x_rows = hT[:, :, :].rearrange("p a b -> p (a b)").rearrange("p (b d) -> p b d", b=NB)

        ident = consts[:, K_ID:K_ID + P]
        rot_diff = consts[:, K_ROTD:K_ROTD + P]
        rot_mla = consts[:, K_ROTM:K_ROTM + QM]
        cos_d, sin_d = consts[:, K_ROPED:K_ROPED + LAT], consts[:, K_ROPED + LAT:K_ROPED + 2 * LAT]
        cos_m, sin_m = consts[:, K_ROPEM:K_ROPEM + LAT], consts[:, K_ROPEM + LAT:K_ROPEM + 2 * LAT]
        iota = consts[:, K_IOTA:K_IOTA + CAP]
        eps = consts[:, K_EPS:K_EPS + 1]

        S = [ctx.enter_context(nc.psum_tensor(f"S{i}", [P, 1024], F32)) for i in range(2)]
        T = ctx.enter_context(nc.psum_tensor("T", [P, 1024], F32))
        U = ctx.enter_context(nc.psum_tensor("U", [P, 1024], F32))
        lat_bank = [T[:, 0:512], T[:, 512:1024]]
        ctx_bank = [U[:, 0:512], U[:, 512:1024]]
        sum_lat, sum_ctx = S[0][:, 0:512], S[0][:, 512:512 + CTX]
        rot_bank = S[1][:, 0:512]
        misc_bank = S[1][:, 512:1024]

        const_in = signal("const_in", 0, 4, 16)
        x_in = signal("x_in", 0, 2, 16)
        fill_done = signal("fill_done", 0, 6)
        xt_ps, xt_sb = signal("xt_ps", 0, KD), signal("xt_sb", 0, KD)
        cond_exp, cond_silu = signal("cond_exp", 0, 1), signal("cond_silu", 0, 1)
        cond_ps, cond_sb = signal("cond_ps", 0, 1), signal("cond_sb", 0, 1)
        slot_in = [signal(f"slot_in{i}", LAYER_CHUNKS // RING, 0, 16) for i in range(RING)]
        vec_in, small_in = signal("vec_in", VECS, 0, 16), signal("small_in", SMALL, 0, 16)
        vec_ps, vec_sb = signal("vec_ps", 1), signal("vec_sb", 1)
        adar_ps, adar_sb = signal("adar_ps", ADA_CHUNKS), signal("adar_sb", ADA_CHUNKS)
        ada_ps, ada_sb = signal("ada_ps", ADA_CHUNKS), signal("ada_sb", ADA_CHUNKS)
        gain_sb = signal("gain_sb", 1)
        sq_done, sq_added = signal("sq_done", 2 * KD), signal("sq_added", 2 * KD)
        sum_ps, rms_done = signal("sum_ps", 2), signal("rms_done", 2)
        xn_done, h_done = signal("xn_done", 2 * KD), signal("h_done", 2 * KD)
        unit_ps = signal("unit_ps", UNITS)
        unit_lat, unit_ctx = signal("unit_lat", UNITS), signal("unit_ctx", UNITS)
        rope_ps, rope_sb = signal("rope_ps", ROPES), signal("rope_sb", ROPES)
        nsq_done, nsum_ps = signal("nsq_done", 3), signal("nsum_ps", 2)
        nrms_done, nscaled = signal("nrms_done", 2), signal("nscaled", 2)
        sub_sq, sub_ps, sub_ln = signal("sub_sq", HEADS), signal("sub_ps", HEADS), signal("sub_ln", 2)
        sub_rms, sub_scaled = signal("sub_rms", 2), signal("sub_scaled", HEADS)
        tr_ps, tr_sb = signal("tr_ps", 4), signal("tr_sb", 4)
        kpe_spread = signal("kpe_spread", 1)
        vm_ps, vm_sb = signal("vm_ps", NB + 1), signal("vm_sb", NB + 1)
        v_ps, v_sb = signal("v_ps", NB), signal("v_sb", NB)
        sc_ps, negm_done, exp_done = signal("sc_ps", GROUPS), signal("negm_done", GROUPS), signal("exp_done", GROUPS)
        probs_done = signal("probs_done", 2 * ATT_IT)
        pt_ps, pt_sb = signal("pt_ps", 2 * ATT_IT), signal("pt_sb", 2 * ATT_IT)
        o_ps, o_sb = signal("o_ps", 2 * ATT_IT), signal("o_sb", 2 * ATT_IT)
        lam_prod, lam_exp, lam_done = signal("lam_prod", 1), signal("lam_exp", 1), signal("lam_done", 1)
        cw_ps, cw_sb = signal("cw_ps", 2), signal("cw_sb", 2)
        fa_ps, fa_sb = signal("fa_ps", NB), signal("fa_sb", NB)
        fb_ps, fb_sb = signal("fb_ps", 2), signal("fb_sb", 2)
        mix_ps, mix_sb = signal("mix_ps", KD), signal("mix_sb", KD)
        outs_done = signal("outs_done", OUTS, 0, 16)
        parts_ps, parts_sb = signal("parts_ps", 1), signal("parts_sb", 1)
        lg_ps, lg_shift, lg_exp, aff_rows = (signal(n, 1) for n in ("lg_ps", "lg_shift", "lg_exp", "aff_rows"))
        aff_ps, pos_done, pr_ps = (signal(n, 1) for n in ("aff_ps", "pos_done", "pr_ps"))
        pr_sb = signal("pr_sb", 1, 1)
        hr_ps, hr_v, hr_a = signal("hr_ps", NB), signal("hr_v", 2), signal("hr_a", NB)
        pick_done, gl_ps, gx_ps = (signal(n, 1) for n in ("pick_done", "gl_ps", "gx_ps"))
        xl_hi, xl_lo, xx_hi, xx_lo = (signal(n, 1) for n in ("xl_hi", "xl_lo", "xx_hi", "xx_lo"))
        gate_cols, gate_ps, gate_sb = (signal(n, 1) for n in ("gate_cols", "gate_ps", "gate_sb"))
        sel_done, place_ps = (signal(n, 1) for n in ("sel_done", "place_ps"))
        back_done = signal("back_done", 1, 1)
        hi_done = signal("hi_done", 12 * PIECES)
        lo_done, lo_done_g = signal("lo_done", len(ON_VECTOR)), signal("lo_done_g", len(ON_GPSIMD))
        piece_ps = signal("piece_ps", 12 * (PIECES - 1), PIECES - 1)
        gr_ps = signal("gr_ps", 12, RING)
        silu_done, hm_done = signal("silu_done", 4), signal("hm_done", 4)
        th_ps, hh_done, hl_done = signal("th_ps", 2), signal("hh_done", 2), signal("hl_done", 2)
        t_clear = signal("t_clear", 1)
        ye0_hi, ye0_lo = signal("ye0_hi", 2), signal("ye0_lo", 2)
        ye1_hi, rows_done = signal("ye1_hi", 2), signal("rows_done", 1)
        add_ps, add_sb = signal("add_ps", KD), signal("add_sb", KD, 1)
        fin_ps, fin_v, fin_a = signal("fin_ps", NB), signal("fin_v", NB), signal("fin_a", NB)
        y_out = signal("y_out", 2, 0, 16)
        step_v = ctx.enter_context(nc.semaphore("step_v"))
        step_a = signal("step_a", 4)

        block = ctx.enter_context(nc.Block())

        @block.sync
        def _(sp):
            sp.dma_start(consts[:, :], a["consts"]).then_inc(const_in.sem, 16)
            sp.dma_start(cond_rows[0:KD, :], a["c_ctx"].rearrange("(k p) -> k p", p=P)).then_inc(const_in.sem, 16)
            sp.dma_start(cond_rows[KD:2 * KD, :], a["c"].rearrange("b (k p) -> (b k) p", p=P)).then_inc(const_in.sem, 16)
            sp.dma_start(cond_rows[2 * KD:3 * KD, :], a["g_final"].rearrange("(k p) -> k p", p=P)).then_inc(const_in.sem, 16)
            sp.dma_start(x_rows[:, 0, :], a["x_prompt"].rearrange("b n d -> (b n) d")).then_inc(x_in.sem, 16)
            sp.dma_start(x_rows[:, 1:NB, :], a["x_sample"].rearrange("b (j p) d -> p (b j) d", p=P)).then_inc(x_in.sem, 16)

            sp.wait_ge(fill_done.sem, 6)
            with sp.Fori(0, DEPTH) as l:
                def vec(dst, src):
                    sp.dma_start(dst, src).then_inc(vec_in.sem, 16)

                def small(dst, src):
                    sp.dma_start(dst, src).then_inc(small_in.sem, 16)

                sp.wait_ge(pr_sb.sem, pr_sb.at(l, 0))
                r = N_MOD * KD
                vec(vec_rows[0:r, :], a["b_ada"][l].rearrange("(k p) -> k p", p=P))
                vec(vec_rows[r:r + KD, :], a["g_attn"][l].rearrange("(k p) -> k p", p=P))
                vec(vec_rows[r + KD:r + 2 * KD, :], a["g_ffn"][l].rearrange("(k p) -> k p", p=P))
                r += 2 * KD
                vec(vec_rows[r:r + 2, :], a["g_mla_q"][l].rearrange("(k p) -> k p", p=P))
                vec(vec_rows[r + 2:r + 3, :], a["g_mla_kv"][l].rearrange("(k p) -> k p", p=P))
                vec(vec_rows[r + 3:r + 4, :], a["g_subln"][l].rearrange("(k p) -> k p", p=P))

                def load(i, src, last_read):
                    if last_read:
                        done, value = last_read
                        sp.wait_ge(done.sem, value)
                    rows = src.rearrange("(k p) n -> p k n", p=P)
                    n = rows.shape[2]
                    sp.dma_start(ring[:, i % RING, :, 0:n], rows).then_inc(slot_in[i % RING].sem, 16)

                def dense_read(c):
                    if c < ADA_CHUNKS:
                        return adar_ps, adar_ps.at(l, c + 1)
                    return {CH_MLA: (unit_ps, unit_ps.at(l, 4)), CH_Q: (unit_ps, unit_ps.at(l, 16)),
                            CH_K: (unit_ps, unit_ps.at(l, 20)), CH_V: (v_ps, v_ps.at(l, NB)),
                            CH_F: (unit_ps, unit_ps.at(l, UNITS)), CH_DFT: (fb_ps, fb_ps.at(l, 2)),
                            CH_OUT: (mix_ps, mix_ps.at(l, 4)), CH_OUT + 1: (mix_ps, mix_ps.at(l, KD))}[c]

                def pair_read(t, j):
                    return gr_ps, gr_ps.at(t, j + 1)

                def dense(c, src):
                    load(c, src, dense_read(c - RING) if c >= RING else pair_read(l * PAIRS, c - RING))

                def small_weights():
                    small(dlam[:, :, :], a["diff_lambda"][l].partition_broadcast(P))
                    small(lamt[:, :], a["lam_init"][l].partition_broadcast(P))
                    small(wuq[:, :, :], a["w_mla_uq"][l].rearrange("(k p) n -> p k n", p=P))
                    small(wukv[:, :], a["w_mla_ukv"][l])
                    small(cache_ckv[:, :], a["cache_mla_ckv"][0, l])
                    small(cache_kpe[:, NOPE:QM], a["cache_mla_kpe"][0, l])
                    small(cache_k[:, :], a["cache_diff_k"][0, l].rearrange("t h d -> t (h d)"))
                    small(cache_v[:, :], a["cache_diff_v"][0, l].rearrange("t h d -> t (h d)"))
                    for j in range(4):
                        half = (j % 2) * F_CH
                        small(wfour[half:half + F_CH, j // 2, half:half + F_CH], a["w_four"][l, j])
                    small(wrt[:, :, 0:E_N], a["w_router"][l].rearrange("(k p) e -> p k e", p=P))

                for c in range(ADA_CHUNKS):
                    dense(c, a["w_ada"][l, :, c * 512:(c + 1) * 512])
                dense(CH_MLA, a["w_in"][l, :, C_CQ:C_END])
                small_weights()
                dense(CH_Q, a["w_in"][l, :, C_Q:C_K])
                dense(CH_K, a["w_in"][l, :, C_K:C_V])
                load(CH_V, a["w_in"][l, :, C_V:C_CQ], dense_read(CH_MLA))
                load(CH_F, a["w_in"][l, :, C_F:C_Q], None)
                dense(CH_DFT, a["dft"])
                for c in range(2):
                    dense(CH_OUT + c, a["w_out"][l, :, c * 512:(c + 1) * 512])

                def expert_piece(pair, j):
                    later, j = divmod(j, PAIR_CHUNKS)
                    i, matrix, half = GROUPS_OF_PAIR[j]
                    name = ("w_e_gate", "w_e_up", "w_e_down")[matrix]
                    return a[name][l, pair * 2 + (2 * later + i), :, half * 512:(half + 1) * 512]

                for j in range(RING):
                    load(j, expert_piece(0, j), dense_read(DENSE_CHUNKS + j - RING))
                with sp.Fori(0, PAIRS - 1) as pair:
                    for j in range(RING, RING + PAIR_CHUNKS):
                        load(j, expert_piece(pair, j), pair_read(l * PAIRS + pair, j - RING))
                for j in range(RING, PAIR_CHUNKS):
                    load(j, expert_piece(PAIRS - 1, j), pair_read(l * PAIRS + PAIRS - 1, j - RING))

            sp.wait_ge(fin_v.sem, NB)
            sp.wait_ge(fin_a.sem, NB)
            out_rows = arena[:, 0:NB * D].rearrange("p (b d) -> p b d", b=NB)
            sp.dma_start(a["y_prompt"].rearrange("b n d -> (b n) d"), out_rows[:, 0, :]).then_inc(y_out.sem, 16)
            sp.dma_start(a["y_sample"].rearrange("b (j p) d -> p (b j) d", p=P), out_rows[:, 1:NB, :]).then_inc(y_out.sem, 16)
            sp.wait_ge(y_out.sem, y_out.at(1, 0))

        @block.gpsimd
        def _(g):
            g.memset(ones[:, :], 1.0).then_inc(fill_done.sem, 1)
            g.memset(wfour[:, :, :], 0.0).then_inc(fill_done.sem, 1)
            g.memset(cache_kpe[:, :], 0.0).then_inc(fill_done.sem, 1)
            g.memset(wrt[:, :, :], 0.0).then_inc(fill_done.sem, 1)
            g.memset(condP[:, :, :], 0.0).then_inc(fill_done.sem, 1)
            g.memset(pos_rows[:, :, E_N:E_N + 2], -1.0).then_inc(fill_done.sem, 1)
            with g.Fori(0, DEPTH) as l:
                with g.Fori(0, PAIRS) as pair:
                    t = l * PAIRS + pair
                    for group, piece in ON_GPSIMD:
                        g.wait_ge(hi_done.sem, hi_done.at(t, group * PIECES + piece + 1))
                        k = slice(2 * piece, 2 * piece + 2)
                        g.tensor_tensor(ring_lo[:, group % RING, k, :], ring[:, group % RING, k, :],
                                        w_hi[:, piece, :, :].bitcast(F32), ALU.subtract).then_inc(lo_done_g.sem, 1)

        def iterations(kind):
            return [(kind, h, b) for h in range(HEADS) for b in range(NB)]

        ITS = iterations("mla") + iterations("diff")

        def groups(it):
            if it < ATT_IT:
                return [it]
            return [ATT_IT + 2 * (it - ATT_IT), ATT_IT + 2 * (it - ATT_IT) + 1]

        def key_cols(b):
            return (0, CTX) if b == 0 else (CTX, KEYS)

        @block.tensor
        def _(pe):
            pe.wait_ge(const_in.sem, const_in.at(0, 0))
            pe.wait_ge(fill_done.sem, 5)
            pe.wait_ge(x_in.sem, x_in.at(0, 0))
            pe.sem_inc(gr_ps.sem, RING)
            pe.sem_inc(piece_ps.sem, PIECES - 1)
            for k in range(KD):
                if k >= 2:
                    pe.wait_ge(xt_sb.sem, k - 1)
                for b in range(NB):
                    dst = ctx_bank[k % 2][:, 0:P] if b == 0 else lat_bank[k % 2][:, (b - 1) * P:b * P]
                    mm = pe.transpose(dst, x_rows[:, b, k * P:(k + 1) * P], ident)
                mm.then_inc(xt_ps.sem, 1)
            pe.wait_ge(cond_silu.sem, 1)
            pe.transpose(misc_bank[:, 0:3 * KD], cond_rows[:, :], ident[0:3 * KD, 0:3 * KD]).then_inc(cond_ps.sem, 1)
            pe.wait_ge(cond_sb.sem, 1)
            pe.wait_ge(xt_sb.sem, KD)

            def slot(turn, i):
                pe.wait_ge(slot_in[i % RING].sem, turn + (i // RING) * 16 + 16)
                return ring[:, i % RING, :, :]

            def product(lat, ctx_out, weights, rhs, steps):
                for k in range(steps):
                    w = weights(k)
                    x = rhs(k)
                    flags = dict(start=(k == 0), stop=(k == steps - 1))
                    pe.matmul(lat, w, x[:, CTX:TOK], **flags)
                    mm = pe.matmul(ctx_out, w, x[:, 0:CTX], **flags)
                return mm

            def wide_norm(l, which):
                pe.wait_ge(sq_added.sem, sq_added.at(l, (which + 1) * KD))
                pe.matmul(sum_lat, ones[:, :], rstd[:, CTX:TOK], start=True, stop=True)
                pe.matmul(sum_ctx, ones[:, :], rstd[:, 0:CTX], start=True, stop=True).then_inc(sum_ps.sem, 1)

            with pe.Fori(0, DEPTH) as l:
                turn = l * (LAYER_CHUNKS // RING * 16)

                pe.wait_ge(vec_in.sem, vec_in.at(l + 1, 0))
                pe.transpose(misc_bank[:, 0:N_VEC], vec_rows[:, :], ident[0:N_VEC, 0:N_VEC]).then_inc(vec_ps.sem, 1)

                def fold(c):
                    pe.wait_ge(adar_sb.sem, adar_sb.at(l, c + 1))
                    if c >= 2:
                        pe.wait_ge(ada_sb.sem, ada_sb.at(l, c - 1))
                    for m in range(4):
                        mm = pe.matmul(ctx_bank[c % 2][:, 2 * m:2 * m + 2], ada_rows[:, c % 2, m * P:(m + 1) * P],
                                       consts[:, K_FOLD:K_FOLD + 2], start=True, stop=True)
                    mm.then_inc(ada_ps.sem, 1)

                for c in range(ADA_CHUNKS):
                    w = slot(turn, c)
                    if c >= 2:
                        pe.wait_ge(adar_sb.sem, adar_sb.at(l, c - 1))
                    for k in range(KD):
                        q = 32 * (k % 4)
                        mm = pe.matmul(lat_bank[c % 2][q:q + 32, :], condP[:, k, :], w[:, k, :],
                                       start=(k < 4), stop=(k >= 4))
                    mm.then_inc(adar_ps.sem, 1)
                    if c >= 1:
                        fold(c - 1)
                    if c == 3:
                        wide_norm(l, 0)
                fold(ADA_CHUNKS - 1)
                pe.wait_ge(ada_sb.sem, ada_sb.at(l, ADA_CHUNKS))

                def unit_banks(u):
                    if u >= 2:
                        pe.wait_ge(unit_lat.sem, unit_lat.at(l, u - 1))
                        pe.wait_ge(unit_ctx.sem, unit_ctx.at(l, u - 1))
                    return lat_bank[u % 2], ctx_bank[u % 2][:, 0:CTX]

                def turn_pairs(r, rows, unit):
                    pe.wait_ge(unit_lat.sem, unit_lat.at(l, unit + 1))
                    if r >= 1:
                        pe.wait_ge(rope_sb.sem, rope_sb.at(l, r))
                    m = rot_diff if rows == slice(0, P) else rot_mla
                    pe.matmul(rot_bank[rows, :], m[rows, rows], rope_a[rows, r % 2, :], start=True, stop=True)\
                      .then_inc(rope_ps.sem, 1)

                w = slot(turn, CH_MLA)

                def normalised(k):
                    pe.wait_ge(h_done.sem, h_done.at(l, k + 1))
                    return hT[:, k, :]

                for u, c0, m in ((0, 0, P), (1, P, P), (2, 2 * P, P), (3, C_END - C_CQ - QM, QM)):
                    lat, cx = unit_banks(u)
                    product(lat[0:m, :], cx[0:m, :], lambda k: w[:, k, c0:c0 + m],
                            normalised if u == 0 else lambda k: hT[:, k, :], KD)\
                        .then_inc(unit_ps.sem, 1)

                def narrow_sum(n, first_sq, blocks):
                    for j in range(blocks):
                        pe.wait_ge(nsq_done.sem, nsq_done.at(l, first_sq + j + 1))
                        flags = dict(start=(j == 0), stop=(j == blocks - 1))
                        s = (first_sq + j) % 2
                        pe.matmul(sum_lat, ones[:, :], scr[:, s, CTX:TOK], **flags)
                        mm = pe.matmul(sum_ctx, ones[:, :], scr[:, s, 0:CTX], **flags)
                    mm.then_inc(nsum_ps.sem, 1)

                narrow_sum(0, 0, 2)
                pe.wait_ge(small_in.sem, small_in.at(l + 1, 0))
                pe.wait_ge(unit_lat.sem, unit_lat.at(l, 4))
                pe.transpose(misc_bank[:, 0:P], cache_ckv[:, :], ident)
                pe.transpose(misc_bank[0:QM, P:2 * P], cache_kpe[:, :], ident).then_inc(tr_ps.sem, 1)
                kpe_at = slice(NOPE, QM)
                pe.matmul(rot_bank[kpe_at, :], rot_mla[kpe_at, kpe_at], rope_a[kpe_at, 0, :], start=True, stop=True)\
                  .then_inc(rope_ps.sem, 1)
                pe.wait_ge(nrms_done.sem, nrms_done.at(l, 1))
                narrow_sum(1, 2, 1)

                pe.wait_ge(nscaled.sem, nscaled.at(l, 1))
                for h in range(HEADS):
                    u = 4 + h
                    lat, cx = unit_banks(u)
                    product(lat[0:QM, :], cx[0:QM, :], lambda k: wuq[:, k, h * QM:(h + 1) * QM], lambda k: cqT[:, k, :], 2)\
                        .then_inc(unit_ps.sem, 1)
                    if h >= 1:
                        turn_pairs(h, slice(0, QM), u - 1)
                pe.wait_ge(nscaled.sem, nscaled.at(l, 2))
                pe.wait_ge(tr_sb.sem, tr_sb.at(l, 1))
                for h in range(HEADS):
                    u = 8 + h
                    lat, _ = unit_banks(u)
                    w0 = wukv[:, h * (NOPE + VDIM):h * (NOPE + VDIM) + NOPE]
                    pe.matmul(lat[0:NOPE, :], w0, ckvT[:, 0:512], start=True, stop=True)
                    pe.matmul(ctx_bank[u % 2][0:NOPE, 0:256], w0, ckvT[:, 512:768], start=True, stop=True)\
                      .then_inc(unit_ps.sem, 1)
                    if h == 0:
                        turn_pairs(4, slice(0, QM), u - 1)
                wv = wukv[:, :].rearrange("p (h c) -> p h c", h=HEADS)[:, :, NOPE:NOPE + VDIM]
                for b in range(NB + 1):
                    if b >= 2:
                        pe.wait_ge(vm_sb.sem, vm_sb.at(l, b - 1))
                    dst = S[0][:, (b % 2) * 512:(b % 2) * 512 + HEADS * VDIM]
                    if b == 0:
                        pe.wait_ge(nrms_done.sem, nrms_done.at(l, 2))
                    pe.matmul(dst, ckvT[:, b * P:(b + 1) * P], wv, start=True, stop=True).then_inc(vm_ps.sem, 1)
                pe.wait_ge(kpe_spread.sem, kpe_spread.at(l, 1))
                pe.transpose(misc_bank[:, 0:P], ckvT[:, 0:P], ident)
                pe.transpose(misc_bank[:, P:P + ROPE], kpeT[NOPE:QM, 0:P], ident[NOPE:QM, NOPE:QM]).then_inc(tr_ps.sem, 1)
                pe.wait_ge(tr_sb.sem, tr_sb.at(l, 2))
                pe.wait_ge(rope_sb.sem, rope_sb.at(l, 5))
                pe.wait_ge(vm_sb.sem, vm_sb.at(l, NB + 1))

                def scores(it):
                    kind, h, b = ITS[it]
                    k0, nk = key_cols(b)
                    for comp, g in enumerate(groups(it)):
                        if g % GROUPS >= 2:
                            pe.wait_ge(exp_done.sem, exp_done.at(l, g - 1))
                        rows = slice(0, QM) if kind == "mla" else slice(comp * DH, (comp + 1) * DH)
                        q = qT[rows, h, b * P:(b + 1) * P]
                        bank = S[g % 2]
                        n = min(nk, 512)
                        mm = pe.matmul(bank[:, 0:n], q, kT[rows, h, k0:k0 + n], start=True, stop=True)
                        if nk > n:
                            mm = pe.matmul(bank[:, n:nk], q, kT[rows, h, k0 + n:k0 + nk], start=True, stop=True)
                        mm.then_inc(sc_ps.sem, 1)

                def turn_probs(it):
                    _, h, b = ITS[it]
                    pe.wait_ge(probs_done.sem, probs_done.at(l, it + 1))
                    if it >= 1:
                        pe.wait_ge(pt_sb.sem, pt_sb.at(l, it))
                    for j in range(1 if b == 0 else NB):
                        mm = pe.transpose(T[:, j * P:(j + 1) * P], probs[it % 3][:, 0, j * P:(j + 1) * P], ident)
                    mm.then_inc(pt_ps.sem, 1)

                def apply_probs(it):
                    kind, h, b = ITS[it]
                    pe.wait_ge(pt_sb.sem, pt_sb.at(l, it + 1))
                    if it >= 2:
                        pe.wait_ge(o_sb.sem, o_sb.at(l, it - 1))
                    blocks = [0] if b == 0 else [1, 2, 3, 4, 5]
                    c0 = (it % 2) * 512
                    for j, kb in enumerate(blocks):
                        if kind == "mla":
                            half = (h % 2) * VDIM
                            out = U[half:half + VDIM, c0:c0 + P]
                            v = vm_rows[:, kb, h * VDIM:(h + 1) * VDIM]
                        else:
                            out = U[:, c0:c0 + P]
                            v = (v_rows[:, kb, h * P:(h + 1) * P] if kb < NB else cache_v[:, h * P:(h + 1) * P])
                        mm = pe.matmul(out, v, probsT[:, it % 2, j, :], start=(j == 0), stop=(j == len(blocks) - 1))
                    mm.then_inc(o_ps.sem, 1)

                def attention(first, last):
                    for i in range(first, last + 3):
                        if i < last:
                            scores(i)
                        if first <= i - 2 < last:
                            turn_probs(i - 2)
                        if i - 3 >= first:
                            apply_probs(i - 3)

                pe.wait_ge(unit_lat.sem, unit_lat.at(l, 12))
                pe.wait_ge(unit_ctx.sem, unit_ctx.at(l, 12))
                attention(0, ATT_IT)
                pe.wait_ge(o_sb.sem, o_sb.at(l, ATT_IT))

                for c, u0 in ((CH_Q, 12), (CH_K, 16)):
                    w = slot(turn, c)
                    for h in range(HEADS):
                        u = u0 + h
                        lat, cx = unit_banks(u)
                        product(lat, cx, lambda k: w[:, k, h * P:(h + 1) * P], lambda k: hT[:, k, :], KD)\
                            .then_inc(unit_ps.sem, 1)
                        if u > 12:
                            turn_pairs(4 + u - 12, slice(0, P), u - 1)
                w = slot(turn, CH_V)
                for b in range(NB):
                    if b >= 2:
                        pe.wait_ge(v_sb.sem, v_sb.at(l, b - 1))
                    dst = S[0][:, (b % 2) * 512:(b % 2 + 1) * 512]
                    for k in range(KD):
                        mm = pe.matmul(dst, hT[:, k, b * P:(b + 1) * P], w[:, k, :], start=(k == 0), stop=(k == KD - 1))
                    mm.then_inc(v_ps.sem, 1)
                    if b == 0:
                        turn_pairs(12, slice(0, P), 19)
                w = slot(turn, CH_F)
                for j in range(2):
                    lat, cx = unit_banks(20 + j)
                    product(lat, cx, lambda k: w[:, k, j * P:(j + 1) * P], lambda k: hT[:, k, :], KD)\
                        .then_inc(unit_ps.sem, 1)

                for h in range(HEADS):
                    mm = pe.transpose(misc_bank[:, h * P:(h + 1) * P], cache_k[:, h * P:(h + 1) * P], ident)
                mm.then_inc(tr_ps.sem, 1)
                pe.wait_ge(tr_sb.sem, tr_sb.at(l, 3))
                for h in range(HEADS):
                    mm = pe.transpose(misc_bank[:, h * P:(h + 1) * P], kT[:, h, 0:P], ident)
                mm.then_inc(tr_ps.sem, 1)

                pe.wait_ge(v_sb.sem, v_sb.at(l, NB))
                for j in range(2):
                    for part in range(2):
                        mm = pe.matmul(S[0][:, j * 512 + part * P:j * 512 + (part + 1) * P],
                                       consts[:, K_CHAN + part * P:K_CHAN + (part + 1) * P], wfour[:, j, :],
                                       start=True, stop=True)
                    mm.then_inc(cw_ps.sem, 1)
                pe.wait_ge(cw_sb.sem, cw_sb.at(l, 2))
                pe.wait_ge(unit_lat.sem, unit_lat.at(l, UNITS))
                pe.wait_ge(unit_ctx.sem, unit_ctx.at(l, UNITS))
                for b in range(NB):
                    if b >= 2:
                        pe.wait_ge(fa_sb.sem, fa_sb.at(l, b - 1))
                    for j in range(2):
                        mm = pe.matmul(lat_bank[b % 2][:, j * 256:(j + 1) * 256], zfT[:, j, b * P:(b + 1) * P],
                                       chanw[:, j, :, :], start=True, stop=True)
                    mm.then_inc(fa_ps.sem, 1)
                w = slot(turn, CH_DFT)
                for j in range(2):
                    lat, cx = S[0][:, 0:512], ctx_bank[1][:, 0:CTX]
                    if j == 0:
                        lat, cx = U[:, 0:512], S[0][:, 512:512 + CTX]
                    pe.wait_ge(fa_sb.sem, fa_sb.at(l, NB))
                    for part in range(2):
                        cols = slice(part * P, (part + 1) * P)
                        for b in range(4):
                            pe.matmul(lat, chan_rows[:, b + 1, j, cols], w[:, 4 * part + b, :],
                                      start=(part == 0 and b == 0), stop=(part == 1 and b == 3))
                    for part in range(2):
                        cols = slice(part * P, (part + 1) * P)
                        mm = pe.matmul(cx, chan_rows[:, 0, j, cols], consts[:, K_SEQX + part * CTX:K_SEQX + (part + 1) * CTX],
                                       start=(part == 0), stop=(part == 1))
                    mm.then_inc(fb_ps.sem, 1)

                pe.wait_ge(fb_sb.sem, fb_sb.at(l, 2))
                pe.wait_ge(rope_sb.sem, rope_sb.at(l, ROPES))
                pe.wait_ge(tr_sb.sem, tr_sb.at(l, 4))
                attention(ATT_IT, 2 * ATT_IT)
                pe.wait_ge(exp_done.sem, exp_done.at(l, GROUPS))

                sub_banks = [S[0][:, 0:512], S[0][:, 512:1024], S[1][:, 0:512], T[:, 512:1024]]
                pe.wait_ge(o_sb.sem, o_sb.at(l, 2 * ATT_IT))
                for h in range(HEADS):
                    pe.wait_ge(sub_sq.sem, sub_sq.at(l, h + 1))
                    pe.matmul(sub_banks[h], ones[:, :], sub_squares[:, h, CTX:TOK], start=True, stop=True)
                    pe.matmul(S[1][:, 512 + h * CTX:512 + (h + 1) * CTX], ones[:, :], sub_squares[:, h, 0:CTX],
                              start=True, stop=True).then_inc(sub_ps.sem, 1)
                order = [0, 1, 6, 7, 2, 3, 4, 5]
                for c in range(2):
                    w = slot(turn, CH_OUT + c)
                    for m in range(4):
                        n = 4 * c + m
                        if n >= 2:
                            pe.wait_ge(mix_sb.sem, mix_sb.at(l, n - 1))
                        for at, k in enumerate(order):
                            if n == 0 and 2 <= k < 6:
                                pe.wait_ge(sub_scaled.sem, sub_scaled.at(l, k - 1))
                            x = yT[:, k, :] if k < 6 else y_mla[:, k - 6, :]
                            flags = dict(start=(at == 0), stop=(at == KD - 1))
                            pe.matmul(lat_bank[n % 2], w[:, k, m * P:(m + 1) * P], x[:, CTX:TOK], **flags)
                            mm = pe.matmul(ctx_bank[n % 2][:, 0:CTX], w[:, k, m * P:(m + 1) * P], x[:, 0:CTX], **flags)
                        mm.then_inc(mix_ps.sem, 1)

                wide_norm(l, 1)
                pe.wait_ge(mix_sb.sem, mix_sb.at(l, KD))
                for k in range(KD):
                    pe.wait_ge(h_done.sem, h_done.at(l, KD + k + 1))
                    q = 32 * (k % 4)
                    flags = dict(start=(k < 4), stop=(k >= 4))
                    pe.matmul(T[q:q + 32, 0:LAT], wrt[:, k, :], hT[:, k, CTX:TOK], **flags)
                    mm = pe.matmul(T[q:q + 32, 512:512 + CTX], wrt[:, k, :], hT[:, k, 0:CTX], **flags)
                mm.then_inc(parts_ps.sem, 1)
                pe.wait_ge(rms_done.sem, rms_done.at(l, 2))

                def rows_of_h(b):
                    if b >= 2:
                        pe.wait_ge(hr_v.sem, hr_v.at(l, min(b - 1, 2)))
                        pe.wait_ge(hr_a.sem, hr_a.at(l, b - 1))
                    for k in range(KD):
                        mm = pe.transpose(S[b % 2][:, k * P:(k + 1) * P], hT[:, k, b * P:(b + 1) * P], ident)
                    mm.then_inc(hr_ps.sem, 1)

                for b in range(2):
                    rows_of_h(b)
                pe.wait_ge(parts_sb.sem, parts_sb.at(l, 1))
                for b in range(NB):
                    mm = pe.matmul(T[:, b * E_N:(b + 1) * E_N], logit_parts[:, b * P:(b + 1) * P],
                                   consts[:, K_FOLD:K_FOLD + E_N], start=True, stop=True)
                mm.then_inc(lg_ps.sem, 1)
                pe.wait_ge(aff_rows.sem, aff_rows.at(l, 1))
                for b in range(NB):
                    dst = U[0:E_N, 512:512 + P] if b == 0 else U[0:E_N, (b - 1) * P:b * P]
                    mm = pe.transpose(dst, lg[:, b, :], ident)
                mm.then_inc(aff_ps.sem, 1)
                for b in range(2, NB):
                    rows_of_h(b)
                pe.wait_ge(pos_done.sem, pos_done.at(l, 1))
                for b in range(NB):
                    mm = pe.matmul(T[:, b * E_N:(b + 1) * E_N], pos[:, b * P:(b + 1) * P].bitcast(F32), ident[0:E_N, 0:E_N],
                                   start=True, stop=True)
                mm.then_inc(pr_ps.sem, 1)

                def gather_lat(u):
                    pe.wait_ge(pick_done.sem, pick_done.at(u, 1))
                    for k in range(KD):
                        for b in range(4):
                            mm = pe.matmul(U[:, k * P:(k + 1) * P], h_rows[:, b + 1, k * P:(k + 1) * P], pick[:, b, :],
                                           start=(b == 0), stop=(b == 3))
                    mm.then_inc(gl_ps.sem, 1)

                def gather_ctx(u):
                    n = 2 * CAPX
                    for k in range(KD):
                        mm = pe.matmul(S[0][:, k * n:(k + 1) * n], h_rows[:, 0, k * P:(k + 1) * P], pickx[:, :],
                                       start=True, stop=True)
                    mm.then_inc(gx_ps.sem, 1)

                u = l * (PAIRS + 1)
                pe.wait_ge(hr_v.sem, hr_v.at(l, 2))
                pe.wait_ge(hr_a.sem, hr_a.at(l, NB))
                gather_lat(u)
                gather_ctx(u)

                def scatter(v, n, lat, cx, ahead):
                    if n >= ahead:
                        pe.wait_ge(add_sb.sem, add_sb.at(v, n - ahead + 1))
                    cols = slice(n * P, (n + 1) * P)
                    pe.matmul(lat, ye_hi[:, cols], back[:, :], start=True, stop=False)
                    pe.matmul(lat, ye_lo[:, cols], back[:, :], start=False, stop=True)
                    pe.matmul(cx, yex[:, cols], backx[:, :], start=True, stop=True).then_inc(add_ps.sem, 1)

                with pe.Fori(0, PAIRS) as pair:
                    t = l * PAIRS + pair
                    u = l * (PAIRS + 1) + pair + 1

                    def group(g, between={}):
                        i, matrix, half = GROUPS_OF_PAIR[g]
                        if matrix == DOWN:
                            out = T[0:SLOT_TOK, half * 512:(half + 1) * 512]
                        else:
                            out = S[half][0:SLOT_TOK, matrix * 512:(matrix + 1) * 512]
                        for piece in range(PIECES):
                            if (g, piece) in ON_GPSIMD:
                                pe.wait_ge(lo_done_g.sem, lo_done_g.at(t, ON_GPSIMD.index((g, piece)) + 1))
                            else:
                                pe.wait_ge(lo_done.sem, lo_done.at(t, ON_VECTOR.index((g, piece)) + 1))
                            for kk in range(2):
                                k = 2 * piece + kk
                                x_hi = hm_hi[:, i, k, :] if matrix == DOWN else xs_hi[:, k, i, :]
                                x_lo = hm_lo[:, i, k, :] if matrix == DOWN else xs_lo[:, k, i, :]
                                w_low = ring_lo[:, g % RING, k, :]
                                pe.matmul(out, x_lo, w_hi[:, piece, kk, :], start=(k == 0), stop=False)
                                pe.matmul(out, x_hi, w_hi[:, piece, kk, :], start=False, stop=False)
                                mm = pe.matmul(out, x_hi, w_low, start=False, stop=(k == KD - 1))
                            mm.then_inc(piece_ps.sem if piece < PIECES - 1 else gr_ps.sem, 1)
                            if piece in between:
                                scatter(u - 1, between[piece], T[:, 0:LAT], T[:, 512:512 + CTX], 1)

                    def turn_middle(i):
                        pe.wait_ge(hm_done.sem, hm_done.at(t, 2 * i + 2))
                        for j in range(KD):
                            c0 = (j // 4) * 512 + (j % 4) * SLOT_TOK
                            mm = pe.transpose(U[:, c0:c0 + SLOT_TOK], hm_rows[i][0:SLOT_TOK, j * P:(j + 1) * P],
                                              ident[0:SLOT_TOK, 0:SLOT_TOK])
                        mm.then_inc(th_ps.sem, 1)

                    pe.wait_ge(back_done.sem, back_done.at(t, 0))
                    pe.wait_ge(gate_cols.sem, gate_cols.at(t, 1))
                    for i in range(2):
                        out = U[:, 256 + i:257 + i]
                        for b in range(4):
                            pe.matmul(out[0:CAP, :], pick[:, b, i * CAP:(i + 1) * CAP], cur_gate[:, b + 1, i:i + 1],
                                      start=(b == 0), stop=(b == 3))
                        mm = pe.matmul(out[CAP:SLOT_TOK, :], pickx[:, i * CAPX:(i + 1) * CAPX], cur_gate[:, 0, i:i + 1],
                                       start=True, stop=True)
                    mm.then_inc(gate_ps.sem, 1)
                    pe.wait_ge(xx_lo.sem, xx_lo.at(u - 1, 1))
                    group(0)
                    pe.wait_ge(rows_done.sem, rows_done.at(u - 1, 1))
                    group(1, {3: 0})
                    group(2, {2: 1})
                    group(3, {1: 2})
                    pe.wait_ge(hm_done.sem, hm_done.at(t, 1))
                    group(4, {1: 3})
                    pe.wait_ge(gate_sb.sem, gate_sb.at(t, 1))
                    turn_middle(0)
                    group(5, {1: 4})
                    pe.wait_ge(hl_done.sem, hl_done.at(t, 1))
                    gather_lat(u)
                    group(6, {0: 5, 2: 6})
                    group(7, {1: 7})
                    pe.wait_ge(add_sb.sem, add_sb.at(u - 1, KD))
                    group(8)
                    pe.wait_ge(xl_lo.sem, xl_lo.at(u, 1))
                    turn_middle(1)
                    gather_ctx(u)
                    group(9)
                    pe.wait_ge(hl_done.sem, hl_done.at(t, 2))
                    pe.wait_ge(ye0_lo.sem, ye0_lo.at(t, 1))
                    group(10)
                    pe.wait_ge(sel_done.sem, sel_done.at(t, 1))
                    pe.matmul(U[:, 0:LAT], sel[:, :, :].rearrange("e i c -> e (i c)"), pos[:, CTX:TOK], start=True, stop=True)
                    pe.matmul(U[:, 512:512 + CTX], selx[:, :, :, :].rearrange("e a i c -> e (a i c)"), pos[:, 0:CTX],
                              start=True, stop=True).then_inc(place_ps.sem, 1)
                    pe.wait_ge(ye0_lo.sem, ye0_lo.at(t, 2))
                    group(11)
                u = l * (PAIRS + 1) + PAIRS
                pe.wait_ge(rows_done.sem, rows_done.at(u, 1))
                for n in range(KD):
                    scatter(u, n, lat_bank[n % 2], ctx_bank[n % 2][:, 0:CTX], 2)
                pe.wait_ge(add_sb.sem, add_sb.at(u, KD))

            wide_norm(DEPTH, 0)
            pe.wait_ge(xn_done.sem, xn_done.at(DEPTH, KD))
            for b in range(NB):
                if b >= 2:
                    pe.wait_ge(fin_v.sem, b - 1)
                    pe.wait_ge(fin_a.sem, b - 1)
                if b == 0:
                    pe.wait_ge(rms_done.sem, rms_done.at(DEPTH, 1))
                for k in range(KD):
                    mm = pe.transpose(S[b % 2][:, k * P:(k + 1) * P], hT[:, k, b * P:(b + 1) * P], ident)
                mm.then_inc(fin_ps.sem, 1)

        @block.scalar
        def _(act):
            act.wait_ge(const_in.sem, const_in.at(0, 0))
            act.activation(cond_e[:, :], cond_rows[0:2 * KD, :], ACT.Exp, scale=-1.0).then_inc(cond_exp.sem, 1)

            def root(n_feat, ready, value, l, s, done):
                act.wait_ge(ready, value)
                act.activation(rstd[:, CTX:TOK], sum_lat, ACT.Ln, bias=eps, scale=1.0 / n_feat)
                act.activation(rstd[:, 0:CTX], sum_ctx, ACT.Ln, bias=eps, scale=1.0 / n_feat).then_inc(step_a.sem, 1)
                act.wait_ge(step_a.sem, step_a.at(l, s))
                act.activation(rstd[:, :], rstd[:, :], ACT.Exp, scale=-0.5).then_inc(done, 1)

            def squares(l, which, blocks=range(KD)):
                for k in blocks:
                    if k >= 3:
                        act.wait_ge(sq_added.sem, sq_added.at(l, which * KD + k - 1))
                    if which == 1:
                        act.wait_ge(mix_sb.sem, mix_sb.at(l, k + 1))
                    dst = rstd[:, :] if k == 0 else scr[:, k % 2, :]
                    act.activation(dst, xT[:, k, :], ACT.Square).then_inc(sq_done.sem, 1)

            def modulate(l, which):
                for k in range(KD):
                    act.wait_ge(xn_done.sem, xn_done.at(l, which * KD + k + 1))
                    sh = 3 * which * KD + k
                    act.activation(hT[:, k, 0:CTX], hT[:, k, 0:CTX], ACT.Identity, bias=mod[:, sh, 0:1],
                                   scale=gain[:, which, k, 0:1])
                    act.activation(hT[:, k, CTX:TOK], hT[:, k, CTX:TOK], ACT.Identity, bias=mod[:, sh, 1:2],
                                   scale=gain[:, which, k, 1:2]).then_inc(h_done.sem, 1)

            act.wait_ge(xt_sb.sem, KD)
            with act.Fori(0, DEPTH) as l:
                act.wait_ge(add_sb.sem, add_sb.at(l * (PAIRS + 1), 0))

                def modulation_rows(chunks):
                    for c in chunks:
                        act.wait_ge(adar_ps.sem, adar_ps.at(l, c + 1))
                        if c >= 2:
                            act.wait_ge(ada_ps.sem, ada_ps.at(l, c - 1))
                        act.activation(ada_rows[:, c % 2, :], lat_bank[c % 2], ACT.Copy).then_inc(adar_sb.sem, 1)

                modulation_rows(range(2))
                squares(l, 0, range(4))
                modulation_rows(range(2, 4))
                squares(l, 0, range(4, KD))
                root(D, sum_ps.sem, sum_ps.at(l, 1), l, 1, rms_done.sem)
                modulation_rows(range(4, ADA_CHUNKS))
                act.wait_ge(gain_sb.sem, gain_sb.at(l, 1))
                modulate(l, 0)
                act.wait_ge(lam_prod.sem, lam_prod.at(l, 1))
                act.activation(lamw[:, 0:2], lamw[:, 0:2], ACT.Exp).then_inc(lam_exp.sem, 1)

                def ctx_copy(u, dst):
                    act.wait_ge(unit_ps.sem, unit_ps.at(l, u + 1))
                    m = dst.shape[0]
                    act.activation(dst, ctx_bank[u % 2][0:m, 0:dst.shape[1]], ACT.Copy).then_inc(unit_ctx.sem, 1)

                def narrow_square(n, src, lat_ready):
                    act.wait_ge(*lat_ready)
                    act.activation(scr[:, n % 2, :], src, ACT.Square).then_inc(nsq_done.sem, 1)

                ctx_copy(0, cqT[:, 0, 0:CTX])
                ctx_copy(1, cqT[:, 1, 0:CTX])
                act.wait_ge(unit_ctx.sem, unit_ctx.at(l, 2))
                narrow_square(0, cqT[:, 0, :], (unit_lat.sem, unit_lat.at(l, 1)))
                narrow_square(1, cqT[:, 1, :], (unit_lat.sem, unit_lat.at(l, 2)))
                ctx_copy(2, ckvT[:, 0:CTX])
                act.wait_ge(unit_ps.sem, unit_ps.at(l, 4))
                act.activation(kpeT[NOPE:QM, 0:CTX], ctx_bank[1][NOPE:QM, 0:CTX], ACT.Copy).then_inc(unit_ctx.sem, 1)
                root(2 * P, nsum_ps.sem, nsum_ps.at(l, 1), l, 2, nrms_done.sem)
                act.wait_ge(unit_ctx.sem, unit_ctx.at(l, 3))
                narrow_square(2, ckvT[:, 0:TOK], (unit_lat.sem, unit_lat.at(l, 3)))
                act.wait_ge(tr_ps.sem, tr_ps.at(l, 1))
                act.activation(ckvT[:, TOK:TOK + PAST], misc_bank[:, 0:P], ACT.Copy)
                act.activation(kpeT[NOPE:QM, TOK:TOK + PAST], misc_bank[NOPE:QM, P:2 * P], ACT.Copy).then_inc(tr_sb.sem, 1)
                act.wait_ge(nscaled.sem, nscaled.at(l, 1))
                root(P, nsum_ps.sem, nsum_ps.at(l, 2), l, 3, nrms_done.sem)
                for h in range(HEADS):
                    ctx_copy(4 + h, qT[0:QM, h, 0:CTX])
                for h in range(HEADS):
                    ctx_copy(8 + h, kT[0:NOPE, h, 512:768])
                for b in range(NB + 1):
                    act.wait_ge(vm_ps.sem, vm_ps.at(l, b + 1))
                    act.activation(vm_rows[:, b, :], S[0][:, (b % 2) * 512:(b % 2) * 512 + HEADS * VDIM], ACT.Copy)\
                       .then_inc(vm_sb.sem, 1)
                act.wait_ge(tr_ps.sem, tr_ps.at(l, 2))
                act.activation(ckv_rows[:, :], misc_bank[:, 0:P], ACT.Copy)
                act.activation(kpe_rows[:, :], misc_bank[:, P:P + ROPE], ACT.Copy).then_inc(tr_sb.sem, 1)
                act.wait_ge(tr_sb.sem, tr_sb.at(l, 2))
                act.dma_start(a["new_mla_ckv"][0, l], ckv_rows[:, :]).then_inc(outs_done.sem, 16)
                act.dma_start(a["new_mla_kpe"][0, l], kpe_rows[:, :]).then_inc(outs_done.sem, 16)

                def attention(first, last):
                    for i in range(first, last + 2):
                        if i < last:
                            kind, h, b = ITS[i]
                            nk = key_cols(b)[1]
                            for comp, g in enumerate(groups(i)):
                                act.wait_ge(negm_done.sem, negm_done.at(l, g + 1))
                                act.activation(probs[i % 3][:, comp, 0:nk], S[g % 2][:, 0:nk], ACT.Exp, bias=negm[:, g % 2:g % 2 + 1],
                                               scale=MLA_SCALE if kind == "mla" else DIFF_SCALE,
                                               accum_out=ssum[:, i % 3, comp:comp + 1]).then_inc(exp_done.sem, 1)
                        if i - 2 >= first:
                            it = i - 2
                            _, h, b = ITS[it]
                            n = P if b == 0 else KEYS
                            act.wait_ge(pt_ps.sem, pt_ps.at(l, it + 1))
                            if it - 2 >= 0:
                                act.wait_ge(o_ps.sem, o_ps.at(l, it - 1))
                            act.activation(probsT[:, it % 2, :, :].rearrange("p j q -> p (j q)")[:, 0:n], T[:, 0:n], ACT.Copy)\
                               .then_inc(pt_sb.sem, 1)

                attention(0, ATT_IT)
                for h in range(HEADS):
                    ctx_copy(12 + h, qT[:, h, 0:CTX])
                for h in range(HEADS):
                    ctx_copy(16 + h, kT[:, h, 0:CTX])
                for b in range(NB):
                    act.wait_ge(v_ps.sem, v_ps.at(l, b + 1))
                    act.activation(v_rows[:, b, :], S[0][:, (b % 2) * 512:(b % 2 + 1) * 512], ACT.Copy).then_inc(v_sb.sem, 1)
                for j in range(2):
                    ctx_copy(20 + j, zfT[:, j, 0:CTX])
                act.wait_ge(v_sb.sem, v_sb.at(l, 1))
                act.dma_start(a["new_diff_v"][0, l].rearrange("t h d -> t (h d)"), v_rows[:, 0, :]).then_inc(outs_done.sem, 16)
                act.wait_ge(tr_ps.sem, tr_ps.at(l, 3))
                act.activation(kT[:, :, TOK:TOK + PAST], misc_bank.rearrange("p (h t) -> p h t", h=HEADS), ACT.Copy)\
                   .then_inc(tr_sb.sem, 1)
                act.wait_ge(tr_ps.sem, tr_ps.at(l, 4))
                act.activation(k_rows[:, :], misc_bank, ACT.Copy).then_inc(tr_sb.sem, 1)
                act.wait_ge(tr_sb.sem, tr_sb.at(l, 4))
                act.dma_start(a["new_diff_k"][0, l].rearrange("t h d -> t (h d)"), k_rows[:, :]).then_inc(outs_done.sem, 16)
                for j in range(2):
                    act.wait_ge(cw_ps.sem, cw_ps.at(l, j + 1))
                    act.activation(chanw[:, j, :, :].rearrange("p a e -> p (a e)"), S[0][:, j * 512:j * 512 + 2 * P], ACT.Copy)\
                       .then_inc(cw_sb.sem, 1)
                for b in range(NB):
                    act.wait_ge(fa_ps.sem, fa_ps.at(l, b + 1))
                    act.activation(chan_rows[:, b, :, :].rearrange("p j e -> p (j e)"), lat_bank[b % 2], ACT.Copy)\
                       .then_inc(fa_sb.sem, 1)
                attention(ATT_IT, 2 * ATT_IT)
                act.wait_ge(o_sb.sem, o_sb.at(l, 2 * ATT_IT))
                for h in range(HEADS):
                    act.activation(sub_squares[:, h, :], yT[:, 2 + h, :], ACT.Square).then_inc(sub_sq.sem, 1)
                act.wait_ge(sub_ps.sem, sub_ps.at(l, 2))
                act.activation(sub_rstd[:, 0:1024], S[0][:, :], ACT.Ln, bias=eps, scale=1.0 / P)
                act.wait_ge(sub_ps.sem, sub_ps.at(l, HEADS))
                act.activation(sub_rstd[:, 1024:2048], S[1][:, :], ACT.Ln, bias=eps, scale=1.0 / P).then_inc(sub_ln.sem, 1)
                act.activation(sub_rstd[:, 2048:2560], T[:, 512:1024], ACT.Ln, bias=eps, scale=1.0 / P).then_inc(sub_ln.sem, 1)
                act.wait_ge(sub_ln.sem, sub_ln.at(l, 1))
                act.activation(sub_rstd[:, 0:2048], sub_rstd[:, 0:2048], ACT.Exp, scale=-0.5).then_inc(sub_rms.sem, 1)
                act.wait_ge(sub_ln.sem, sub_ln.at(l, 2))
                act.activation(sub_rstd[:, 2048:2560], sub_rstd[:, 2048:2560], ACT.Exp, scale=-0.5).then_inc(sub_rms.sem, 1)

                squares(l, 1)
                root(D, sum_ps.sem, sum_ps.at(l, 2), l, 4, rms_done.sem)
                modulate(l, 1)
                act.wait_ge(parts_ps.sem, parts_ps.at(l, 1))
                act.activation(logit_parts[:, 0:CTX], T[:, 512:512 + CTX], ACT.Copy)
                act.activation(logit_parts[:, CTX:TOK], T[:, 0:LAT], ACT.Copy).then_inc(parts_sb.sem, 1)
                act.wait_ge(lg_shift.sem, lg_shift.at(l, 1))
                act.activation(lg[:, :, :], lg[:, :, :], ACT.Exp).then_inc(lg_exp.sem, 1)
                act.wait_ge(outs_done.sem, outs_done.at(l + 1, 0))
                for b in range(NB):
                    act.wait_ge(hr_ps.sem, hr_ps.at(l, b + 1))
                    first = 512 if b < 2 else 0
                    act.activation(h_rows[:, b, first:D], S[b % 2][:, first:D], ACT.Copy).then_inc(hr_a.sem, 1)

                def high_lat(u):
                    act.wait_ge(gl_ps.sem, gl_ps.at(u, 1))
                    act.activation(xs_hi[:, :, :, 0:CAP], U[:, :].rearrange("p (k i c) -> p k i c", k=KD, i=2), ACT.Copy)\
                       .then_inc(xl_hi.sem, 1)

                def high_ctx(u):
                    act.wait_ge(gx_ps.sem, gx_ps.at(u, 1))
                    act.activation(xs_hi[:, :, :, CAP:SLOT_TOK],
                                   S[0][:, 0:KD * 2 * CAPX].rearrange("p (k i c) -> p k i c", k=KD, i=2), ACT.Copy)\
                       .then_inc(xx_hi.sem, 1)

                u = l * (PAIRS + 1)
                high_lat(u)
                high_ctx(u)

                def out_rows(i, half, done):
                    cols = slice(half * 512, (half + 1) * 512)
                    act.activation(ye_hi[i * CAP:(i + 1) * CAP, cols], T[0:CAP, cols], ACT.Copy)
                    act.activation(yex[i * XROW:i * XROW + CAPX, cols], T[CAP:SLOT_TOK, cols], ACT.Copy)\
                       .then_inc(done.sem, 1)

                with act.Fori(0, PAIRS) as pair:
                    t = l * PAIRS + pair
                    u = l * (PAIRS + 1) + pair + 1

                    def high_pieces(g):
                        act.wait_ge(slot_in[g % RING].sem,
                                    (l * LAYER_CHUNKS + DENSE_CHUNKS + pair * PAIR_CHUNKS) * (16 // RING) + (g // RING + 1) * 16)
                        for piece in range(PIECES):
                            if piece < PIECES - 1:
                                act.wait_ge(piece_ps.sem, piece_ps.at(t, (g - 1) * (PIECES - 1) + piece + 1))
                            else:
                                act.wait_ge(gr_ps.sem, gr_ps.at(t, g))
                            act.activation(w_hi[:, piece, :, :], ring[:, g % RING, 2 * piece:2 * piece + 2, :], ACT.Copy)\
                               .then_inc(hi_done.sem, 1)

                    def silu(i, half):
                        act.wait_ge(gr_ps.sem, gr_ps.at(t, 4 * i + 2 * half + 1))
                        act.activation(hm_rows[i][0:SLOT_TOK, half * 512:(half + 1) * 512], S[half][0:SLOT_TOK, 0:512], ACT.Silu)\
                           .then_inc(silu_done.sem, 1)

                    def high_middle(i):
                        act.wait_ge(th_ps.sem, th_ps.at(t, i + 1))
                        act.activation(hm_hi[:, i, :, :].rearrange("p (b j) c -> p b (j c)", b=2),
                                       U[:, :].rearrange("p (b n) -> p b n", b=2)[:, :, 0:4 * SLOT_TOK], ACT.Copy)\
                           .then_inc(hh_done.sem, 1)

                    high_pieces(0)
                    act.wait_ge(gate_ps.sem, gate_ps.at(t, 1))
                    act.activation(gates[:, :], U[0:SLOT_TOK, 256:258], ACT.Copy).then_inc(gate_sb.sem, 1)
                    act.wait_ge(gr_ps.sem, gr_ps.at(t, 0))
                    act.wait_ge(t_clear.sem, t_clear.at(l, 1))
                    out_rows(1, 0, ye1_hi)
                    out_rows(1, 1, ye1_hi)
                    high_pieces(1)
                    silu(0, 0)
                    high_pieces(2)
                    high_pieces(3)
                    silu(0, 1)
                    high_pieces(4)
                    high_pieces(5)
                    high_middle(0)
                    silu(1, 0)
                    high_pieces(6)
                    high_pieces(7)
                    silu(1, 1)
                    high_pieces(8)
                    act.wait_ge(gr_ps.sem, gr_ps.at(t, 8))
                    high_lat(u)
                    high_pieces(9)
                    high_middle(1)
                    high_ctx(u)
                    act.wait_ge(gr_ps.sem, gr_ps.at(t, 9))
                    out_rows(0, 0, ye0_hi)
                    high_pieces(10)
                    act.wait_ge(gr_ps.sem, gr_ps.at(t, 10))
                    out_rows(0, 1, ye0_hi)
                    high_pieces(11)
                act.wait_ge(gr_ps.sem, gr_ps.at((l + 1) * PAIRS, 0))
                out_rows(1, 0, ye1_hi)
                out_rows(1, 1, ye1_hi)

            act.wait_ge(add_sb.sem, add_sb.at(DEPTH * (PAIRS + 1), 0))
            squares(DEPTH, 0)
            root(D, sum_ps.sem, sum_ps.at(DEPTH, 1), DEPTH, 1, rms_done.sem)
            for b in range(NB):
                act.wait_ge(fin_ps.sem, b + 1)
                act.activation(arena[:, b * D + 512:(b + 1) * D], S[b % 2][:, 512:1024], ACT.Copy).then_inc(fin_a.sem, 1)

        @block.vector
        def _(ve):
            count = [0]

            def link(ins):
                count[0] += 1
                ins.then_inc(step_v, 1)
                ve.wait_ge(step_v, count[0])

            ve.sem_inc(pr_sb.sem, 1)
            ve.wait_ge(cond_exp.sem, 1)
            link(ve.tensor_scalar(cond_e[:, :], cond_e[:, :], 1.0, None, ALU.add))
            link(ve.reciprocal(cond_e[:, :], cond_e[:, :]))
            ve.tensor_tensor(cond_rows[0:2 * KD, :], cond_rows[0:2 * KD, :], cond_e[:, :], ALU.mult).then_inc(cond_silu.sem, 1)
            for k in range(KD):
                ve.wait_ge(xt_ps.sem, k + 1)
                ve.tensor_copy(xT[:, k, 0:CTX], ctx_bank[k % 2][:, 0:CTX])
                ve.tensor_copy(xT[:, k, CTX:TOK], lat_bank[k % 2]).then_inc(xt_sb.sem, 1)
            ve.wait_ge(cond_ps.sem, 1)
            link(ve.tensor_copy(condT[:, :], misc_bank[:, 0:3 * KD]))
            ve.tensor_copy(condP[:, :, 0:2], condT[:, 0:2 * KD].rearrange("p (s k) -> p k s", s=2)).then_inc(cond_sb.sem, 1)
            ve.sem_inc(add_sb.sem, 1)
            ve.sem_inc(back_done.sem, 1)

            def add_squares(l, which, k):
                ve.wait_ge(sq_done.sem, sq_done.at(l, which * KD + k + 1))
                if k == 0:
                    ve.sem_inc(sq_added.sem, 1)
                    return
                if k >= 2:
                    ve.wait_ge(sq_added.sem, sq_added.at(l, which * KD + k))
                ve.tensor_tensor(rstd[:, :], rstd[:, :], scr[:, k % 2, :], ALU.add).then_inc(sq_added.sem, 1)

            def normalise(l, which):
                ve.wait_ge(rms_done.sem, rms_done.at(l, which + 1))
                for k in range(KD):
                    ve.tensor_tensor(hT[:, k, :], xT[:, k, :], rstd[:, :], ALU.mult).then_inc(xn_done.sem, 1)

            with ve.Fori(0, DEPTH) as l:
                ve.sem_clear(step_v)
                count[0] = 0
                ve.wait_ge(vec_ps.sem, vec_ps.at(l, 1))
                ve.tensor_copy(vecT[:, :], misc_bank[:, 0:N_VEC]).then_inc(vec_sb.sem, 1)
                ve.wait_ge(vec_sb.sem, vec_sb.at(l, 1))

                def modulation(chunks):
                    for c in chunks:
                        ve.wait_ge(ada_ps.sem, ada_ps.at(l, c + 1))
                        ve.tensor_tensor(mod[:, 4 * c:4 * c + 4, :], ctx_bank[c % 2][:, 0:8].rearrange("p (m s) -> p m s", s=2),
                                         vecT[:, 4 * c:4 * c + 4].unsqueeze(2).broadcast_to([P, 4, 2]), ALU.add)\
                          .then_inc(ada_sb.sem, 1)

                for k in range(4):
                    add_squares(l, 0, k)
                modulation(range(2))
                for k in range(4, KD):
                    add_squares(l, 0, k)
                modulation(range(2, 4))
                normalise(l, 0)
                modulation(range(4, ADA_CHUNKS))
                ve.wait_ge(ada_sb.sem, ada_sb.at(l, ADA_CHUNKS))
                for which in range(2):
                    g0 = N_MOD * KD + which * KD
                    s0 = (3 * which + 1) * KD
                    ins = ve.scalar_tensor_tensor(out=gain[:, which, :, :], in0=mod[:, s0:s0 + KD, :], scalar=1.0,
                                                  in1=vecT[:, g0:g0 + KD].unsqueeze(2).broadcast_to([P, KD, 2]),
                                                  op0=ALU.add, op1=ALU.mult)
                ins.then_inc(gain_sb.sem, 1)
                ve.wait_ge(small_in.sem, small_in.at(l + 1, 0))
                pairs = dlam[:, :, :].rearrange("p (a b) d -> p a b d", b=2)
                link(ve.tensor_tensor(dprod[:, :, :], pairs[:, :, 0, :], pairs[:, :, 1, :], ALU.mult))
                ve.reduce_sum(lamw[:, 0:2], dprod[:, :, :], AX.X).then_inc(lam_prod.sem, 1)
                ve.wait_ge(lam_exp.sem, lam_exp.at(l, 1))
                link(ve.scalar_tensor_tensor(out=lamw[:, 2:3], in0=lamw[:, 1:2], scalar=lamw[:, 0:1], in1=lamt[:, 0:1],
                                                op0=ALU.subtract, op1=ALU.subtract))
                ve.tensor_tensor(gsub[:, :], vecT[:, N_VEC - 1:N_VEC], lamt[:, 1:2], ALU.mult).then_inc(lam_done.sem, 1)
                ve.wait_ge(lam_done.sem, lam_done.at(l, 1))

                rope_n = [0]

                def lat_copy(u, dst):
                    ve.wait_ge(unit_ps.sem, unit_ps.at(l, u + 1))
                    ve.tensor_copy(dst, lat_bank[u % 2][0:dst.shape[0], :]).then_inc(unit_lat.sem, 1)

                def rope_parts(u, dst, rows, cos, sin):
                    r = rope_n[0]
                    ve.wait_ge(unit_ps.sem, unit_ps.at(l, u + 1))
                    if r >= 2:
                        ve.wait_ge(rope_ps.sem, rope_ps.at(l, r - 1))
                    z = lat_bank[u % 2][rows, :]
                    ve.tensor_tensor(dst, z, cos[rows, :], ALU.mult)
                    ve.tensor_tensor(rope_a[rows, r % 2, :], z, sin[rows, :], ALU.mult).then_inc(unit_lat.sem, 1)
                    rope_n[0] += 1

                def rope_add(r, dst, rows):
                    ve.wait_ge(rope_ps.sem, rope_ps.at(l, r + 1))
                    ve.tensor_tensor(dst, rot_bank[rows, :], dst, ALU.add).then_inc(rope_sb.sem, 1)

                def narrow_scale(n, dst, g_col):
                    ve.wait_ge(nrms_done.sem, nrms_done.at(l, n + 1))
                    for j, blk in enumerate(dst):
                        ins = ve.scalar_tensor_tensor(out=blk, in0=blk, scalar=g_col[:, j:j + 1], in1=rstd[:, :],
                                                      op0=ALU.mult, op1=ALU.mult)
                    ins.then_inc(nscaled.sem, 1)

                lat_copy(0, cqT[:, 0, CTX:TOK])
                lat_copy(1, cqT[:, 1, CTX:TOK])
                lat_copy(2, ckvT[:, CTX:TOK])
                kpe_rows_at = slice(NOPE, QM)
                rope_parts(3, kpeT[NOPE:QM, CTX:TOK], kpe_rows_at, cos_m, sin_m)
                gq = N_VEC - 4
                narrow_scale(0, [cqT[:, 0, :], cqT[:, 1, :]], vecT[:, gq:gq + 2])
                rope_add(0, kpeT[NOPE:QM, CTX:TOK], kpe_rows_at)
                ve.wait_ge(rope_sb.sem, rope_sb.at(l, 1))
                ve.wait_ge(unit_ctx.sem, unit_ctx.at(l, 4))
                ve.wait_ge(tr_sb.sem, tr_sb.at(l, 1))
                for h in range(HEADS):
                    ins = ve.tensor_copy(kT[NOPE:QM, h, :], kpeT[NOPE:QM, :])
                ins.then_inc(kpe_spread.sem, 1)
                narrow_scale(1, [ckvT[:, 0:TOK]], vecT[:, gq + 2:gq + 3])
                q_rows_at = slice(0, QM)
                for h in range(HEADS):
                    rope_parts(4 + h, qT[0:QM, h, CTX:TOK], q_rows_at, cos_m, sin_m)
                    if h >= 1:
                        rope_add(h, qT[0:QM, h - 1, CTX:TOK], q_rows_at)
                lat_copy(8, kT[0:NOPE, 0, 0:512])
                rope_add(4, qT[0:QM, HEADS - 1, CTX:TOK], q_rows_at)
                for h in range(1, HEADS):
                    lat_copy(8 + h, kT[0:NOPE, h, 0:512])

                def attention(first, last):
                    for i in range(first, last + 4):
                        if first <= i - 1 < last:
                            it = i - 1
                            kind, h, b = ITS[it]
                            n = key_cols(b)[1]
                            s = it % 3
                            ve.wait_ge(exp_done.sem, exp_done.at(l, groups(it)[-1] + 1))
                            if kind == "mla":
                                link(ve.reciprocal(srec[:, s, 0:1], ssum[:, s, 0:1]))
                                ve.tensor_scalar(probs[s][:, 0, 0:n], probs[s][:, 0, 0:n], srec[:, s, 0:1], None, ALU.mult)\
                                  .then_inc(probs_done.sem, 1)
                            else:
                                link(ve.reciprocal(srec[:, s, :], ssum[:, s, :]))
                                ve.tensor_scalar(probs[s][:, 0, 0:n], probs[s][:, 0, 0:n], srec[:, s, 0:1], None, ALU.mult)
                                link(ve.tensor_scalar(srec[:, s, 1:2], srec[:, s, 1:2], lamw[:, 2:3], None, ALU.mult))
                                ve.scalar_tensor_tensor(out=probs[s][:, 0, 0:n], in0=probs[s][:, 1, 0:n], scalar=srec[:, s, 1:2],
                                                        in1=probs[s][:, 0, 0:n], op0=ALU.mult, op1=ALU.add)\
                                  .then_inc(probs_done.sem, 1)
                        if i < last:
                            kind, h, b = ITS[i]
                            nk = key_cols(b)[1]
                            for g in groups(i):
                                c = slice(g % 2, g % 2 + 1)
                                ve.wait_ge(sc_ps.sem, sc_ps.at(l, g + 1))
                                link(ve.reduce_max(smax[:, c], S[g % 2][:, 0:nk], AX.X))
                                ve.tensor_scalar(negm[:, c], smax[:, c], -(MLA_SCALE if kind == "mla" else DIFF_SCALE), None,
                                                 ALU.mult).then_inc(negm_done.sem, 1)
                        if i - 4 >= first:
                            it = i - 4
                            kind, h, b = ITS[it]
                            c0 = (it % 2) * 512
                            ve.wait_ge(o_ps.sem, o_ps.at(l, it + 1))
                            if kind == "mla":
                                half = slice((h % 2) * VDIM, (h % 2 + 1) * VDIM)
                                ins = ve.tensor_copy(y_mla[half, h // 2, b * P:(b + 1) * P], U[half, c0:c0 + P])
                            else:
                                ins = ve.tensor_copy(yT[:, 2 + h, b * P:(b + 1) * P], U[:, c0:c0 + P])
                            ins.then_inc(o_sb.sem, 1)

                attention(0, ATT_IT)
                all_rows = slice(0, P)
                for j in range(8):
                    dst = qT if j < 4 else kT
                    rope_parts(12 + j, dst[:, j % 4, CTX:TOK], all_rows, cos_d, sin_d)
                    if j >= 1:
                        prev = qT if j - 1 < 4 else kT
                        rope_add(4 + j, prev[:, (j - 1) % 4, CTX:TOK], all_rows)
                rope_add(12, kT[:, 3, CTX:TOK], all_rows)
                for j in range(2):
                    lat_copy(20 + j, zfT[:, j, CTX:TOK])
                for j in range(2):
                    lat, cx = (U[:, 0:512], S[0][:, 512:512 + CTX]) if j == 0 else (S[0][:, 0:512], ctx_bank[1][:, 0:CTX])
                    ve.wait_ge(fb_ps.sem, fb_ps.at(l, j + 1))
                    ve.tensor_copy(yT[:, j, CTX:TOK], lat)
                    ve.tensor_copy(yT[:, j, 0:CTX], cx).then_inc(fb_sb.sem, 1)
                attention(ATT_IT, 2 * ATT_IT)
                ve.wait_ge(o_sb.sem, o_sb.at(l, 2 * ATT_IT))
                for h in range(HEADS):
                    ve.wait_ge(sub_rms.sem, sub_rms.at(l, 1 if h < 3 else 2))
                    for cols, at in ((slice(CTX, TOK), sub_lat[h]), (slice(0, CTX), sub_ctx[h])):
                        y = yT[:, 2 + h, cols]
                        ins = ve.scalar_tensor_tensor(out=y, in0=y, scalar=gsub[:, 0:1], in1=sub_rstd[:, at:at + y.shape[1]],
                                                      op0=ALU.mult, op1=ALU.mult)
                    ins.then_inc(sub_scaled.sem, 1)

                def residual(n, gate_block, lat, cx):
                    ve.scalar_tensor_tensor(out=xT[:, n, CTX:TOK], in0=lat, scalar=mod[:, gate_block + n, 1:2],
                                            in1=xT[:, n, CTX:TOK], op0=ALU.mult, op1=ALU.add)
                    return ve.scalar_tensor_tensor(out=xT[:, n, 0:CTX], in0=cx,
                                                   scalar=mod[:, gate_block + n, 0:1], in1=xT[:, n, 0:CTX],
                                                   op0=ALU.mult, op1=ALU.add)

                for n in range(KD):
                    ve.wait_ge(mix_ps.sem, mix_ps.at(l, n + 1))
                    residual(n, 2 * KD, lat_bank[n % 2], ctx_bank[n % 2][:, 0:CTX]).then_inc(mix_sb.sem, 1)
                    if n >= 1:
                        add_squares(l, 1, n - 1)
                add_squares(l, 1, KD - 1)

                ve.wait_ge(mix_sb.sem, mix_sb.at(l, KD))
                normalise(l, 1)
                ve.wait_ge(outs_done.sem, outs_done.at(l + 1, 0))
                ve.wait_ge(xn_done.sem, xn_done.at(l, 2 * KD))
                for zeros in (ye_hi, yex, ye_lo, back, backx):
                    ve.memset(zeros[:, :].bitcast(F32), 0.0)
                for b in range(2):
                    ve.wait_ge(hr_ps.sem, hr_ps.at(l, b + 1))
                    ve.tensor_copy(h_rows[:, b, 0:512], S[b % 2][:, 0:512]).then_inc(hr_v.sem, 1)
                ve.wait_ge(lg_ps.sem, lg_ps.at(l, 1))
                logits = T[:, 0:NB * E_N].rearrange("p (b e) -> p b e", b=NB)
                link(ve.reduce_max(lmax[:, :], logits, AX.X))
                ve.tensor_tensor(lg[:, :, :], logits, lmax[:, :].unsqueeze(2).broadcast_to([P, NB, E_N]), ALU.subtract)\
                  .then_inc(lg_shift.sem, 1)
                ve.wait_ge(lg_exp.sem, lg_exp.at(l, 1))
                link(ve.reduce_sum(lmax[:, :], lg[:, :, :], AX.X))
                link(ve.reciprocal(lmax[:, :], lmax[:, :]))
                ve.tensor_tensor(lg[:, :, :], lg[:, :, :], lmax[:, :].unsqueeze(2).broadcast_to([P, NB, E_N]), ALU.mult)\
                  .then_inc(aff_rows.sem, 1)
                ve.wait_ge(aff_ps.sem, aff_ps.at(l, 1))
                ve.tensor_copy(work[0:E_N, 0:CTX], U[0:E_N, 512:512 + CTX])
                link(ve.tensor_copy(work[0:E_N, CTX:TOK], U[0:E_N, 0:LAT]))
                for cols, cap in ((slice(0, CTX), CAPX), (slice(CTX, TOK), CAP)):
                    for _ in range(cap // 8):
                        link(ve.max(top8[:, :], work[0:E_N, cols]))
                        link(ve.match_replace(work[0:E_N, cols], top8[:, :], work[0:E_N, cols], -1.0))
                link(ve.tensor_scalar(mask[0:E_N, :], work[0:E_N, :], 0.0, None, ALU.is_lt))
                for cols in (slice(0, CTX), slice(CTX, TOK)):
                    link(ve.tensor_tensor_scan(rank[:, cols], mask[0:E_N, cols], mask[0:E_N, cols], 0.0, ALU.add, ALU.max))
                link(ve.tensor_tensor(rank[:, :], rank[:, :], mask[0:E_N, :], ALU.mult))
                ve.tensor_scalar(pos, rank[:, :], -1.0, None, ALU.add).then_inc(pos_done.sem, 1)
                ve.wait_ge(pr_ps.sem, pr_ps.at(l, 1))
                ve.tensor_copy(pos_rows[:, :, 0:E_N], T[:, 0:NB * E_N].rearrange("p (b e) -> p b e", b=NB)).then_inc(pr_sb.sem, 1)

                def choose(u, first):
                    ve.wait_ge(pr_sb.sem, pr_sb.at(l, 1))
                    link(ve.tensor_copy(cur[:, :, :], pos_rows[:, :, first]))
                    for i in range(2):
                        ve.tensor_tensor(pick[:, :, i * CAP:(i + 1) * CAP], iota.unsqueeze(1).broadcast_to([P, 4, CAP]),
                                         cur[:, 1:NB, i].unsqueeze(2).broadcast_to([P, 4, CAP]), ALU.is_equal)
                    ve.tensor_tensor(pickx[:, :].rearrange("p (i c) -> p i c", i=2),
                                     iota[:, 0:CAPX].unsqueeze(1).broadcast_to([P, 2, CAPX]),
                                     cur[:, 0, :].unsqueeze(2).broadcast_to([P, 2, CAPX]), ALU.is_equal)\
                      .then_inc(pick_done.sem, 1)

                def low_lat(u):
                    ve.wait_ge(xl_hi.sem, xl_hi.at(u, 1))
                    ve.tensor_tensor(xs_lo[:, :, :, 0:CAP], U[:, :].rearrange("p (k i c) -> p k i c", k=KD, i=2),
                                     xs_hi[:, :, :, 0:CAP].bitcast(F32), ALU.subtract).then_inc(xl_lo.sem, 1)

                def low_ctx(u):
                    ve.wait_ge(xx_hi.sem, xx_hi.at(u, 1))
                    ve.tensor_tensor(xs_lo[:, :, :, CAP:SLOT_TOK],
                                     S[0][:, 0:KD * 2 * CAPX].rearrange("p (k i c) -> p k i c", k=KD, i=2),
                                     xs_hi[:, :, :, CAP:SLOT_TOK].bitcast(F32), ALU.subtract).then_inc(xx_lo.sem, 1)

                def low_rows(i, half, hi_ready):
                    ve.wait_ge(*hi_ready)
                    cols = slice(half * 512, (half + 1) * 512)
                    ve.tensor_tensor(ye_lo[i * CAP:(i + 1) * CAP, cols], T[0:CAP, cols],
                                     ye_hi[i * CAP:(i + 1) * CAP, cols].bitcast(F32), ALU.subtract)
                    at = i * XROW
                    return ve.tensor_tensor(yex[2 * XROW + at:2 * XROW + at + CAPX, cols], T[CAP:SLOT_TOK, cols],
                                            yex[at:at + CAPX, cols].bitcast(F32), ALU.subtract)

                def add_back(v, n, lat, cx):
                    ve.wait_ge(add_ps.sem, add_ps.at(v, n + 1))
                    residual(n, 5 * KD, lat, cx).then_inc(add_sb.sem, 1)

                u = l * (PAIRS + 1)
                choose(u, slice(0, 2))
                low_lat(u)
                low_ctx(u)
                ve.memset(T[0:SLOT_TOK, :], 0.0).then_inc(t_clear.sem, 1)
                with ve.Fori(0, PAIRS) as pair:
                    t = l * PAIRS + pair
                    u = l * (PAIRS + 1) + pair + 1
                    ve.sem_clear(step_v)
                    count[0] = 0

                    def low_pieces(g, between={}):
                        for piece in range(PIECES):
                            if (g, piece) in ON_VECTOR:
                                ve.wait_ge(hi_done.sem, hi_done.at(t, g * PIECES + piece + 1))
                                k = slice(2 * piece, 2 * piece + 2)
                                ve.tensor_tensor(ring_lo[:, g % RING, k, :], ring[:, g % RING, k, :],
                                                 w_hi[:, piece, :, :].bitcast(F32), ALU.subtract).then_inc(lo_done.sem, 1)
                            if piece in between:
                                add_back(u - 1, between[piece], T[:, 0:LAT], T[:, 512:512 + CTX])

                    def middle(i, half):
                        ve.wait_ge(silu_done.sem, silu_done.at(t, 2 * i + half + 1))
                        ve.wait_ge(gr_ps.sem, gr_ps.at(t, 4 * i + 2 * half + 2))
                        rows = hm_rows[i][0:SLOT_TOK, half * 512:(half + 1) * 512]
                        ve.scalar_tensor_tensor(out=rows, in0=S[half][0:SLOT_TOK, 512:1024], scalar=gates[:, i:i + 1], in1=rows,
                                                op0=ALU.mult, op1=ALU.mult).then_inc(hm_done.sem, 1)

                    def low_middle(i):
                        ve.wait_ge(hh_done.sem, hh_done.at(t, i + 1))
                        ve.tensor_tensor(hm_lo[:, i, :, :].rearrange("p (b j) c -> p b (j c)", b=2),
                                         U[:, :].rearrange("p (b n) -> p b n", b=2)[:, :, 0:4 * SLOT_TOK],
                                         hm_hi[:, i, :, :].bitcast(F32).rearrange("p (b j) c -> p b (j c)", b=2),
                                         ALU.subtract).then_inc(hl_done.sem, 1)

                    ve.wait_ge(aff_rows.sem, aff_rows.at(l, 1))
                    ve.tensor_copy(cur_gate[:, :, :], lg[:, :, bass.ds(pair * 2, 2)]).then_inc(gate_cols.sem, 1)
                    low_pieces(0)
                    low_rows(1, 0, (ye1_hi.sem, ye1_hi.at(u - 1, 1)))
                    low_rows(1, 1, (ye1_hi.sem, ye1_hi.at(u - 1, 2))).then_inc(rows_done.sem, 1)
                    low_pieces(1)
                    ve.wait_ge(gate_sb.sem, gate_sb.at(t, 1))
                    choose(u, bass.ds(pair * 2 + 2, 2))
                    for copy in range(2):
                        ve.tensor_copy(selx[:, copy, :, :],
                                       ident[0:E_N, bass.ds(pair * 2, 2)].unsqueeze(2).broadcast_to([E_N, 2, XROW]))
                    ve.tensor_copy(sel[:, :, :], ident[0:E_N, bass.ds(pair * 2, 2)].unsqueeze(2).broadcast_to([E_N, 2, CAP]))\
                      .then_inc(sel_done.sem, 1)
                    low_pieces(2, {3: 0})
                    middle(0, 0)
                    low_pieces(3, {2: 1})
                    low_pieces(4, {1: 2})
                    middle(0, 1)
                    low_pieces(5, {1: 3})
                    low_middle(0)
                    low_pieces(6, {1: 4})
                    middle(1, 0)
                    low_pieces(7, {0: 5, 2: 6})
                    low_pieces(8, {1: 7})
                    middle(1, 1)
                    low_lat(u)
                    low_pieces(9)
                    low_middle(1)
                    low_ctx(u)
                    low_rows(0, 0, (ye0_hi.sem, ye0_hi.at(t, 1))).then_inc(ye0_lo.sem, 1)
                    low_pieces(10)
                    low_rows(0, 1, (ye0_hi.sem, ye0_hi.at(t, 2))).then_inc(ye0_lo.sem, 1)
                    low_pieces(11)
                    ve.wait_ge(place_ps.sem, place_ps.at(t, 1))
                    ve.tensor_scalar(back[:, :], U[:, 0:LAT], consts[:, K_SLOT:K_SLOT + 1], None, ALU.is_equal)
                    ve.tensor_scalar(backx[:, :], U[:, 512:512 + CTX], consts[:, K_SLOTX:K_SLOTX + 1], None, ALU.is_equal)\
                      .then_inc(back_done.sem, 1)
                u = l * (PAIRS + 1) + PAIRS
                low_rows(1, 0, (ye1_hi.sem, ye1_hi.at(u, 1)))
                low_rows(1, 1, (ye1_hi.sem, ye1_hi.at(u, 2))).then_inc(rows_done.sem, 1)
                for n in range(KD):
                    add_back(u, n, lat_bank[n % 2], ctx_bank[n % 2][:, 0:CTX])
                ve.wait_ge(add_sb.sem, add_sb.at(u, KD))

            for k in range(KD):
                add_squares(DEPTH, 0, k)
            ve.wait_ge(rms_done.sem, rms_done.at(DEPTH, 1))
            for k in range(KD):
                ve.scalar_tensor_tensor(out=hT[:, k, :], in0=xT[:, k, :], scalar=condT[:, 2 * KD + k:2 * KD + k + 1],
                                        in1=rstd[:, :], op0=ALU.mult, op1=ALU.mult).then_inc(xn_done.sem, 1)
            for b in range(NB):
                ve.wait_ge(fin_ps.sem, b + 1)
                ve.tensor_copy(arena[:, b * D:b * D + 512], S[b % 2][:, 0:512]).then_inc(fin_v.sem, 1)


_INS = ["x_prompt", "x_sample", "cache_diff_k", "cache_diff_v", "cache_mla_ckv", "cache_mla_kpe", "c", "c_ctx", "w_ada",
        "b_ada", "g_attn", "g_ffn", "w_in", "w_four", "diff_lambda", "g_subln", "g_mla_q", "w_mla_uq", "g_mla_kv",
        "w_mla_ukv", "w_out", "w_router", "w_e_gate", "w_e_up", "w_e_down", "g_final"]
_OUTS = [("y_prompt", (1, CTX, D)), ("y_sample", (1, LAT, D)), ("new_diff_k", (1, DEPTH, CTX, HEADS, 2 * DH)),
         ("new_diff_v", (1, DEPTH, CTX, HEADS, 2 * DH)), ("new_mla_ckv", (1, DEPTH, CTX, P)),
         ("new_mla_kpe", (1, DEPTH, CTX, ROPE))]


def _rope_tables(dim):
    rows = LAT // GRID_W
    row = np.repeat(np.arange(rows, dtype=np.float32), GRID_W)
    col = np.tile(np.arange(GRID_W, dtype=np.float32), rows)
    nf = dim // 4
    inv = (np.float32(ROPE_BASE) ** (-np.arange(nf, dtype=np.float32) / np.float32(nf))).astype(np.float32)
    ang = np.concatenate([row[:, None] * inv, col[:, None] * inv], axis=-1)
    return np.cos(ang).astype(np.float32).T, np.sin(ang).astype(np.float32).T


def _constants():
    c = np.zeros((P, K_W), np.float32)
    c[:, K_ID:K_ID + P] = np.eye(P)
    def rot(m, at, half):
        for i in range(half):
            m[at + half + i, at + i] = -1.0
            m[at + i, at + half + i] = 1.0
    rot(c[:, K_ROTD:K_ROTD + P], 0, DH // 2)
    rot(c[:, K_ROTD:K_ROTD + P], DH, DH // 2)
    rot(c[:, K_ROTM:K_ROTM + QM], NOPE, ROPE // 2)
    cos, sin = _rope_tables(DH)
    c[:, K_ROPED:K_ROPED + LAT] = np.tile(cos, (4, 1))
    c[:, K_ROPED + LAT:K_ROPED + 2 * LAT] = np.tile(sin, (4, 1))
    cos, sin = _rope_tables(ROPE)
    c[0:NOPE, K_ROPEM:K_ROPEM + LAT] = 1.0
    c[NOPE:QM, K_ROPEM:K_ROPEM + LAT] = np.tile(cos, (2, 1))
    c[NOPE:QM, K_ROPEM + LAT:K_ROPEM + 2 * LAT] = np.tile(sin, (2, 1))

    def dft(n):
        turn = 2.0 * np.pi * (np.outer(np.arange(n), np.arange(n)) % n) / n
        return np.cos(turn) / np.sqrt(n), np.sin(turn) / np.sqrt(n)

    for part, m in enumerate(dft(F_CH)):
        for j in range(2):
            c[j * F_CH:(j + 1) * F_CH, K_CHAN + part * P + j * F_CH:K_CHAN + part * P + (j + 1) * F_CH] = m
    co, si = dft(CTX)
    c[:, K_SEQX:K_SEQX + CTX], c[:, K_SEQX + CTX:K_SEQX + 2 * CTX] = co, -si
    c[:, K_IOTA:K_IOTA + CAP] = np.arange(CAP)
    c[:, K_SLOT] = np.arange(P) % CAP
    c[:, K_SLOTX] = np.arange(P) % XROW
    c[:, K_FOLD:K_FOLD + E_N] = np.arange(P)[:, None] % 32 == np.arange(E_N)[None, :]
    c[:, K_EPS] = EPS
    co, si = dft(LAT)
    seq = np.concatenate([co, -si]).astype(np.float32)
    init = 0.8 - 0.6 * np.exp(-0.3 * np.arange(DEPTH))
    lam = np.stack([init, 1.0 - init], axis=1).astype(np.float32)
    return c, seq, lam


def kernel(**inputs):
    import concourse.bacc as bacc
    from concourse.bass_utils import run_bass_kernel_spmd

    nc = bacc.Bacc("TRN2", target_bir_lowering=False, num_devices=1)
    arrays, aps = {}, {}
    consts, seq, lam = _constants()
    given = [(n, inputs[n]) for n in _INS] + [("consts", consts), ("dft", seq), ("lam_init", lam)]
    for name, value in given:
        v = np.ascontiguousarray(value)
        arrays[f"in_{name}_dram"] = v
        aps[name] = nc.dram_tensor(f"in_{name}_dram", v.shape, mybir.dt.from_np(v.dtype), kind="ExternalInput").ap()
    for name, shape in _OUTS:
        aps[name] = nc.dram_tensor(f"out_{name}_dram", shape, F32, kind="ExternalOutput").ap()
    build(nc, aps)
    r = run_bass_kernel_spmd(nc, [arrays], core_ids=[0])
    return tuple(r.results[0][f"out_{name}_dram"] for name, _ in _OUTS)
```
